# Optimizing a Trainium2 kernel written in Bass

```python
import math
import jax, jax.numpy as jnp
from jax import lax
import numpy as np

D_MODEL = 1024
BATCH = 1
SEQ = 256
DEPTH = 2
DEC_BATCH = 1
DEC_SEQ = 32
PAST_LEN = 128

CHUNK = 64
N_MIXERS = 2
N_MLA_LAYERS = (DEPTH + 1) // 2
N_GM_LAYERS = DEPTH // 2

N_HEADS = 8
QK_NOPE = 128
QK_ROPE = 64
V_HEAD = 128
Q_LORA = 384
KV_LORA = 256
ROPE_THETA = 10000.0
Q_BLOCK = 128
ATTN_SCALE = (QK_NOPE + QK_ROPE) ** -0.5

GM_CHUNK = 128
GM_GROUPS = 8
GM_WIDTH = D_MODEL
GM_GROUP_DIM = GM_WIDTH // GM_GROUPS

D_FF = 2816
N_EXPERTS = 8
TOP_K = 2
D_FF_EXPERT = 3584

PLE_DIM = 256

ALPHA = (2 * DEPTH) ** 0.25
BETA = (8 * DEPTH) ** -0.25

kernel_name = "hybrid_mla_gmlp_streaming_step"

def layer_norm(x, g, b, eps=1e-5):
    xf = x.astype(jnp.float32)
    mu = jnp.mean(xf, -1, keepdims=True)
    var = jnp.mean(jnp.square(xf - mu), -1, keepdims=True)
    return ((xf - mu) * lax.rsqrt(var + eps)).astype(x.dtype) * g + b

def rms_norm(x, g, eps=1e-6):
    xf = x.astype(jnp.float32)
    return (xf * lax.rsqrt(jnp.mean(xf * xf, -1, keepdims=True) + eps)).astype(x.dtype) * g

def rope_tables(pos, dtype):
    half = QK_ROPE // 2
    inv = ROPE_THETA ** (-jnp.arange(half, dtype=jnp.float32) / half)
    ang = pos.astype(jnp.float32)[:, None] * inv[None, :]
    return jnp.cos(ang).astype(dtype), jnp.sin(ang).astype(dtype)

def apply_rope(x, cos, sin):
    half = QK_ROPE // 2
    x1, x2 = x[..., :half], x[..., half:]
    return jnp.concatenate([x1 * cos - x2 * sin, x1 * sin + x2 * cos], -1)

def mla_project(x, pos, w_in, g_q, w_q_up, g_kv):
    B, S, _ = x.shape
    h = x @ w_in
    c_q, c_kv, k_r = jnp.split(h, [Q_LORA, Q_LORA + KV_LORA], axis=-1)
    q = (rms_norm(c_q, g_q) @ w_q_up).reshape(B, S, N_HEADS, QK_NOPE + QK_ROPE)
    c_kv = rms_norm(c_kv, g_kv)
    cos, sin = rope_tables(pos, x.dtype)
    q_nope = q[..., :QK_NOPE]
    q_rope = apply_rope(q[..., QK_NOPE:], cos[:, None, :], sin[:, None, :])
    k_rope = apply_rope(k_r, cos, sin)
    return q_nope, q_rope, c_kv, k_rope

def mla_attention(q_nope, q_rope, q_start, c_all, kr_all, w_kv_up):
    B, S = q_nope.shape[:2]
    T = c_all.shape[1]
    kv = (c_all @ w_kv_up).reshape(B, T, N_HEADS, QK_NOPE + V_HEAD)
    k_nope, v = kv[..., :QK_NOPE], kv[..., QK_NOPE:]
    kv_chunk = jnp.arange(T) // CHUNK
    nb = S // Q_BLOCK if S % Q_BLOCK == 0 else 1
    qb = S // nb
    qn_b = q_nope.reshape(B, nb, qb, N_HEADS, QK_NOPE).transpose(1, 0, 2, 3, 4)
    qr_b = q_rope.reshape(B, nb, qb, N_HEADS, QK_ROPE).transpose(1, 0, 2, 3, 4)

    def block(args):
        qn, qr, i = args
        q_chunk = (q_start + i * qb + jnp.arange(qb)) // CHUNK
        mask = kv_chunk[None, :] <= q_chunk[:, None]
        s = (jnp.einsum('bqhd,bkhd->bhqk', qn, k_nope)
             + jnp.einsum('bqhr,bkr->bhqk', qr, kr_all)).astype(jnp.float32) * ATTN_SCALE
        s = jnp.where(mask, s, -jnp.inf)
        p = jax.nn.softmax(s, axis=-1).astype(v.dtype)
        return jnp.einsum('bhqk,bkhd->bqhd', p, v)

    o = lax.map(block, (qn_b, qr_b, jnp.arange(nb)))
    return o.transpose(1, 0, 2, 3, 4).reshape(B, S, N_HEADS * V_HEAD)

def gmlp_mix(x, w_in, ln_g, ln_b, w_s, b_s, w_out):
    B, S, _ = x.shape
    L = min(S, GM_CHUNK)
    nc = S // L
    h = jax.nn.gelu(x @ w_in)
    u, v = jnp.split(h, 2, axis=-1)
    v = layer_norm(v, ln_g, ln_b)
    wm = jnp.tril(w_s[:, :L, :L])
    vg = v.reshape(B, nc, L, GM_GROUPS, GM_GROUP_DIM)
    mixed = jnp.einsum('gts,bnsgc->bntgc', wm, vg) + b_s[:, :L].T[None, None, :, :, None]
    y = (u * mixed.reshape(B, S, GM_WIDTH)) @ w_out
    return y, v

def swiglu(x, wg, wu, wd):
    return (jax.nn.silu(x @ wg) * (x @ wu)) @ wd

def moe_swiglu(x, w_router, wg, wu, wd):
    probs = jax.nn.softmax((x @ w_router).astype(jnp.float32), axis=-1)
    top_p, top_i = lax.top_k(probs, TOP_K)
    top_p = top_p / jnp.sum(top_p, -1, keepdims=True)
    combine = jnp.sum(jax.nn.one_hot(top_i, N_EXPERTS, dtype=jnp.float32) * top_p[..., None], axis=-2)
    combine = combine.astype(x.dtype)
    y = jnp.zeros_like(x)
    for e in range(N_EXPERTS):
        y = y + combine[..., e:e + 1] * swiglu(x, wg[e], wu[e], wd[e])
    return y

def run_trunk(x, p, past_latent, past_krope, W):
    B, S, _ = x.shape
    past = 0 if past_latent is None else past_latent.shape[2]
    q_pos = past + jnp.arange(S)
    new_lat, new_kr, new_v = [], [], []
    for i in range(DEPTH):
        j = i // N_MIXERS
        if i % N_MIXERS == 0:
            qn, qr, c_kv, k_r = mla_project(x, q_pos, W['w_mla_in'][j], W['g_q_norm'][j],
                                            W['w_q_up'][j], W['g_kv_norm'][j])
            new_lat.append(c_kv)
            new_kr.append(k_r)
            if past_latent is None:
                c_all, kr_all = c_kv, k_r
            else:
                c_all = jnp.concatenate([past_latent[j], c_kv], axis=1)
                kr_all = jnp.concatenate([past_krope[j], k_r], axis=1)
            att = mla_attention(qn, qr, past, c_all, kr_all, W['w_kv_up'][j])
            h = att @ W['w_mla_out'][j]
        else:
            h, v_rows = gmlp_mix(x, W['w_gm_in'][j], W['g_gm_norm'][j], W['b_gm_norm'][j],
                                 W['w_gm_spatial'][j], W['b_gm_spatial'][j], W['w_gm_out'][j])
            new_v.append(v_rows[:, ((S - 1) // GM_CHUNK) * GM_CHUNK:])
        x = layer_norm(ALPHA * x + h, W['ln1_g'][i], W['ln1_b'][i])
        if i % 2 == 0:
            f = swiglu(x, W['w_ffn_gate'][j], W['w_ffn_up'][j], W['w_ffn_down'][j])
        else:
            f = moe_swiglu(x, W['w_router'][j], W['w_moe_gate'][j], W['w_moe_up'][j], W['w_moe_down'][j])
        x = layer_norm(ALPHA * x + f, W['ln2_g'][i], W['ln2_b'][i])
        x = x + jax.nn.sigmoid(x @ W['w_ple_gate'][i]) * (p[i] @ W['w_ple_proj'][i])
    return x, jnp.stack(new_lat), jnp.stack(new_kr), jnp.stack(new_v)

def setup_inputs(seed: int = 0) -> dict:
    key = jax.random.key(seed)
    ks = iter(list(jax.random.split(key, 48)))
    f32 = jnp.float32

    def nrm(shape, scale=1.0):
        return jax.random.normal(next(ks), shape, f32) * scale

    def gain(shape):
        return 1.0 + 0.02 * jax.random.normal(next(ks), shape, f32)

    nm, ng = N_MLA_LAYERS, N_GM_LAYERS
    return {
        'x_prompt': nrm((BATCH, SEQ, D_MODEL)),
        'x_sample': nrm((DEC_BATCH, DEC_SEQ, D_MODEL)),
        'cache_mla_latent': nrm((nm, DEC_BATCH, PAST_LEN, KV_LORA)),
        'cache_mla_krope': nrm((nm, DEC_BATCH, PAST_LEN, QK_ROPE)),
        'p_prompt': nrm((DEPTH, BATCH, SEQ, PLE_DIM)),
        'p_sample': nrm((DEPTH, DEC_BATCH, DEC_SEQ, PLE_DIM)),
        'w_mla_in': nrm((nm, D_MODEL, Q_LORA + KV_LORA + QK_ROPE), D_MODEL ** -0.5),
        'g_q_norm': gain((nm, Q_LORA)),
        'w_q_up': nrm((nm, Q_LORA, N_HEADS * (QK_NOPE + QK_ROPE)), Q_LORA ** -0.5),
        'g_kv_norm': gain((nm, KV_LORA)),
        'w_kv_up': nrm((nm, KV_LORA, N_HEADS * (QK_NOPE + V_HEAD)), KV_LORA ** -0.5),
        'w_mla_out': nrm((nm, N_HEADS * V_HEAD, D_MODEL), BETA * (N_HEADS * V_HEAD) ** -0.5),
        'w_gm_in': nrm((ng, D_MODEL, 2 * GM_WIDTH), D_MODEL ** -0.5),
        'g_gm_norm': gain((ng, GM_WIDTH)),
        'b_gm_norm': nrm((ng, GM_WIDTH), 0.02),
        'w_gm_spatial': nrm((ng, GM_GROUPS, GM_CHUNK, GM_CHUNK), GM_CHUNK ** -0.5),
        'b_gm_spatial': gain((ng, GM_GROUPS, GM_CHUNK)),
        'w_gm_out': nrm((ng, GM_WIDTH, D_MODEL), BETA * GM_WIDTH ** -0.5),
        'w_ffn_gate': nrm((nm, D_MODEL, D_FF), D_MODEL ** -0.5),
        'w_ffn_up': nrm((nm, D_MODEL, D_FF), D_MODEL ** -0.5),
        'w_ffn_down': nrm((nm, D_FF, D_MODEL), BETA * D_FF ** -0.5),
        'w_router': nrm((ng, D_MODEL, N_EXPERTS), D_MODEL ** -0.5),
        'w_moe_gate': nrm((ng, N_EXPERTS, D_MODEL, D_FF_EXPERT), D_MODEL ** -0.5),
        'w_moe_up': nrm((ng, N_EXPERTS, D_MODEL, D_FF_EXPERT), D_MODEL ** -0.5),
        'w_moe_down': nrm((ng, N_EXPERTS, D_FF_EXPERT, D_MODEL), BETA * D_FF_EXPERT ** -0.5),
        'ln1_g': gain((DEPTH, D_MODEL)),
        'ln1_b': nrm((DEPTH, D_MODEL), 0.02),
        'ln2_g': gain((DEPTH, D_MODEL)),
        'ln2_b': nrm((DEPTH, D_MODEL), 0.02),
        'w_ple_gate': nrm((DEPTH, D_MODEL, D_MODEL), D_MODEL ** -0.5),
        'w_ple_proj': nrm((DEPTH, PLE_DIM, D_MODEL), PLE_DIM ** -0.5),
    }

def reference(x_prompt, x_sample, cache_mla_latent, cache_mla_krope, p_prompt, p_sample,
              w_mla_in, g_q_norm, w_q_up, g_kv_norm, w_kv_up, w_mla_out,
              w_gm_in, g_gm_norm, b_gm_norm, w_gm_spatial, b_gm_spatial, w_gm_out,
              w_ffn_gate, w_ffn_up, w_ffn_down,
              w_router, w_moe_gate, w_moe_up, w_moe_down,
              ln1_g, ln1_b, ln2_g, ln2_b,
              w_ple_gate, w_ple_proj):
    W = dict(w_mla_in=w_mla_in, g_q_norm=g_q_norm, w_q_up=w_q_up, g_kv_norm=g_kv_norm,
             w_kv_up=w_kv_up, w_mla_out=w_mla_out,
             w_gm_in=w_gm_in, g_gm_norm=g_gm_norm, b_gm_norm=b_gm_norm,
             w_gm_spatial=w_gm_spatial, b_gm_spatial=b_gm_spatial, w_gm_out=w_gm_out,
             w_ffn_gate=w_ffn_gate, w_ffn_up=w_ffn_up, w_ffn_down=w_ffn_down,
             w_router=w_router, w_moe_gate=w_moe_gate, w_moe_up=w_moe_up, w_moe_down=w_moe_down,
             ln1_g=ln1_g, ln1_b=ln1_b, ln2_g=ln2_g, ln2_b=ln2_b,
             w_ple_gate=w_ple_gate, w_ple_proj=w_ple_proj)
    y_prompt, lat_p, kr_p, v_p = run_trunk(x_prompt, p_prompt, None, None, W)
    y_sample, lat_s, kr_s, v_s = run_trunk(x_sample, p_sample, cache_mla_latent, cache_mla_krope, W)
    return (y_prompt, y_sample, lat_p, kr_p, lat_s, kr_s, v_p, v_s)


_drawn_inputs = setup_inputs


def setup_inputs(seed=0):
    import zlib

    import numpy as np

    out = dict(_drawn_inputs(seed))
    spreads = {}
    factors = {'g_q_norm': 8.0,
     'g_kv_norm': 2.745,
     'g_gm_norm': 7.476,
     'b_gm_norm': 7.825,
     'b_gm_spatial': 20.689}
    for name, (base, spread) in spreads.items():
        noise = np.random.default_rng([zlib.crc32(name.encode()), seed]).standard_normal(out[name].shape)
        drawn = base * np.exp(spread * noise) if base else spread * noise
        out[name] = __import__('jax').numpy.asarray(drawn.astype(out[name].dtype))
    for name, factor in factors.items():
        out[name] = (out[name] * factor).astype(out[name].dtype)
    return out
```

```python
from contextlib import ExitStack

import numpy as np

import concourse.bass as bass
from concourse import mybir

F32 = mybir.dt.float32
I32 = mybir.dt.int32
U32 = mybir.dt.uint32
ALU = mybir.AluOpType
ACT = mybir.ActivationFunctionType
AX_X = mybir.AxisListType.X

P = 128
D = 1024
DC = D // P
TP, TS = 256, 32
T = TP + TS
PAST = 128
KEYS = T + PAST
CHUNK = 64
H, NOPE, ROPE, VH = 8, 128, 64, 128
QL, KVL = 384, 256
QC, KC = QL // P, KVL // P
FF = 2816
FC = FF // P
E, FE = 8, 3584
FB = FE // 512
PLE = 256
PC = PLE // P
ALPHA = 4.0 ** 0.25
SCALE = (NOPE + ROPE) ** -0.5
EPS_LN, EPS_RMS = 1e-5, 1e-6
GM_CHUNK = 128

SLOTS = 7
BLK = 4096
TRUNK = [("mla_in", 2, DC * 384), ("q_up", 2, QC * 768), ("kv_up", 1, KC * 2048), ("mla_out", 2, DC * 512),
         ("ffn_in", 11, DC * 512), ("ffn_down", 8, FC * 128), ("ple_gate0", 2, DC * 512),
         ("ple_proj0", 1, PC * 1024), ("gm_in", 4, DC * 512), ("gm_out", 2, DC * 512)]
TAIL = [("ple_gate1", 2, DC * 512), ("ple_proj1", 1, PC * 1024)]
N_TRUNK = sum(n for _, n, _ in TRUNK)
EB = 3 * FB
assert N_TRUNK % SLOTS == 0 and EB % SLOTS == 0
MAX_TILES = 12

G_Q, G_KV, G_GM, B_GM = 0, 3, 5, 13
LN_G = {0: 21, 1: 37, 3: 29, 4: 45}
LN_B = {0: 53, 1: 69, 3: 61, 4: 77}
N_VEC = 85

PLAN = [("in", 6), ("rms", 2), ("krot", 1), ("qrope", 4), ("qnope", 8), ("qrot", 4), ("kup", 8), ("vup", 8)]
ATT = {}
_n = sum(n for _, n in PLAN)
ATT["S", 0] = _n
_n += 2
for _h in range(H):
    if _h + 1 < H:
        ATT["S", _h + 1] = _n
        _n += 2
    ATT["T", _h] = _n
    _n += 1
    if _h:
        ATT["O", _h - 1] = _n
        _n += 1
ATT["O", H - 1] = _n
_n += 1
PLAN += [("attention", _n - sum(n for _, n in PLAN)), ("att_out", 8), ("ln0", 2), ("ffn", 4 * 11), ("down", 8),
         ("ln1", 2), ("gate0", 8), ("proj0", 8), ("gm", 16), ("ln2", 2), ("vtr", 8), ("mix", 8), ("gm_out", 8),
         ("ln3", 2), ("logits", 1), ("xtr", 8), ("rank", 1), ("ln4", 2), ("gate1", 8), ("proj1", 8)]
TILE = {}
_n = 0
for _name, _k in PLAN:
    TILE[_name] = _n
    _n += _k

LAST_TILE = []
for _name, _k, _per in (("in", 2, 3), ("qrope", 2, 6), ("kup", 1, 16), ("att_out", 2, 4), ("ffn", 11, 4),
                        ("down", 8, 1), ("gate0", 2, 4), ("proj0", 1, 8), ("gm", 4, 4), ("gm_out", 2, 4)):
    LAST_TILE += [TILE[_name] + _per * (_b + 1) - 1 for _b in range(_k)]
assert len(LAST_TILE) == N_TRUNK


def constants():
    ones = np.ones((P, P), np.float32)
    ident = np.eye(P, dtype=np.float32)
    half = ROPE // 2
    rot = np.zeros((P, P), np.float32)
    for b in range(P // ROPE):
        for i in range(half):
            rot[b * ROPE + half + i, b * ROPE + i] = -1.0
            rot[b * ROPE + i, b * ROPE + half + i] = 1.0
    before = np.triu(ones, 1)
    ramp = np.broadcast_to(np.arange(P, dtype=np.float32), (P, P))
    pos = np.concatenate([np.arange(TP), PAST + np.arange(TS)]).astype(np.float32)
    inv = (np.float32(10000.0) ** (-np.arange(half, dtype=np.float32) / np.float32(half))).astype(np.float32)
    ang = (pos[None, :] * inv[:, None]).astype(np.float32)
    cos = np.tile(np.cos(ang), (P // half, 1)).astype(np.float32)
    sin = np.tile(np.sin(ang), (P // half, 1)).astype(np.float32)
    eps = np.tile(np.array([[EPS_LN, EPS_RMS]], np.float32), (P, 1))
    base = np.broadcast_to(np.arange(E, dtype=np.float32) * P, (P, E))
    return np.ascontiguousarray(np.concatenate([ones, ident, rot, before, ramp, cos, sin, eps, base], axis=1))


C_ONES, C_ID, C_ROT, C_BEF, C_RAMP, C_COS = 0, 128, 256, 384, 512, 640
C_SIN = C_COS + T
C_EPS = C_SIN + T
C_BASE = C_EPS + 2
N_CONST = C_BASE + E


def build(nc, a, out):
    with ExitStack() as ctx:
        def sb(name, shape, dt=F32):
            return ctx.enter_context(nc.sbuf_tensor(name, shape, dt))

        names = {}

        def sem(name):
            if name not in names:
                names[name] = ctx.enter_context(nc.semaphore(name))
            return names[name]

        ring = [sb(f"ring{i}", [P, BLK]) for i in range(SLOTS)]
        const = sb("const", [P, N_CONST])
        vec = sb("vec", [P, N_VEC])
        work = sb("work", [P, 22464])
        w_router = sb("w_router", [P, DC, E])
        small = sb("small", [P, 400])
        table = sb("table", [P, 16], I32)
        maxidx = sb("maxidx", [P, 3, 8], U32)
        bank = [ctx.enter_context(nc.psum_tensor(f"bank{i}", [P, 512], F32)) for i in range(8)]

        ones, ident, rot_m = const[:, 0:128], const[:, 128:256], const[:, 256:384]
        before, ramp = const[:, C_BEF:C_BEF + P], const[:, C_RAMP:C_RAMP + P]
        cos, sin = const[:, C_COS:C_COS + T], const[:, C_SIN:C_SIN + T]
        eps_ln, eps_rms = const[:, C_EPS:C_EPS + 1], const[:, C_EPS + 1:C_EPS + 2]

        def area(at, chunks, width):
            return work[:, at:at + chunks * width].rearrange("p (c t) -> p c t", c=chunks)

        x = area(0, DC, T)
        raw = area(2304, 6, T)
        cqn = area(2304 + 6 * T, QC, T)
        att = area(2304, DC, T)
        qn = area(4896, DC, T)
        qr = area(7200, 4, T)
        qr_raw = area(8352, 4, T)
        kT = area(9504, H, KEYS)
        res = area(9504, DC, T)
        v = area(12832, 4, 1024)
        sq = area(12832, DC, T)
        lat = area(16928, KC, KEYS)
        kr = work[:, 17760:18176]
        probs = area(18176, 2, 544)
        probsT = area(19264, 2, 448)
        rope_tmp = area(18176, 4, T)
        kr_tmp = area(20160, 2, T)
        stat = area(20160, 4, T)
        ple_p = [area(21312, PC, T), area(21888, PC, T)]
        hid = area(2304, FC, T)
        sil = area(8640, 3, T)
        ple_s = area(2304, DC, T)
        gm_v = area(2304, DC, T)
        gm_u = area(4608, DC, T)
        gm_bias = area(6912, 8, T)
        gm_vtok = area(15136, 8, 3 * P)
        gm_w = area(18208, 8, P)
        gm_tmp = area(19232, 2, T)
        xtok = area(2304, 3, D)
        xg = area(5376, DC, P)
        hbuf = area(6400, 2, 512)
        sbuf = area(7424, 2, 512)
        y_sl = work[:, 8448:9472]
        hT = area(11808, 28, P)
        onehot = area(15392, 3, P)
        onehot_c = area(15776, 3, P)
        eq = area(16160, 6, P)
        ct = work[:, 16928:16928 + T]
        sm = small
        mx = sm[:, 0:6].rearrange("p (b c) -> p b c", b=2)
        nmx = sm[:, 6:12].rearrange("p (b c) -> p b c", b=2)
        psum_r = sm[:, 12:18].rearrange("p (b c) -> p b c", b=2)
        prec = sm[:, 18:24].rearrange("p (b c) -> p b c", b=2)
        lg = sm[:, 24:48].rearrange("p (b c) -> p b c", b=3)
        mx8 = sm[:, 48:72].rearrange("p (b c) -> p b c", b=3)
        idx = sm[:, 72:96].rearrange("p (b c) -> p b c", b=3)
        oneA = sm[:, 96:120].rearrange("p (b c) -> p b c", b=3)
        oneB = sm[:, 120:144].rearrange("p (b c) -> p b c", b=3)
        sel = sm[:, 144:168].rearrange("p (b c) -> p b c", b=3)
        rank = sm[:, 168:200].rearrange("p (b c) -> p b c", b=4)
        big = sm[:, 200:224].rearrange("p (b c) -> p b c", b=3)
        slot_of = sm[:, 224:248].rearrange("p (b c) -> p b c", b=3)
        picked = sm[:, 248:296].rearrange("p (k b c) -> p k b c", k=2, b=3)
        where = sm[:, 296:302].rearrange("p (k b) -> p k b", k=2)
        share = sm[:, 302:308].rearrange("p (k b) -> p k b", k=2)
        over1, over, cum, shift = sm[:, 308:316], sm[:, 316:324], sm[:, 324:333], sm[:, 333:341]
        diff, e2, den, rden = sm[:, 341:344], sm[:, 344:347], sm[:, 347:350], sm[:, 350:353]
        ids = sm[:, 353:367]
        cmp = sm[:, 370:374]

        free_by = {}

        def filled(eng, name, i=0):
            n = TILE[name] + i
            eng.wait_ge(sem("tile_filled"), n + 1)
            return bank[n % 8]

        def filled_at(eng, n):
            eng.wait_ge(sem("tile_filled"), n + 1)
            return bank[n % 8]

        def frees(name, i, signal, value):
            free_by[TILE[name] + i] = (signal, value)

        block = ctx.enter_context(nc.Block())
        LN_OF = {0: "att_out", 1: "down", 3: "gm_out"}

        @block.vector
        def _(dve):
            def residual(n):
                for c in range(DC):
                    ps = filled(dve, LN_OF[n], c)
                    dve.scalar_tensor_tensor(res[:, c, :], x[:, c, :], ALPHA, ps[:, 0:T], ALU.mult,
                                             ALU.add).then_inc(sem("residual"), 1)
                    frees(LN_OF[n], c, "residual", 8 * len(done) + c + 1)
                    add_up(c, "residual", 8 * len(done) + c + 1)
                done.append(n)

            def add_up(c, signal, value):
                if c == 0:
                    return
                dve.wait_ge(sem(signal), value)
                first = res[:, 0, :] if c == 1 else stat[:, 0, :]
                if c > 1:
                    dve.wait_ge(sem("summed"), sums[0])
                dve.tensor_tensor(stat[:, 0, :], first, res[:, c, :], ALU.add).then_inc(sem("summed"), 1)
                sums[0] += 1

            def normalise(n):
                mean = filled(dve, f"ln{n}", 0)
                for c in range(DC):
                    dve.scalar_tensor_tensor(res[:, c, :], mean[:, 0:T], -1.0 / D, res[:, c, :], ALU.mult,
                                             ALU.add).then_inc(sem("centred"), 1)
                frees(f"ln{n}", 0, "centred", 8 * n + 8)
                for c in range(1, DC):
                    dve.wait_ge(sem("squared"), 8 * n + c + 1)
                    first = sq[:, 0, :] if c == 1 else stat[:, 1, :]
                    if c > 1:
                        dve.wait_ge(sem("sq_summed"), 7 * n + c - 1)
                    dve.tensor_tensor(stat[:, 1, :], first, sq[:, c, :], ALU.add).then_inc(sem("sq_summed"), 1)
                dve.wait_ge(sem("deviation"), n + 1)
                dve.reciprocal(stat[:, 3, :], stat[:, 2, :]).then_inc(sem("rstd"), 1)
                dve.wait_ge(sem("rstd"), n + 1)
                for c in range(DC):
                    dve.tensor_tensor(res[:, c, :], res[:, c, :], stat[:, 3, :], ALU.mult)\
                       .then_inc(sem("scaled"), 1)

            def ple(n):
                for c in range(DC):
                    ps = filled(dve, f"proj{n}", c)
                    dve.wait_ge(sem("ple_sigmoid"), 8 * n + c + 1)
                    dve.tensor_tensor(ple_s[:, c, :], ple_s[:, c, :], ps[:, 0:T], ALU.mult)\
                       .then_inc(sem("ple_gated"), 1)
                    frees(f"proj{n}", c, "ple_gated", 8 * n + c + 1)
                    dve.wait_ge(sem("ple_gated"), 8 * n + c + 1)
                    dve.tensor_tensor(x[:, c, :], x[:, c, :], ple_s[:, c, :], ALU.add)\
                       .then_inc(sem("ple_added"), 1)

            done, sums = [], [0]
            dve.memset(small[:, :], 0.0).then_inc(sem("small_zero"), 1)
            for i in range(2):
                dve.wait_ge(sem("rms_dev"), i + 1)
                dve.reciprocal(stat[:, 2 + i, :], stat[:, i, :]).then_inc(sem("rms_rstd"), 1)
                dve.wait_ge(sem("rms_rstd"), i + 1)
                for c in (range(QC) if i == 0 else range(QC, QC + KC)):
                    to = cqn[:, c, :] if c < QC else lat[:, c - QC, 0:T]
                    dve.scalar_tensor_tensor(to, raw[:, c, :], vec[:, G_Q + c:G_Q + c + 1], stat[:, 2 + i, :],
                                             ALU.mult, ALU.mult).then_inc(sem("latent"), 1)
            dve.wait_ge(sem("in_copied"), 6)
            dve.tensor_tensor(kr[:, 0:T], raw[:, 5, :], cos, ALU.mult).then_inc(sem("kr_part"), 1)
            ps = filled(dve, "krot")
            dve.tensor_tensor(rope_tmp[:, 0, :], ps[:, 0:T], sin, ALU.mult).then_inc(sem("kr_part"), 1)
            frees("krot", 0, "kr_part", 2)
            dve.wait_ge(sem("kr_part"), 2)
            dve.tensor_tensor(kr[:, 0:T], kr[:, 0:T], rope_tmp[:, 0, :], ALU.add).then_inc(sem("kr_ready"), 1)
            for c in range(4):
                dve.wait_ge(sem("qr_copied"), c + 1)
                dve.tensor_tensor(qr[:, c, :], qr_raw[:, c, :], cos, ALU.mult).then_inc(sem("qr_part"), 1)
                ps = filled(dve, "qrot", c)
                if c == 0:
                    dve.wait_ge(sem("kr_ready"), 1)
                dve.tensor_tensor(rope_tmp[:, c, :], ps[:, 0:T], sin, ALU.mult).then_inc(sem("qr_part"), 1)
                frees("qrot", c, "qr_part", 2 * c + 2)
                dve.wait_ge(sem("qr_part"), 2 * c + 2)
                dve.tensor_tensor(qr[:, c, :], qr[:, c, :], rope_tmp[:, c, :], ALU.add)\
                   .then_inc(sem("qr_ready"), 1)
            dve.wait_ge(sem("qr_ready"), 4)
            dve.memset(probs[:, :, :], 0.0).then_inc(sem("probs_zero"), 1)
            for i in range(8):
                ps = filled(dve, "vup", i)
                rows = P if i < 6 else TS
                dve.tensor_copy(v[0:rows, i // 2, 512 * (i % 2):512 * (i % 2) + 512], ps[0:rows, :])\
                   .then_inc(sem("v_ready"), 1)
                frees("vup", i, "v_ready", i + 1)

            def regions(h, ps_p, ps_s):
                b = probs[:, h % 2, :]
                out_ = []
                for blk, at in ((0, 0), (1, P)):
                    for half in range(2):
                        rows = slice(CHUNK * half, CHUNK * half + CHUNK)
                        n = P * blk + CHUNK * (half + 1)
                        out_.append((ps_p[rows, at:at + n], b[rows, at:at + n], rows, blk))
                out_.append((ps_s[0:TS, 0:TS + PAST], b[0:TS, 384:384 + TS + PAST], slice(0, TS), 2))
                return out_

            def row_max(h):
                n = ATT["S", h]
                ps_p, ps_s = filled_at(dve, n), filled_at(dve, n + 1)
                if h == 0:
                    dve.wait_ge(sem("small_zero"), 1)
                for s, _, rows, col in regions(h, ps_p, ps_s):
                    dve.tensor_reduce(mx[rows, h % 2, col:col + 1], s, AX_X, ALU.max).then_inc(sem("row_max"), 1)
                dve.wait_ge(sem("row_max"), 5 * h + 5)
                if h >= 2:
                    dve.wait_ge(sem("exp_done"), 5 * (h - 1))
                dve.tensor_scalar(nmx[:, h % 2, :], mx[:, h % 2, :], -SCALE, None, ALU.mult)\
                   .then_inc(sem("neg_max"), 1)

            def row_scale(h):
                dve.wait_ge(sem("exp_done"), 5 * h + 5)
                if h == 0:
                    dve.wait_ge(sem("probs_zero"), 1)
                for i, rows in enumerate((P, P, TS)):
                    dve.reciprocal(prec[0:rows, h % 2, i:i + 1], psum_r[0:rows, h % 2, i:i + 1])\
                       .then_inc(sem("row_recip"), 1)
                dve.wait_ge(sem("row_recip"), 3 * h + 3)
                for i, (rows, lo, hi) in enumerate(((P, 0, P), (P, P, 3 * P), (TS, 384, 384 + TS + PAST))):
                    t = probs[0:rows, h % 2, lo:hi]
                    dve.tensor_scalar(t, t, prec[0:rows, h % 2, i:i + 1], None, ALU.mult)\
                       .then_inc(sem("probs_ready"), 1)

            def head_out(h):
                ps = filled_at(dve, ATT["O", h])
                dve.tensor_copy(att[:, h, :], ps[:, 0:T]).then_inc(sem("head_out"), 1)
                free_by[ATT["O", h]] = ("head_out", h + 1)

            row_max(0)
            for h in range(H):
                if h + 1 < H:
                    row_max(h + 1)
                row_scale(h)
                if h:
                    head_out(h - 1)
            head_out(H - 1)
            residual(0)
            normalise(0)
            for i in range(FC):
                ps = filled(dve, "ffn", 2 * i + 1)
                dve.wait_ge(sem("ffn_silu"), i + 1)
                dve.tensor_tensor(hid[:, i, :], sil[:, i % 3, :], ps[:, 0:T], ALU.mult).then_inc(sem("ffn_hidden"), 1)
                frees("ffn", 2 * i + 1, "ffn_hidden", i + 1)
            residual(1)
            normalise(1)
            ple(0)
            for c in range(1, DC):
                add_up(c, "gelu", c + 1)
            normalise(2)
            dve.wait_ge(sem("gm_loaded"), 32)
            for g in range(8):
                ps = filled(dve, "mix", g)
                dve.tensor_tensor(gm_tmp[:, g % 2, :], ps[:, 0:T], gm_bias[:, g, :], ALU.add)\
                   .then_inc(sem("mix_biased"), 1)
                frees("mix", g, "mix_biased", g + 1)
                dve.wait_ge(sem("mix_biased"), g + 1)
                dve.tensor_tensor(gm_u[:, g, :], gm_u[:, g, :], gm_tmp[:, g % 2, :], ALU.mult)\
                   .then_inc(sem("mixed"), 1)
            residual(3)
            normalise(3)

            route = [0]

            def r_(ins):
                ins.then_inc(sem("route_step"), 1)
                route[0] += 1
                dve.wait_ge(sem("route_step"), route[0])

            ps = filled(dve, "logits")
            for i, rows in enumerate((P, P, TS)):
                r_(dve.tensor_copy(lg[0:rows, i, :], ps[0:rows, 8 * i:8 * i + 8]))
                r_(dve.max(mx8[0:rows, i, :], lg[0:rows, i, :]))
                r_(dve.max_index(maxidx[0:rows, i, :], mx8[0:rows, i, :], lg[0:rows, i, :]))
                r_(dve.tensor_copy(idx[0:rows, i, :], maxidx[0:rows, i, :]))
                r_(dve.tensor_scalar(oneA[0:rows, i, :], ramp[0:rows, 0:8], idx[0:rows, i, 0:1], None, ALU.is_equal))
                r_(dve.tensor_scalar(oneB[0:rows, i, :], ramp[0:rows, 0:8], idx[0:rows, i, 1:2], None, ALU.is_equal))
                r_(dve.tensor_tensor(sel[0:rows, i, :], oneA[0:rows, i, :], oneB[0:rows, i, :], ALU.add))
                r_(dve.tensor_tensor(diff[0:rows, i:i + 1], mx8[0:rows, i, 1:2], mx8[0:rows, i, 0:1], ALU.subtract))
            frees("logits", 0, "route_step", route[0])
            dve.wait_ge(sem("share_exp"), 1)
            r_(dve.tensor_scalar(den[:, :], e2[:, :], 1.0, None, ALU.add))
            r_(dve.reciprocal(share[:, 0, :], den[:, :]))
            r_(dve.tensor_tensor(share[:, 1, :], share[:, 0, :], e2[:, :], ALU.mult))
            ps = filled(dve, "rank")
            r_(dve.tensor_copy(rank[:, :, :], ps[:, 0:32].rearrange("p (b c) -> p b c", b=4)))
            frees("rank", 0, "route_step", route[0])
            r_(dve.tensor_scalar(over1[:, :], rank[:, 3, :], float(P), None, ALU.is_gt))
            r_(dve.tensor_scalar(over[:, :], rank[:, 3, :], float(2 * P), None, ALU.is_gt))
            r_(dve.tensor_tensor(over[:, :], over[:, :], over1[:, :], ALU.add))
            for e in range(E):
                r_(dve.tensor_tensor(cum[:, e + 1:e + 2], cum[:, e:e + 1], over[:, e:e + 1], ALU.add))
            r_(dve.tensor_scalar(shift[:, :], cum[:, 0:E], float(P), float(P * (E - 1)), ALU.mult, ALU.add))
            r_(dve.tensor_tensor(shift[:, :], shift[:, :], const[:, C_BASE:C_BASE + E], ALU.subtract))
            for i in range(3):
                r_(dve.tensor_scalar(big[:, i, :], rank[:, i, :], float(P), None, ALU.is_ge))
                r_(dve.tensor_tensor(big[:, i, :], big[:, i, :], shift[:, :], ALU.mult))
                r_(dve.tensor_tensor(big[:, i, :], big[:, i, :], rank[:, i, :], ALU.add))
                r_(dve.tensor_tensor(big[:, i, :], big[:, i, :], const[:, C_BASE:C_BASE + E], ALU.add))
                r_(dve.tensor_scalar(slot_of[:, i, :], big[:, i, :], 1.0, None, ALU.add))
                for k, one in enumerate((oneA, oneB)):
                    r_(dve.tensor_tensor(picked[:, k, i, :], slot_of[:, i, :], one[:, i, :], ALU.mult))
                    r_(dve.tensor_reduce(where[:, k, i:i + 1], picked[:, k, i, :], AX_X, ALU.add))
            r_(dve.tensor_scalar(where[:, :, :], where[:, :, :], -1.0, None, ALU.add))
            r_(dve.tensor_copy(ids[:, 0:12], ramp[:, 0:12]))
            r_(dve.memset(ids[:, 8:12], 0.0))
            for e in range(E - 1):
                r_(dve.tensor_scalar(cmp[:, 0:4], ramp[:, 0:4], cum[:, e + 1:e + 2], None, ALU.is_ge))
                r_(dve.tensor_tensor(ids[:, 8:12], ids[:, 8:12], cmp[:, 0:4], ALU.add))
            r_(dve.tensor_scalar(ids[:, 12:13], cum[:, E:E + 1], float(E), None, ALU.add))
            r_(dve.tensor_scalar(ids[:, 13:14], ids[:, 12:13], -1.0, None, ALU.add))
            dve.tensor_copy(table[:, 0:14], ids[:, 0:14]).then_inc(sem("table_ready"), 1)
            dve.wait_ge(sem("normed"), 8 * 4)
            for c in range(DC):
                s = "res_started" if c < DC - 1 else "added"
                dve.tensor_scalar(res[:, c, :], x[:, c, :], ALPHA, None, ALU.mult).then_inc(sem(s), 1)
            dve.wait_ge(sem("table_ready"), 1)
            tiles = dve.value_load(table[0:1, 12:13], min_val=E, max_val=MAX_TILES)
            with dve.Fori(0, tiles) as t:
                for i in range(3):
                    g0, g1 = where[:, 0, i:i + 1], where[:, 1, i:i + 1]
                    dve.tensor_scalar(eq[:, i, :], ramp, g0, None, ALU.is_equal).then_inc(sem("eq_a"), 1)
                    dve.tensor_scalar(eq[:, 3 + i, :], ramp, g1, share[:, 1, i:i + 1], ALU.is_equal, ALU.mult)\
                       .then_inc(sem("eq_a"), 1)
                    dve.wait_ge(sem("eq_a"), t * 6 + (2 * i + 2))
                    dve.scalar_tensor_tensor(onehot[:, i, :], ramp, g1, eq[:, i, :], ALU.is_equal, ALU.add)\
                       .then_inc(sem("onehot_ready"), 1)
                    dve.scalar_tensor_tensor(onehot_c[:, i, :], eq[:, i, :], share[:, 0, i:i + 1],
                                             eq[:, 3 + i, :], ALU.mult, ALU.add).then_inc(sem("onehot_c_ready"), 1)
                dve.wait_ge(sem("gathered"), t * 2 + 2)
                dve.tensor_copy(xg[:, 4:8, :], bank[5][:, :].rearrange("p (c s) -> p c s", c=4))\
                   .then_inc(sem("xg_high"), 1)
                for f in range(FB):
                    dve.wait_ge(sem("block_used"), t * EB + (2 * f + 2))
                    dve.wait_ge(sem("silu_done"), t * FB + (f + 1))
                    if f >= 2:
                        dve.wait_ge(sem("turned"), t * FB + (f - 1))
                    dve.tensor_tensor(hbuf[:, f % 2, :], sbuf[:, f % 2, :], bank[1 + 2 * (f % 2)][:, :], ALU.mult)\
                       .then_inc(sem("hidden_ready"), 1)
                dve.wait_ge(sem("block_used"), t * EB + EB)
                dve.tensor_copy(y_sl[:, 0:512], bank[6][:, :]).then_inc(sem("y_low"), 1)
                dve.tensor_scalar(where[:, :, :], where[:, :, :], -float(P), None, ALU.add)\
                   .then_inc(sem("where_moved"), 1)
                for c in range(DC):
                    dve.wait_ge(sem("scattered"), t * DC + (c + 1))
                    dve.tensor_tensor(res[:, c, :], res[:, c, :], bank[c % 6][:, 0:T], ALU.add)\
                       .then_inc(sem("added"), 1)
                dve.wait_ge(sem("where_moved"), t + 1)
            dve.wait_ge(sem("added"), tiles * DC + 1)
            for c in range(1, DC):
                add_up(c, "table_ready", 1)
            normalise(4)
            ple(1)

        @block.scalar
        def _(act):
            act.dma_start(const[:, :], a["const"]).then_inc(sem("const_loaded"), 16)
            act.dma_start(vec[:, :], a["vec"]).then_inc(sem("vec_loaded"), 16)
            act.dma_start(w_router[:, :, :], a["w_router"]).then_inc(sem("router_loaded"), 16)
            act.dma_start(lat[:, :, T:KEYS], a["cache_lat"]).then_inc(sem("cache_loaded"), 16)
            act.dma_start(kr[:, T:KEYS], a["cache_kr"]).then_inc(sem("cache_kr_loaded"), 16)
            for n in range(2):
                act.dma_start(ple_p[n], a["p"][n]).then_inc(sem(f"p_loaded{n}"), 16)

            def norm_tail(n):
                for c in range(DC):
                    act.wait_ge(sem("centred"), 8 * n + c + 1)
                    act.activation(sq[:, c, :], res[:, c, :], ACT.Square).then_inc(sem("squared"), 1)
                var = filled(act, f"ln{n}", 1)
                act.activation(stat[:, 2, :], var[:, 0:T], ACT.Sqrt, bias=eps_ln, scale=1.0 / D)\
                   .then_inc(sem("deviation"), 1)
                frees(f"ln{n}", 1, "deviation", n + 1)
                to = gm_v if n == 2 else x
                g = G_GM if n == 2 else LN_G[n]
                b = B_GM if n == 2 else LN_B[n]
                for c in range(DC):
                    act.wait_ge(sem("scaled"), 8 * n + c + 1)
                    act.activation(to[:, c, :], res[:, c, :], ACT.Identity, bias=vec[:, b + c:b + c + 1],
                                   scale=vec[:, g + c:g + c + 1]).then_inc(sem("normed"), 1)

            def ple_gate(n):
                for c in range(DC):
                    ps = filled(act, f"gate{n}", c)
                    act.activation(ple_s[:, c, :], ps[:, 0:T], ACT.Sigmoid).then_inc(sem("ple_sigmoid"), 1)
                    frees(f"gate{n}", c, "ple_sigmoid", 8 * n + c + 1)

            act.wait_ge(sem("const_loaded"), 16)
            act.wait_ge(sem("vec_loaded"), 16)
            for c in range(6):
                ps = filled(act, "in", c)
                act.activation(raw[:, c, :], ps[:, 0:T], ACT.Copy).then_inc(sem("in_copied"), 1)
                if c < 5:
                    act.activation(sq[:, c, :], ps[:, 0:T], ACT.Square).then_inc(sem("in_squared"), 1)
                    frees("in", c, "in_squared", c + 1)
            frees("in", 5, "in_copied", 6)
            for i, width in enumerate((QL, KVL)):
                ps = filled(act, "rms", i)
                act.activation(stat[:, i, :], ps[:, 0:T], ACT.Sqrt, bias=eps_rms, scale=1.0 / width)\
                   .then_inc(sem("rms_dev"), 1)
                frees("rms", i, "rms_dev", i + 1)
            for c in range(4):
                ps = filled(act, "qrope", c)
                act.activation(qr_raw[:, c, :], ps[:, 0:T], ACT.Copy).then_inc(sem("qr_copied"), 1)
                frees("qrope", c, "qr_copied", c + 1)
            for c in range(DC):
                ps = filled(act, "qnope", c)
                act.activation(qn[:, c, :], ps[:, 0:T], ACT.Copy).then_inc(sem("qn_ready"), 1)
                frees("qnope", c, "qn_ready", c + 1)
            for c in range(H):
                ps = filled(act, "kup", c)
                act.activation(kT[:, c, :], ps[:, 0:KEYS], ACT.Copy).then_inc(sem("k_ready"), 1)
                frees("kup", c, "k_ready", c + 1)

            def exps(h):
                n = ATT["S", h]
                ps_p, ps_s = bank[n % 8], bank[(n + 1) % 8]
                act.wait_ge(sem("neg_max"), h + 1)
                if h == 0:
                    act.wait_ge(sem("probs_zero"), 1)
                if h >= 2:
                    filled_at(act, ATT["T", h - 2])
                b = probs[:, h % 2, :]
                for blk, at in ((0, 0), (1, P)):
                    for half in range(2):
                        rows = slice(CHUNK * half, CHUNK * half + CHUNK)
                        m = P * blk + CHUNK * (half + 1)
                        act.activation(b[rows, at:at + m], ps_p[rows, at:at + m], ACT.Exp,
                                       bias=nmx[rows, h % 2, blk:blk + 1], scale=SCALE,
                                       accum_out=psum_r[rows, h % 2, blk:blk + 1]).then_inc(sem("exp_done"), 1)
                act.activation(b[0:TS, 384:384 + TS + PAST], ps_s[0:TS, 0:TS + PAST], ACT.Exp,
                               bias=nmx[0:TS, h % 2, 2:3], scale=SCALE,
                               accum_out=psum_r[0:TS, h % 2, 2:3]).then_inc(sem("exp_done"), 1)
                free_by[n] = ("exp_done", 5 * h + 4)
                free_by[n + 1] = ("exp_done", 5 * h + 5)

            def turned_probs(h):
                ps = filled_at(act, ATT["T", h])
                if h >= 2:
                    filled_at(act, ATT["O", h - 2])
                act.activation(probsT[:, h % 2, 0:416], ps[:, 0:416], ACT.Copy).then_inc(sem("probsT_ready"), 1)
                act.activation(probsT[0:TS, h % 2, 416:448], ps[0:TS, 416:448], ACT.Copy)\
                   .then_inc(sem("probsT_ready"), 1)
                free_by[ATT["T", h]] = ("probsT_ready", 2 * h + 2)

            for h in range(H):
                exps(h)
                if h:
                    turned_probs(h - 1)
            turned_probs(H - 1)
            norm_tail(0)
            for i in range(FC):
                ps = filled(act, "ffn", 2 * i)
                if i >= 3:
                    act.wait_ge(sem("ffn_hidden"), i - 2)
                act.activation(sil[:, i % 3, :], ps[:, 0:T], ACT.Silu).then_inc(sem("ffn_silu"), 1)
                frees("ffn", 2 * i, "ffn_silu", i + 1)
            norm_tail(1)
            ple_gate(0)
            for c in range(2 * DC):
                ps = filled(act, "gm", c)
                to = res[:, c, :] if c < DC else gm_u[:, c - DC, :]
                act.activation(to, ps[:, 0:T], ACT.Gelu_apprx_tanh).then_inc(sem("gelu"), 1)
                frees("gm", c, "gelu", c + 1)
            norm_tail(2)
            act.wait_ge(sem("normed"), 24)
            act.dma_start(out["gm_v"], gm_v[:, :, P:T]).then_inc(sem("gm_v_out"), 16)
            act.wait_ge(sem("lat_out"), 16)
            act.wait_ge(sem("kr_out"), 16)
            for g in range(8):
                ps = filled(act, "vtr", g)
                act.activation(gm_vtok[:, g, 0:256], ps[:, 0:256], ACT.Copy).then_inc(sem("vtok"), 1)
                act.activation(gm_vtok[0:TS, g, 256:384], ps[0:TS, 256:384], ACT.Copy).then_inc(sem("vtok"), 1)
                frees("vtr", g, "vtok", 2 * g + 2)
            norm_tail(3)
            act.wait_ge(sem("gm_v_out"), 16)
            for c in range(DC):
                ps = filled(act, "xtr", c)
                act.activation(xtok[:, 0:2, c * P:c * P + P], ps[:, 0:256].rearrange("p (b s) -> p b s", b=2),
                               ACT.Copy).then_inc(sem("xtok"), 1)
                act.activation(xtok[0:TS, 2, c * P:c * P + P], ps[0:TS, 256:384], ACT.Copy)\
                   .then_inc(sem("xtok"), 1)
                frees("xtr", c, "xtok", 2 * c + 2)
            act.wait_ge(sem("route_step"), 24)
            act.activation(e2[:, :], diff[:, :], ACT.Exp).then_inc(sem("share_exp"), 1)

            act.wait_ge(sem("table_ready"), 1)
            tiles = act.value_load(table[0:1, 12:13], min_val=E, max_val=MAX_TILES)
            with act.Fori(0, tiles) as t:
                act.wait_ge(sem("gathered"), t * 2 + 1)
                act.activation(xg[:, 0:4, :], bank[4][:, :].rearrange("p (c s) -> p c s", c=4), ACT.Copy)\
                   .then_inc(sem("xg_low"), 1)

                def turn(f):
                    act.wait_ge(sem("turned"), t * FB + (f + 1))
                    act.activation(hT[:, 4 * f:4 * f + 4, :],
                                   bank[4 + f % 2][:, :].rearrange("p (c s) -> p c s", c=4), ACT.Copy)\
                       .then_inc(sem("hT_ready"), 1)

                for f in range(FB):
                    act.wait_ge(sem("block_used"), t * EB + (2 * f + 1))
                    if f >= 2:
                        act.wait_ge(sem("hidden_ready"), t * FB + (f - 1))
                    act.activation(sbuf[:, f % 2, :], bank[2 * (f % 2)][:, :], ACT.Silu)\
                       .then_inc(sem("silu_done"), 1)
                    if f:
                        turn(f - 1)
                turn(FB - 1)
                act.wait_ge(sem("ct_turned"), t + 1)
                act.activation(ct[:, :], bank[5][:, 0:T], ACT.Copy).then_inc(sem("ct_ready"), 1)
                act.wait_ge(sem("block_used"), t * EB + EB)
                act.activation(y_sl[:, 512:1024], bank[7][:, :], ACT.Copy).then_inc(sem("y_high"), 1)
            norm_tail(4)
            ple_gate(1)

        @block.gpsimd
        def _(pool):
            pool.wait_ge(sem("gm_loaded"), 32)
            pool.affine_select(out=gm_w[:, :, :], in_=gm_w[:, :, :], compare_op=ALU.is_ge, fill=0.0, base=0,
                               pattern=[[0, 8], [1, P]], channel_multiplier=-1).then_inc(sem("gm_masked"), 1)

        @block.tensor
        def _(pe):
            number = [0]

            def claim(n):
                if n >= 8:
                    signal, value = free_by[n - 8]
                    pe.wait_ge(sem(signal), value)
                return bank[n % 8]

            def weights(kc):
                n = number[0]
                number[0] += 1
                pe.wait_ge(sem(f"landed{n % SLOTS}"), 16 * (n // SLOTS + 1))
                return ring[n % SLOTS], kc

            def view(w, kc, m):
                return w[:, 0:kc * m].rearrange("p (k m) -> p k m", k=kc)

            def dense(name, blocks, kc, per, rhs, before_chunk=None, widths=None, load=None):
                i = 0
                for _b in range(blocks):
                    w = load() if load else weights(kc)[0]
                    wv = view(w, kc, per * P)
                    for j in range(per):
                        ps = claim(TILE[name] + i)
                        for k in range(kc):
                            if i == 0 and before_chunk:
                                before_chunk(k)
                            mm = pe.matmul(ps[:, 0:T], wv[:, k, j * P:j * P + P], rhs[:, k, :],
                                           start=(k == 0), stop=(k == kc - 1))
                        mm.then_inc(sem("tile_filled"), 1)
                        i += 1

            def norm_stats(n, summed):
                ps = claim(TILE[f"ln{n}"])
                pe.wait_ge(sem("summed"), summed)
                pe.matmul(ps[:, 0:T], ones, stat[:, 0, :], start=True, stop=True).then_inc(sem("tile_filled"), 1)
                ps = claim(TILE[f"ln{n}"] + 1)
                pe.wait_ge(sem("sq_summed"), 7 * (n + 1))
                pe.matmul(ps[:, 0:T], ones, stat[:, 1, :], start=True, stop=True).then_inc(sem("tile_filled"), 1)

            pe.wait_ge(sem("const_loaded"), 16)
            pe.wait_ge(sem("x_loaded"), 16)
            dense("in", 2, DC, 3, x)
            ps = claim(TILE["rms"])
            for c in range(QC):
                pe.wait_ge(sem("in_squared"), c + 1)
                mm = pe.matmul(ps[:, 0:T], ones, sq[:, c, :], start=(c == 0), stop=(c == QC - 1))
            mm.then_inc(sem("tile_filled"), 1)
            ps = claim(TILE["rms"] + 1)
            for c in range(KC):
                pe.wait_ge(sem("in_squared"), QC + c + 1)
                mm = pe.matmul(ps[:, 0:T], ones, sq[:, QC + c, :], start=(c == 0), stop=(c == KC - 1))
            mm.then_inc(sem("tile_filled"), 1)
            ps = claim(TILE["krot"])
            pe.wait_ge(sem("in_copied"), 6)
            pe.matmul(ps[:, 0:T], rot_m, raw[:, 5, :], start=True, stop=True).then_inc(sem("tile_filled"), 1)
            for b in range(2):
                wv = view(weights(QC)[0], QC, 6 * P)
                for j in range(6):
                    i = 6 * b + j
                    ps = claim(TILE["qrope"] + i)
                    for k in range(QC):
                        pe.wait_ge(sem("latent"), k + 1)
                        mm = pe.matmul(ps[:, 0:T], wv[:, k, j * P:j * P + P], cqn[:, k, :],
                                       start=(k == 0), stop=(k == QC - 1))
                    mm.then_inc(sem("tile_filled"), 1)
            for c in range(4):
                ps = claim(TILE["qrot"] + c)
                pe.wait_ge(sem("qr_copied"), c + 1)
                pe.matmul(ps[:, 0:T], rot_m, qr_raw[:, c, :], start=True, stop=True).then_inc(sem("tile_filled"), 1)
            pe.wait_ge(sem("latent"), QC + KC)
            pe.wait_ge(sem("cache_loaded"), 16)
            wv = view(weights(KC)[0], KC, 2048)
            for h in range(H):
                ps = claim(TILE["kup"] + h)
                for k in range(KC):
                    mm = pe.matmul(ps[:, 0:KEYS], wv[:, k, h * P:h * P + P], lat[:, k, :],
                                   start=(k == 0), stop=(k == KC - 1))
                mm.then_inc(sem("tile_filled"), 1)
            for i in range(8):
                ps = claim(TILE["vup"] + i)
                rows = P if i < 6 else TS
                at = P * (i // 2)
                for k in range(KC):
                    mm = pe.matmul(ps[0:rows, :], lat[:, k, at:at + rows],
                                   wv[:, k, 1024 + 512 * (i % 2):1536 + 512 * (i % 2)],
                                   start=(k == 0), stop=(k == KC - 1))
                mm.then_inc(sem("tile_filled"), 1)

            def scores(h):
                if h == 0:
                    pe.wait_ge(sem("kr_ready"), 1)
                    pe.wait_ge(sem("cache_kr_loaded"), 16)
                pe.wait_ge(sem("qn_ready"), h + 1)
                pe.wait_ge(sem("k_ready"), h + 1)
                pe.wait_ge(sem("qr_ready"), h // 2 + 1)
                rr = slice(ROPE * (h % 2), ROPE * (h % 2) + ROPE)
                n = ATT["S", h]
                for ps, parts in ((claim(n), ((0, P, 0, P, 0), (P, 2 * P, 0, 2 * P, P))),
                                  (claim(n + 1), ((TP, T, TP, KEYS, 0),))):
                    for q0, q1, k0, k1, at in parts:
                        o = ps[0:q1 - q0, at:at + k1 - k0]
                        pe.matmul(o, qn[:, h, q0:q1], kT[:, h, k0:k1], start=True, stop=False)
                        mm = pe.matmul(o, qr[rr, h // 2, q0:q1], kr[rr, k0:k1], start=False, stop=True)
                    mm.then_inc(sem("tile_filled"), 1)

            def turn_probs(h):
                ps = claim(ATT["T", h])
                pe.wait_ge(sem("probs_ready"), 3 * h + 3)
                b = probs[:, h % 2, :]
                for j in range(3):
                    pe.transpose(ps[:, j * P:j * P + P], b[:, j * P:j * P + P], ident)
                pe.transpose(ps[:, 384:416], b[0:TS, 384:512], ident[0:TS, 0:TS])
                pe.transpose(ps[0:TS, 416:448], b[0:TS, 512:544], ident[0:TS, 0:TS])\
                  .then_inc(sem("tile_filled"), 1)

            def values(h):
                ps = claim(ATT["O", h])
                if h == 0:
                    pe.wait_ge(sem("v_ready"), 8)
                pe.wait_ge(sem("probsT_ready"), 2 * h + 2)
                b, cols = probsT[:, h % 2, :], slice(h * VH, h * VH + VH)
                pe.matmul(ps[:, 0:TP], v[:, 0, cols], b[:, 0:TP], start=True, stop=False)
                pe.matmul(ps[:, P:TP], v[:, 1, cols], b[:, TP:TP + P], start=False, stop=True)
                pe.matmul(ps[:, TP:T], v[:, 2, cols], b[:, 384:416], start=True, stop=False)
                pe.matmul(ps[:, TP:T], v[0:TS, 3, cols], b[0:TS, 416:448], start=False, stop=True)\
                  .then_inc(sem("tile_filled"), 1)

            scores(0)
            for h in range(H):
                if h + 1 < H:
                    scores(h + 1)
                turn_probs(h)
                if h:
                    values(h - 1)
            values(H - 1)
            dense("att_out", 2, DC, 4, att, lambda k: pe.wait_ge(sem("head_out"), k + 1))
            norm_stats(0, 7)
            dense("ffn", 11, DC, 4, x, lambda k: pe.wait_ge(sem("normed"), k + 1))
            dense("down", 8, FC, 1, hid, lambda k: pe.wait_ge(sem("ffn_hidden"), k + 1))
            norm_stats(1, 14)
            dense("gate0", 2, DC, 4, x, lambda k: pe.wait_ge(sem("normed"), 8 + k + 1))
            pe.wait_ge(sem("p_loaded0"), 16)
            dense("proj0", 1, PC, 8, ple_p[0])
            dense("gm", 4, DC, 4, x, lambda k: pe.wait_ge(sem("ple_added"), k + 1))
            norm_stats(2, 21)
            for g in range(8):
                ps = claim(TILE["vtr"] + g)
                pe.wait_ge(sem("normed"), 16 + g + 1)
                pe.transpose(ps[:, 0:P], gm_v[:, g, 0:P], ident)
                pe.transpose(ps[:, P:2 * P], gm_v[:, g, P:2 * P], ident)
                pe.transpose(ps[0:TS, 2 * P:3 * P], gm_v[:, g, TP:T], ident).then_inc(sem("tile_filled"), 1)
            pe.wait_ge(sem("gm_masked"), 1)
            for g in range(8):
                ps = claim(TILE["mix"] + g)
                pe.wait_ge(sem("vtok"), 2 * g + 2)
                for b in range(2):
                    pe.matmul(ps[:, b * P:b * P + P], gm_vtok[:, g, b * P:b * P + P], gm_w[:, g, :],
                              start=True, stop=True)
                pe.matmul(ps[:, TP:T], gm_vtok[0:TS, g, 2 * P:3 * P], gm_w[0:TS, g, 0:TS], start=True, stop=True)\
                  .then_inc(sem("tile_filled"), 1)
            dense("gm_out", 2, DC, 4, gm_u, lambda k: pe.wait_ge(sem("mixed"), k + 1))
            norm_stats(3, 28)
            ps = claim(TILE["logits"])
            pe.wait_ge(sem("router_loaded"), 16)
            pe.wait_ge(sem("normed"), 32)
            for i, rows in enumerate((P, P, TS)):
                for k in range(DC):
                    mm = pe.matmul(ps[0:rows, 8 * i:8 * i + 8], x[:, k, i * P:i * P + rows], w_router[:, k, :],
                                   start=(k == 0), stop=(k == DC - 1))
            mm.then_inc(sem("tile_filled"), 1)
            for c in range(DC):
                ps = claim(TILE["xtr"] + c)
                pe.transpose(ps[:, 0:P], x[:, c, 0:P], ident)
                pe.transpose(ps[:, P:2 * P], x[:, c, P:2 * P], ident)
                pe.transpose(ps[0:TS, 2 * P:3 * P], x[:, c, TP:T], ident).then_inc(sem("tile_filled"), 1)
            ps = claim(TILE["rank"])
            pe.wait_ge(sem("route_step"), 24)
            for i in range(4):
                o = ps[:, 8 * i:8 * i + 8]
                for j in range(min(i + 1, 3)):
                    mm = pe.matmul(o, before if j == i else ones, sel[:, j, :], start=(j == 0),
                                   stop=(j == min(i, 2)))
            mm.then_inc(sem("tile_filled"), 1)
            for signal, value in (free_by[TILE["rank"]], free_by[TILE["xtr"] + 7]):
                pe.wait_ge(sem(signal), value)

            pe.wait_ge(sem("table_ready"), 1)
            tiles = pe.value_load(table[0:1, 12:13], min_val=E, max_val=MAX_TILES)
            with pe.Fori(0, tiles) as t:
                pe.wait_ge(sem("added"), t * DC + 1)
                pe.wait_ge(sem("onehot_ready"), t * 3 + 3)
                for half in range(2):
                    for c in range(4):
                        d = 4 * half + c
                        for i, rows in enumerate((P, P, TS)):
                            mm = pe.matmul(bank[4 + half][:, c * P:c * P + P],
                                           xtok[0:rows, i, d * P:d * P + P], onehot[0:rows, i, :],
                                           start=(i == 0), stop=(i == 2))
                    mm.then_inc(sem("gathered"), 1)

                def expert_block(j):
                    pe.wait_ge(sem(f"landed{j % SLOTS}"),
                               t * (16 * EB // SLOTS) + 16 * (N_TRUNK // SLOTS + j // SLOTS + 1))
                    return ring[j % SLOTS]

                def turn(f):
                    pe.wait_ge(sem("hidden_ready"), t * FB + (f + 1))
                    if f >= 2:
                        pe.wait_ge(sem("hT_ready"), t * FB + (f - 1))
                    for c in range(4):
                        tr = pe.transpose(bank[4 + f % 2][:, c * P:c * P + P], hbuf[:, f % 2, c * P:c * P + P],
                                          ident)
                    tr.then_inc(sem("turned"), 1)

                for f in range(FB):
                    for k_, freed in enumerate(("silu_done", "hidden_ready")):
                        w = expert_block(2 * f + k_)
                        wv = view(w, DC, 512)
                        if f >= 2:
                            pe.wait_ge(sem(freed), t * FB + (f - 1))
                        for k in range(DC):
                            if f == 0 and k_ == 0:
                                if k == 0:
                                    pe.wait_ge(sem("xg_low"), t + 1)
                                if k == 4:
                                    pe.wait_ge(sem("xg_high"), t + 1)
                            mm = pe.matmul(bank[2 * (f % 2) + k_][:, :], xg[:, k, :], wv[:, k, :],
                                           start=(k == 0), stop=(k == DC - 1))
                        mm.then_inc(sem("block_used"), 1)
                    if f:
                        turn(f - 1)
                for q in range(FB):
                    if q == 1:
                        turn(FB - 1)
                    wv = view(expert_block(2 * FB + q), 4, 1024)
                    pe.wait_ge(sem("hT_ready"), t * FB + (q + 1))
                    for k in range(4):
                        for half in range(2):
                            mm = pe.matmul(bank[6 + half][:, :], hT[:, 4 * q + k, :],
                                           wv[:, k, half * 512:half * 512 + 512],
                                           start=(q == 0 and k == 0), stop=(q == FB - 1 and k == 3))
                    mm.then_inc(sem("block_used"), 1)
                    if q == 2:
                        pe.wait_ge(sem("onehot_c_ready"), t * 3 + 3)
                        pe.wait_ge(sem("hT_ready"), t * FB + 6)
                        for i, rows in enumerate((P, P, TS)):
                            tr = pe.transpose(bank[5][:, i * P:i * P + rows], onehot_c[0:rows, i, :],
                                              ident[0:rows, 0:rows])
                        tr.then_inc(sem("ct_turned"), 1)
                pe.wait_ge(sem("ct_ready"), t + 1)
                pe.wait_ge(sem("y_low"), t + 1)
                for c in range(DC):
                    if c == 4:
                        pe.wait_ge(sem("y_high"), t + 1)
                    if c >= 6:
                        pe.wait_ge(sem("added"), t * DC + (c - 6 + 2))
                    pe.matmul(bank[c % 6][:, 0:T], y_sl[:, c * P:c * P + P], ct[:, :], start=True, stop=True)\
                      .then_inc(sem("scattered"), 1)
            pe.wait_ge(sem("added"), tiles * DC + 1)
            norm_stats(4, 35)

            tail = [0]

            def tail_block():
                s = tail[0]
                tail[0] += 1
                pe.wait_ge(sem(f"landed{s}"), tiles * (16 * EB // SLOTS) + 16 * (N_TRUNK // SLOTS + 1))
                return ring[s]

            dense("gate1", 2, DC, 4, x, lambda k: pe.wait_ge(sem("normed"), 32 + k + 1), load=tail_block)
            pe.wait_ge(sem("p_loaded1"), 16)
            dense("proj1", 1, PC, 8, ple_p[1], load=tail_block)

        @block.sync
        def _(sp):
            sp.dma_start(x, a["x"]).then_inc(sem("x_loaded"), 16)
            n = 0
            for name, blocks, width in TRUNK:
                for b in range(blocks):
                    if n >= SLOTS:
                        sp.wait_ge(sem("tile_filled"), LAST_TILE[n - SLOTS] + 1)
                    sp.dma_start(ring[n % SLOTS][:, 0:width], a[name][b]).then_inc(sem(f"landed{n % SLOTS}"), 16)
                    n += 1
                if name == "mla_out":
                    sp.wait_ge(sem("latent"), QC + KC)
                    sp.dma_start(out["lat"], lat[:, :, 0:T]).then_inc(sem("lat_out"), 16)
                    sp.wait_ge(sem("kr_ready"), 1)
                    sp.dma_start(out["kr"], kr[0:ROPE, 0:T]).then_inc(sem("kr_out"), 16)
                if name == "ffn_down":
                    sp.wait_ge(sem("tile_filled"), TILE["down"] + 8)
                    sp.dma_start(gm_bias[:, :, :], a["gm_bias"].broadcast_to([P, 8 * T]).rearrange("p (g t) -> p g t", g=8))\
                      .then_inc(sem("gm_loaded"), 16)
                    sp.dma_start(gm_w[:, :, :], a["gm_w"]).then_inc(sem("gm_loaded"), 16)
            for j in range(SLOTS):
                sp.wait_ge(sem("tile_filled"), LAST_TILE[N_TRUNK - SLOTS + j] + 1)
                sp.dma_start(ring[j][:, :], a["moe"][0, j]).then_inc(sem(f"landed{j}"), 16)
            sp.wait_ge(sem("table_ready"), 1)
            last = sp.value_load(table[0:1, 13:14], min_val=E - 1, max_val=MAX_TILES - 1)

            def expert_load(t, e, j):
                sp.wait_ge(sem("block_used"), t * EB + (j - SLOTS + 1))
                sp.dma_start(ring[j % SLOTS][:, :], a["moe"][bass.ds(e, 1), j % EB].rearrange("a p n -> p (a n)"))\
                  .then_inc(sem(f"landed{j % SLOTS}"), 16)

            with sp.Fori(0, last) as t:
                e = sp.value_load(table[0:1, bass.ds(t, 1)], min_val=0, max_val=E - 1)
                for j in range(SLOTS, EB):
                    expert_load(t, e, j)
                e = sp.value_load(table[0:1, bass.ds(t + 1, 1)], min_val=0, max_val=E - 1)
                for j in range(SLOTS):
                    expert_load(t, e, EB + j)
            e = sp.value_load(table[0:1, bass.ds(last, 1)], min_val=0, max_val=E - 1)
            for j in range(SLOTS, EB):
                expert_load(last, e, j)
            s = 0
            for name, blocks, width in TAIL:
                for b in range(blocks):
                    sp.wait_ge(sem("block_used"), last * EB + (EB + s - SLOTS + 1))
                    sp.dma_start(ring[s][:, 0:width], a[name][b]).then_inc(sem(f"landed{s}"), 16)
                    s += 1
            sp.wait_ge(sem("ple_added"), 16)
            sp.dma_start(out["y"], x).then_inc(sem("y_out"), 16)
            for name in ("lat_out", "kr_out", "gm_v_out", "y_out"):
                sp.wait_ge(sem(name), 16)


def by_chunk(w, kc, per):
    n = w.shape[1] // (per * P)
    return np.ascontiguousarray(w.reshape(kc, P, n, per * P).transpose(2, 1, 0, 3).reshape(n, P, kc * per * P))


def feature_major(x):
    return np.ascontiguousarray(x.T.reshape(-1, P, x.shape[0]).transpose(1, 0, 2))


def token_major(x):
    return np.ascontiguousarray(x.transpose(1, 0, 2).reshape(-1, x.shape[2]).T)


def kernel(**inputs):
    import concourse.bacc as bacc
    from concourse.bass_utils import run_bass_kernel_spmd

    i = {k: np.asarray(v) for k, v in inputs.items()}
    w_in = i["w_mla_in"][0]
    w_in = np.concatenate([w_in, w_in[:, QL + KVL:]], axis=1)
    w_q = i["w_q_up"][0].reshape(QL, H, NOPE + ROPE)
    w_q = np.concatenate([w_q[:, :, NOPE:].reshape(QL, -1), w_q[:, :, :NOPE].reshape(QL, -1)], axis=1)
    w_kv = i["w_kv_up"][0].reshape(KVL, H, NOPE + VH)
    w_kv = np.concatenate([w_kv[:, :, :NOPE].reshape(KVL, -1), w_kv[:, :, NOPE:].reshape(KVL, -1)], axis=1)
    w_f = np.stack([i["w_ffn_gate"][0].reshape(D, FC, P), i["w_ffn_up"][0].reshape(D, FC, P)], axis=2)
    w_gm = i["w_gm_in"][0]
    w_gm = np.concatenate([w_gm[:, D:], w_gm[:, :D]], axis=1)
    moe = np.empty((E, EB, P, BLK), np.float32)
    for e in range(E):
        for k, name in enumerate(("w_moe_gate", "w_moe_up")):
            moe[e, k:2 * FB:2] = i[name][0, e].reshape(DC, P, FB, 512).transpose(2, 1, 0, 3).reshape(FB, P, BLK)
        moe[e, 2 * FB:] = i["w_moe_down"][0, e].reshape(FB, 4, P, D).transpose(0, 2, 1, 3).reshape(FB, P, BLK)
    cols = [i["g_q_norm"][0].reshape(QC, P), i["g_kv_norm"][0].reshape(KC, P), i["g_gm_norm"][0].reshape(DC, P),
            i["b_gm_norm"][0].reshape(DC, P)]
    for name in ("ln1_g", "ln2_g", "ln1_b", "ln2_b"):
        cols.append(i[name].reshape(2 * DC, P))
    b_s = i["b_gm_spatial"][0]
    arrays = {
        "x": feature_major(np.concatenate([i["x_prompt"][0], i["x_sample"][0]])),
        "cache_lat": feature_major(i["cache_mla_latent"][0, 0]),
        "cache_kr": np.ascontiguousarray(np.concatenate([i["cache_mla_krope"][0, 0].T] * 2)),
        "p": np.stack([feature_major(np.concatenate([i["p_prompt"][n, 0], i["p_sample"][n, 0]])) for n in range(2)]),
        "vec": np.ascontiguousarray(np.concatenate(cols).T),
        "w_router": np.ascontiguousarray(i["w_router"][0].reshape(DC, P, E).transpose(1, 0, 2)),
        "gm_w": np.ascontiguousarray(i["w_gm_spatial"][0].transpose(2, 0, 1)),
        "gm_bias": np.ascontiguousarray(np.concatenate([b_s, b_s, b_s[:, :TS]], axis=1).reshape(1, 8 * T)),
        "mla_in": by_chunk(w_in, DC, 3), "q_up": by_chunk(w_q, QC, 6), "kv_up": by_chunk(w_kv, KC, 16),
        "mla_out": by_chunk(i["w_mla_out"][0], DC, 4), "ffn_in": by_chunk(w_f.reshape(D, -1), DC, 4),
        "ffn_down": by_chunk(i["w_ffn_down"][0], FC, 1), "gm_in": by_chunk(w_gm, DC, 4),
        "gm_out": by_chunk(i["w_gm_out"][0], DC, 4), "moe": moe,
    }
    for n in range(2):
        arrays[f"ple_gate{n}"] = by_chunk(i["w_ple_gate"][n], DC, 4)
        arrays[f"ple_proj{n}"] = by_chunk(i["w_ple_proj"][n], PC, 8)
    outputs = {"lat": (P, KC, T), "kr": (ROPE, T), "gm_v": (P, DC, GM_CHUNK + TS), "y": (P, DC, T)}

    nc = bacc.Bacc("TRN2", target_bir_lowering=False, num_devices=1)
    a = {n: nc.dram_tensor(f"in_{n}", v.shape, F32, kind="ExternalInput").ap() for n, v in arrays.items()}
    a["const"] = nc.inline_tensor(constants(), "tables")[:, :]
    out = {n: nc.dram_tensor(f"out_{n}", s, F32, kind="ExternalOutput").ap() for n, s in outputs.items()}
    build(nc, a, out)
    r = run_bass_kernel_spmd(nc, [{f"in_{n}": v for n, v in arrays.items()}], core_ids=[0]).results[0]
    y, lat, gm_v = token_major(r["out_y"]), token_major(r["out_lat"]), token_major(r["out_gm_v"])
    kr = np.ascontiguousarray(r["out_kr"].T)
    return (y[None, :TP], y[None, TP:], lat[None, None, :TP], kr[None, None, :TP], lat[None, None, TP:],
            kr[None, None, TP:], gm_v[None, None, :GM_CHUNK], gm_v[None, None, GM_CHUNK:])
```

```python
from contextlib import ExitStack

import numpy as np

import concourse.bass as bass
from concourse import mybir

F32 = mybir.dt.float32
F32R = mybir.dt.float32r
I32 = mybir.dt.int32
U32 = mybir.dt.uint32
ALU = mybir.AluOpType
ACT = mybir.ActivationFunctionType
AX_X = mybir.AxisListType.X

P = 128
D = 1024
DC = D // P
TP, TS = 256, 32
T = TP + TS
PAST = 128
KEYS = T + PAST
CHUNK = 64
H, NOPE, ROPE, VH = 8, 128, 64, 128
QL, KVL = 384, 256
QC, KC = QL // P, KVL // P
FF = 2816
FC = FF // P
E, FE = 8, 3584
FB = FE // 512
PLE = 256
PC = PLE // P
ALPHA = 4.0 ** 0.25
SCALE = (NOPE + ROPE) ** -0.5
EPS_LN, EPS_RMS = 1e-5, 1e-6
GM_CHUNK = 128

SLOTS = 7
TRUNK_SLOTS = 5
BLK = 4096
PIECE = 2048
HIGHS = 3
TRUNK = [("mla_in", 2, DC * 384), ("q_up", 2, QC * 768), ("kv_up", 1, KC * 2048), ("mla_out", 2, DC * 512),
         ("ffn_in", 11, DC * 512), ("ffn_down", 8, FC * 128), ("ple_gate0", 2, DC * 512),
         ("ple_proj0", 1, PC * 1024), ("gm_in", 4, DC * 512), ("gm_out", 2, DC * 512)]
TAIL = [("ple_gate1", 2, DC * 512), ("ple_proj1", 1, PC * 1024)]
N_TRUNK = sum(n for _, n, _ in TRUNK)
EB = 3 * FB
assert N_TRUNK % TRUNK_SLOTS == 0 and EB % SLOTS == 0
MAX_TILES = 12

G_Q, G_KV, G_GM, B_GM = 0, 3, 5, 13
LN_G = {0: 21, 1: 37, 3: 29, 4: 45}
LN_B = {0: 53, 1: 69, 3: 61, 4: 77}
N_VEC = 85

PLAN = [("in", 6), ("rms", 2), ("krot", 1), ("qrope", 4), ("qnope", 8), ("qrot", 4), ("kup", 8), ("vup", 8)]
ATT = {}
_n = sum(n for _, n in PLAN)
ATT["S", 0] = _n
_n += 2
for _h in range(H):
    if _h + 1 < H:
        ATT["S", _h + 1] = _n
        _n += 2
    ATT["T", _h] = _n
    _n += 1
    if _h:
        ATT["O", _h - 1] = _n
        _n += 1
ATT["O", H - 1] = _n
_n += 1
PLAN += [("attention", _n - sum(n for _, n in PLAN)), ("att_out", 8), ("ln0", 2), ("ffn", 4 * 11), ("down", 8),
         ("ln1", 2), ("gate0", 8), ("proj0", 8), ("gm", 16), ("ln2", 2), ("vtr", 8), ("mix", 8), ("gm_out", 8),
         ("ln3", 2), ("logits", 1), ("xtr", 8), ("rank", 1), ("ln4", 2), ("gate1", 8), ("proj1", 8)]
TILE = {}
_n = 0
for _name, _k in PLAN:
    TILE[_name] = _n
    _n += _k

LAST_TILE = []
for _name, _k, _per in (("in", 2, 3), ("qrope", 2, 6), ("kup", 1, 16), ("att_out", 2, 4), ("ffn", 11, 4),
                        ("down", 8, 1), ("gate0", 2, 4), ("proj0", 1, 8), ("gm", 4, 4), ("gm_out", 2, 4)):
    LAST_TILE += [TILE[_name] + _per * (_b + 1) - 1 for _b in range(_k)]
assert len(LAST_TILE) == N_TRUNK

PIECES = []
for _b in range(2):
    PIECES += [(_b, DC, 384, 0, DC, 0, 256, ("tile_filled", TILE["in"] + 3 * _b + 2)),
               (_b, DC, 384, 0, DC, 256, 384, ("tile_filled", TILE["in"] + 3 * _b + 3))]
for _b in range(4):
    PIECES.append((2 + _b // 2, QC, 768, 0, QC, 384 * (_b % 2), 384 * (_b % 2) + 384,
                   ("tile_filled", TILE["qrope"] + 3 * _b + 3)))
for _b, _name in enumerate(("kup", "vup")):
    PIECES.append((4, KC, 2048, 0, KC, 1024 * _b, 1024 * _b + 1024, ("tile_filled", TILE[_name] + 8)))


def _by_columns(name, block, n):
    for b in range(n):
        for h_ in range(2):
            PIECES.append((block + b, DC, 512, 0, DC, 256 * h_, 256 * h_ + 256,
                           ("tile_filled", TILE[name] + 4 * b + 2 * h_ + 2)))


_by_columns("att_out", 5, 2)
_by_columns("ffn", 7, 11)
for _b in range(8):
    PIECES += [(18 + _b, FC, P, 0, FC // 2, 0, P, ("down_half", _b + 1)),
               (18 + _b, FC, P, FC // 2, FC, 0, P, ("tile_filled", TILE["down"] + _b + 1))]
_by_columns("gate0", 26, 2)
for _b in range(2):
    PIECES.append((28, PC, 1024, 0, PC, 512 * _b, 512 * _b + 512, ("tile_filled", TILE["proj0"] + 4 * _b + 4)))
_by_columns("gm", 29, 4)
_by_columns("gm_out", 33, 2)
NP = len(PIECES)
assert NP == 2 * N_TRUNK and (2 * EB) % HIGHS == 0
EP = 2 * EB
ORDER = [("g", 0), ("u", 0)]
for _f in range(1, FB):
    ORDER += [("g", _f), ("u", _f), ("d", _f - 1)]
ORDER += [("d", FB - 1)]
AT = {_k: [_j for _j, (_kind, _) in enumerate(ORDER) if _kind == _k] for _k in "gud"}


def constants():
    ones = np.ones((P, P), np.float32)
    ident = np.eye(P, dtype=np.float32)
    half = ROPE // 2
    rot = np.zeros((P, P), np.float32)
    for b in range(P // ROPE):
        for i in range(half):
            rot[b * ROPE + half + i, b * ROPE + i] = -1.0
            rot[b * ROPE + i, b * ROPE + half + i] = 1.0
    before = np.triu(ones, 1)
    ramp = np.broadcast_to(np.arange(P, dtype=np.float32), (P, P))
    pos = np.concatenate([np.arange(TP), PAST + np.arange(TS)]).astype(np.float32)
    inv = (np.float32(10000.0) ** (-np.arange(half, dtype=np.float32) / np.float32(half))).astype(np.float32)
    ang = (pos[None, :] * inv[:, None]).astype(np.float32)
    cos = np.tile(np.cos(ang), (P // half, 1)).astype(np.float32)
    sin = np.tile(np.sin(ang), (P // half, 1)).astype(np.float32)
    eps = np.tile(np.array([[EPS_LN, EPS_RMS]], np.float32), (P, 1))
    base = np.broadcast_to(np.arange(E, dtype=np.float32) * P, (P, E))
    ramp8 = np.tile(np.arange(E, dtype=np.float32), (P, 3))
    ramp8[TS:, 2 * E:] = -1.0
    base1 = np.tile(np.arange(E, dtype=np.float32) * P + 1.0, (P, 3))
    ramp4 = np.tile(np.repeat(np.arange(4, dtype=np.float32), E - 1), (P, 1))
    return np.ascontiguousarray(
        np.concatenate([ones, ident, rot, before, ramp, cos, sin, eps, base, ramp8, base1, ramp4], axis=1))


C_ONES, C_ID, C_ROT, C_BEF, C_RAMP, C_COS = 0, 128, 256, 384, 512, 640
C_SIN = C_COS + T
C_EPS = C_SIN + T
C_BASE = C_EPS + 2
C_RAMP8 = C_BASE + E
C_BASE1 = C_RAMP8 + 3 * E
C_RAMP4 = C_BASE1 + 3 * E
N_CONST = C_RAMP4 + 4 * (E - 1)
SEL_STEP = 13


def build(nc, a, out):
    with ExitStack() as ctx:
        names = {}

        def sem(name):
            if name not in names:
                names[name] = ctx.enter_context(nc.semaphore(name))
            return names[name]

        start = (nc.sbuf_base + 31) // 32 * 32
        place = [start]

        def sb(name, shape, dt=F32, at=None):
            if at is None:
                at = place[0]
                place[0] += (int(np.prod(shape[1:])) * 4 + 31) // 32 * 32
            return nc.alloc_sbuf_tensor_at(name, shape, dt, offset=at)

        const = sb("const", [P, N_CONST])
        vec = sb("vec", [P, N_VEC])
        w_router = sb("w_router", [P, DC, E])
        small = sb("small", [P, 400])
        table = sb("table", [P, 16], I32)
        maxidx = sb("maxidx", [P, 3, 8], U32)
        high = [sb(f"high{i}", [P, PIECE], F32R) for i in range(HIGHS)]
        ring, low = [], []
        for i in range(TRUNK_SLOTS):
            ring.append(sb(f"ring{i}", [P, BLK]))
            low.append(sb(f"low{i}", [P, BLK], F32R, at=place[0] - 4 * BLK))
        base = place[0]
        WORK = 24672
        LENT = WORK - (SLOTS - TRUNK_SLOTS) * BLK
        assert base + 4 * WORK <= nc.sbuf_usable_end
        for i in range(TRUNK_SLOTS, SLOTS):
            at = base + 4 * (LENT + BLK * (i - TRUNK_SLOTS))
            ring.append(sb(f"ring{i}", [P, BLK], at=at))
            low.append(sb(f"low{i}", [P, BLK], F32R, at=at))

        def area(name, at, chunks, width, dt=F32):
            assert at + chunks * width <= WORK
            return sb(name, [P, chunks, width], dt, at=base + 4 * at)[:, :, :]

        bank = [ctx.enter_context(nc.psum_tensor(f"bank{i}", [P, 512], F32)) for i in range(8)]

        ones, ident, rot_m = const[:, 0:128], const[:, 128:256], const[:, 256:384]
        before, ramp = const[:, C_BEF:C_BEF + P], const[:, C_RAMP:C_RAMP + P]
        cos, sin = const[:, C_COS:C_COS + T], const[:, C_SIN:C_SIN + T]
        eps_ln, eps_rms = const[:, C_EPS:C_EPS + 1], const[:, C_EPS + 1:C_EPS + 2]

        x = area("x", 0, DC, T)
        x_h = area("x_h", 2304, DC, T, F32R)
        x_l = area("x_l", 4608, DC, T, F32R)
        res = area("res", 2304, DC, T)
        sq = area("sq", 4608, DC, T)
        stat = area("stat", 6912, 4, T)
        kT = area("kT", 2304, H, KEYS)
        probsT = area("probsT", 5632, 2, 448)
        raw = area("raw", 8064, 6, T)
        cq_h = area("cq_h", 9792, QC, T, F32R)
        cq_l = area("cq_l", 10656, QC, T, F32R)
        lat_h = area("lat_h", 11520, KC, 512, F32R)
        lat_l = area("lat_l", 12544, KC, 512, F32R)
        att_h = area("att_h", 8064, DC, T, F32R)
        att_l = area("att_l", 10368, DC, T, F32R)
        qn = area("qn", 13568, DC, T)
        in_sq = area("in_sq", 13568, QC + KC, T)
        qr = area("qr", 15872, 4, T)
        qr_raw = area("qr_raw", 17024, 4, T)
        v = area("v", 18176, 4, 1024)
        kr = area("kr", 22272, 1, KEYS)[:, 0, :]
        lat = area("lat", 22688, KC, KEYS)
        probs = area("probs", 23520, 2, 544)
        rope_tmp = area("rope_tmp", 23520, 4, T)
        hid_h = area("hid_h", 8064, FC, T, F32R)
        hid_l = area("hid_l", 14400, FC, T, F32R)
        sil = area("sil", 20736, 3, T)
        hid = area("hid", 21600, 3, T)
        ple_s = area("ple_s", 8064, DC, T)
        p_raw = [area("p_raw0", 23520, PC, T), area("p_raw1", 15904, PC, T)]
        p_l = [area("p_l0", 23520, PC, T, F32R), area("p_l1", 15904, PC, T, F32R)]
        p_h = [area("p_h0", 24096, PC, T, F32R), area("p_h1", 10368, PC, T, F32R)]
        gm_res = area("gm_res", 8064, DC, T)
        gm_v = area("gm_v", 10368, DC, T)
        um_h = area("um_h", 8064, DC, T, F32R)
        um_l = area("um_l", 10368, DC, T, F32R)
        gm_u = area("gm_u", 12672, DC, T)
        gm_vtok = area("gm_vtok", 14976, 8, 3 * P)
        gm_sq = area("gm_sq", 14976, DC, T)
        gm_bias = area("gm_bias", 18048, 8, T)
        gm_w = area("gm_w", 20352, 8, P)
        gm_tmp = area("gm_tmp", 21376, 2, T)
        eq = area("eq", 0, 6, P)
        xtok = area("xtok", 4608, 3, D)
        xg_h = area("xg_h", 7680, DC, P, F32R)
        xg_l = area("xg_l", 8704, DC, P, F32R)
        hT_h = area("hT_h", 9728, 8, P, F32R)
        hT_l = area("hT_l", 10752, 8, P, F32R)
        hbuf = area("hbuf", 11776, 2, 512)
        sbuf = area("sbuf", 12800, 2, 512)
        y_sl = area("y_sl", 13824, 1, D)[:, 0, :]
        onehot = area("onehot", 14848, 3, P)
        onehot_c = area("onehot_c", 15232, 3, P)
        ct = area("ct", 15616, 1, T)[:, 0, :]
        sm = small
        mx = sm[:, 0:6].rearrange("p (b c) -> p b c", b=2)
        nmx = sm[:, 6:12].rearrange("p (b c) -> p b c", b=2)
        psum_r = sm[:, 12:18].rearrange("p (b c) -> p b c", b=2)
        prec = sm[:, 18:24].rearrange("p (b c) -> p b c", b=2)
        lg = sm[:, 24:48].rearrange("p (b c) -> p b c", b=3)
        mx8 = sm[:, 48:72].rearrange("p (b c) -> p b c", b=3)
        idx = sm[:, 72:96].rearrange("p (b c) -> p b c", b=3)
        oneA = sm[:, 96:120].rearrange("p (b c) -> p b c", b=3)
        oneB = sm[:, 120:144].rearrange("p (b c) -> p b c", b=3)
        sel = sm[:, 144:168].rearrange("p (b c) -> p b c", b=3)
        rank = sm[:, 168:200].rearrange("p (b c) -> p b c", b=4)
        big = sm[:, 200:224].rearrange("p (b c) -> p b c", b=3)
        slot_of = sm[:, 224:248].rearrange("p (b c) -> p b c", b=3)
        picked = sm[:, 248:296].rearrange("p (k b c) -> p k b c", k=2, b=3)
        where = sm[:, 296:302].rearrange("p (k b) -> p k b", k=2)
        share = sm[:, 302:308].rearrange("p (k b) -> p k b", k=2)
        over1, over, shift = sm[:, 308:316], sm[:, 316:324], sm[:, 333:341]
        sums_a, sums_b = sm[:, 367:383], sm[:, 383:399]
        diff, e2, den, rden = sm[:, 341:344], sm[:, 344:347], sm[:, 347:350], sm[:, 350:353]
        ids = sm[:, 353:367]
        cmp = sm[:, 248:276].rearrange("p (b c) -> p b c", b=4)

        free_by = {}

        def filled(eng, name, i=0):
            n = TILE[name] + i
            eng.wait_ge(sem("tile_filled"), n + 1)
            return bank[n % 8]

        def filled_at(eng, n):
            eng.wait_ge(sem("tile_filled"), n + 1)
            return bank[n % 8]

        def frees(name, i, signal, value):
            free_by[TILE[name] + i] = (signal, value)

        block = ctx.enter_context(nc.Block())
        LN_OF = {0: "att_out", 1: "down", 3: "gm_out"}

        def piece(q, tensors):
            n, kc, width, k0, k1, c0, c1, _ = PIECES[q]
            m = tensors[n % TRUNK_SLOTS][:, 0:kc * width].rearrange("p (k m) -> p k m", k=kc)
            return m[:, k0:k1, c0:c1]

        def piece_high(q):
            _, _, _, k0, k1, c0, c1, _ = PIECES[q]
            m = high[q % HIGHS][:, 0:(k1 - k0) * (c1 - c0)]
            return m.rearrange("p (k m) -> p k m", k=k1 - k0)

        def expert_piece(p, tensors):
            return tensors[p // 2 % SLOTS][:, PIECE * (p % 2):PIECE * (p % 2) + PIECE]

        def expert_high(p):
            return high[(NP + p) % HIGHS][:, :]

        SCATTER = (4, 5, 0, 1, 6, 7, 4, 5)

        def tail_piece(p, tensors):
            n = PIECE if p < 4 else PC * 512
            return tensors[p // 2][:, n * (p % 2):n * (p % 2) + n]

        def tail_high(p):
            return high[(NP + p) % HIGHS][:, 0:PIECE if p < 4 else PC * 512]

        def landed_before(s):
            return N_TRUNK // TRUNK_SLOTS if s < TRUNK_SLOTS else 0

        @block.vector
        def _(dve):
            def residual(n, q, per):
                for c in range(DC):
                    ps = filled(dve, LN_OF[n], c)
                    dve.scalar_tensor_tensor(res[:, c, :], x[:, c, :], ALPHA, ps[:, 0:T], ALU.mult,
                                             ALU.add).then_inc(sem("residual"), 1)
                    frees(LN_OF[n], c, "residual", 8 * len(done) + c + 1)
                    add_up(c, "residual", 8 * len(done) + c + 1)
                    if per == 2 and c % 2:
                        after(q + c // 2)
                    elif per == 0:
                        after(q + 2 * c)
                        after(q + 2 * c + 1)
                done.append(n)

            def split_low(q):
                dve.wait_ge(sem("high_ready"), q + 1)
                dve.tensor_tensor(piece(q, low), piece(q, ring), piece_high(q).bitcast(F32), ALU.subtract)\
                   .then_inc(sem("low_ready"), 1)

            def first_lows():
                for p in range(HIGHS):
                    dve.wait_ge(sem("high_ready"), NP + p + 1)
                    dve.tensor_tensor(expert_piece(p, low), expert_piece(p, ring), expert_high(p).bitcast(F32),
                                      ALU.subtract).then_inc(sem("low_ready"), 1)

            def after(q):
                if q + HIGHS < NP:
                    split_low(q + HIGHS)

            def add_up(c, signal, value, of=res):
                if c == 0:
                    return
                dve.wait_ge(sem(signal), value)
                first = of[:, 0, :] if c == 1 else stat[:, 0, :]
                if c > 1:
                    dve.wait_ge(sem("summed"), sums[0])
                dve.tensor_tensor(stat[:, 0, :], first, of[:, c, :], ALU.add).then_inc(sem("summed"), 1)
                sums[0] += 1

            def split_x(signal, value):
                for c in range(DC):
                    dve.wait_ge(sem(signal), value + c + 1)
                    dve.tensor_tensor(x_l[:, c, :], x[:, c, :], x_h[:, c, :].bitcast(F32), ALU.subtract)\
                       .then_inc(sem("x_split"), 1)

            def normalise(n):
                mean = filled(dve, f"ln{n}", 0)
                to, s2 = (gm_res, gm_sq) if n == 2 else (res, sq)
                for c in range(DC):
                    dve.scalar_tensor_tensor(to[:, c, :], mean[:, 0:T], -1.0 / D, to[:, c, :], ALU.mult,
                                             ALU.add).then_inc(sem("centred"), 1)
                frees(f"ln{n}", 0, "centred", 8 * n + 8)
                for c in range(1, DC):
                    dve.wait_ge(sem("squared"), 8 * n + c + 1)
                    first = s2[:, 0, :] if c == 1 else stat[:, 1, :]
                    if c > 1:
                        dve.wait_ge(sem("sq_summed"), 7 * n + c - 1)
                    dve.tensor_tensor(stat[:, 1, :], first, s2[:, c, :], ALU.add).then_inc(sem("sq_summed"), 1)
                dve.wait_ge(sem("deviation"), n + 1)
                dve.reciprocal(stat[:, 3, :], stat[:, 2, :]).then_inc(sem("rstd"), 1)
                dve.wait_ge(sem("rstd"), n + 1)
                for c in range(DC):
                    dve.tensor_tensor(to[:, c, :], to[:, c, :], stat[:, 3, :], ALU.mult)\
                       .then_inc(sem("scaled"), 1)

            def ple(n):
                for q in range(4):
                    if n == 0:
                        filled(dve, "gate0", 2 * q + 1)
                        after(52 + q)
                    elif q == 3:
                        for p in range(HIGHS, 6):
                            dve.wait_ge(sem("high_tail"), p - HIGHS + 1)
                            dve.tensor_tensor(tail_piece(p, low), tail_piece(p, ring), tail_high(p).bitcast(F32),
                                              ALU.subtract).then_inc(sem("low_tail"), 1)
                for c in range(DC):
                    ps = filled(dve, f"proj{n}", c)
                    dve.wait_ge(sem("ple_sigmoid"), 8 * n + c + 1)
                    dve.tensor_tensor(ple_s[:, c, :], ple_s[:, c, :], ps[:, 0:T], ALU.mult)\
                       .then_inc(sem("ple_gated"), 1)
                    frees(f"proj{n}", c, "ple_gated", 8 * n + c + 1)
                    dve.wait_ge(sem("ple_gated"), 8 * n + c + 1)
                    dve.tensor_tensor(x[:, c, :], x[:, c, :], ple_s[:, c, :], ALU.add)\
                       .then_inc(sem("ple_added"), 1)
                    if n == 0 and c % 4 == 3:
                        after(56 + c // 4)

            done, sums = [], [0]
            dve.memset(lat_h.bitcast(F32), 0.0).then_inc(sem("lat_zero"), 1)
            dve.memset(lat_l.bitcast(F32), 0.0).then_inc(sem("lat_zero"), 1)
            split_x("x_high", 0)
            for q in range(HIGHS):
                split_low(q)
            for q in range(4):
                after(q)
            dve.memset(small[:, :], 0.0).then_inc(sem("small_zero"), 1)
            for i in range(2):
                dve.wait_ge(sem("rms_dev"), i + 1)
                dve.reciprocal(stat[:, 2 + i, :], stat[:, i, :]).then_inc(sem("rms_rstd"), 1)
                dve.wait_ge(sem("rms_rstd"), i + 1)
                for c in (range(QC) if i == 0 else range(QC, QC + KC)):
                    to = raw[:, c, :] if c < QC else lat[:, c - QC, 0:T]
                    dve.scalar_tensor_tensor(to, raw[:, c, :], vec[:, G_Q + c:G_Q + c + 1], stat[:, 2 + i, :],
                                             ALU.mult, ALU.mult).then_inc(sem("latent"), 1)
                dve.wait_ge(sem("latent"), QC + KC * i)
                if i == 0:
                    full, to_h, to_l = raw[:, 0:QC, :], cq_h, cq_l
                else:
                    full, to_h, to_l = lat, lat_h[:, :, 0:KEYS], lat_l[:, :, 0:KEYS]
                    dve.wait_ge(sem("cache_loaded"), 16)
                    dve.wait_ge(sem("lat_zero"), 2)
                dve.tensor_copy(to_h, full).then_inc(sem("latent_high"), 1)
                dve.wait_ge(sem("latent_high"), i + 1)
                dve.tensor_tensor(to_l, full, to_h.bitcast(F32), ALU.subtract).then_inc(sem("latent_low"), 1)
            dve.wait_ge(sem("in_copied"), 6)
            dve.tensor_tensor(kr[:, 0:T], raw[:, 5, :], cos, ALU.mult).then_inc(sem("kr_part"), 1)
            ps = filled(dve, "krot")
            dve.tensor_tensor(rope_tmp[:, 0, :], ps[:, 0:T], sin, ALU.mult).then_inc(sem("kr_part"), 1)
            frees("krot", 0, "kr_part", 2)
            dve.wait_ge(sem("kr_part"), 2)
            dve.tensor_tensor(kr[:, 0:T], kr[:, 0:T], rope_tmp[:, 0, :], ALU.add).then_inc(sem("kr_ready"), 1)
            for q in range(4, 8):
                after(q)
            for c in range(4):
                dve.wait_ge(sem("qr_copied"), c + 1)
                dve.tensor_tensor(qr[:, c, :], qr_raw[:, c, :], cos, ALU.mult).then_inc(sem("qr_part"), 1)
                ps = filled(dve, "qrot", c)
                if c == 0:
                    dve.wait_ge(sem("kr_ready"), 1)
                dve.tensor_tensor(rope_tmp[:, c, :], ps[:, 0:T], sin, ALU.mult).then_inc(sem("qr_part"), 1)
                frees("qrot", c, "qr_part", 2 * c + 2)
                dve.wait_ge(sem("qr_part"), 2 * c + 2)
                dve.tensor_tensor(qr[:, c, :], qr[:, c, :], rope_tmp[:, c, :], ALU.add)\
                   .then_inc(sem("qr_ready"), 1)
            dve.wait_ge(sem("qr_ready"), 4)
            dve.memset(probs[:, :, :], 0.0).then_inc(sem("probs_zero"), 1)
            after(8)
            for i in range(8):
                ps = filled(dve, "vup", i)
                rows = P if i < 6 else TS
                dve.tensor_copy(v[0:rows, i // 2, 512 * (i % 2):512 * (i % 2) + 512], ps[0:rows, :])\
                   .then_inc(sem("v_ready"), 1)
                frees("vup", i, "v_ready", i + 1)
            after(9)

            def regions(h, ps_p, ps_s):
                b = probs[:, h % 2, :]
                out_ = []
                for blk, at in ((0, 0), (1, P)):
                    for half in range(2):
                        rows = slice(CHUNK * half, CHUNK * half + CHUNK)
                        n = P * blk + CHUNK * (half + 1)
                        out_.append((ps_p[rows, at:at + n], b[rows, at:at + n], rows, blk))
                out_.append((ps_s[0:TS, 0:TS + PAST], b[0:TS, 384:384 + TS + PAST], slice(0, TS), 2))
                return out_

            def row_max(h):
                n = ATT["S", h]
                ps_p, ps_s = filled_at(dve, n), filled_at(dve, n + 1)
                if h == 0:
                    dve.wait_ge(sem("small_zero"), 1)
                for s, _, rows, col in regions(h, ps_p, ps_s):
                    dve.tensor_reduce(mx[rows, h % 2, col:col + 1], s, AX_X, ALU.max).then_inc(sem("row_max"), 1)
                dve.wait_ge(sem("row_max"), 5 * h + 5)
                if h >= 2:
                    dve.wait_ge(sem("exp_done"), 5 * (h - 1))
                dve.tensor_scalar(nmx[:, h % 2, :], mx[:, h % 2, :], -SCALE, None, ALU.mult)\
                   .then_inc(sem("neg_max"), 1)

            def row_scale(h):
                dve.wait_ge(sem("exp_done"), 5 * h + 5)
                if h == 0:
                    dve.wait_ge(sem("probs_zero"), 1)
                for i, rows in enumerate((P, P, TS)):
                    dve.reciprocal(prec[0:rows, h % 2, i:i + 1], psum_r[0:rows, h % 2, i:i + 1])\
                       .then_inc(sem("row_recip"), 1)
                dve.wait_ge(sem("row_recip"), 3 * h + 3)
                for i, (rows, lo, hi) in enumerate(((P, 0, P), (P, P, 3 * P), (TS, 384, 384 + TS + PAST))):
                    t = probs[0:rows, h % 2, lo:hi]
                    dve.tensor_scalar(t, t, prec[0:rows, h % 2, i:i + 1], None, ALU.mult)\
                       .then_inc(sem("probs_ready"), 1)

            def head_out(h):
                ps = filled_at(dve, ATT["O", h])
                dve.wait_ge(sem("head_high"), h + 1)
                dve.tensor_tensor(att_l[:, h, :], ps[:, 0:T], att_h[:, h, :].bitcast(F32), ALU.subtract)\
                   .then_inc(sem("head_low"), 1)
                free_by[ATT["O", h]] = ("head_low", h + 1)

            row_max(0)
            for h in range(H):
                if h + 1 < H:
                    row_max(h + 1)
                row_scale(h)
                if h:
                    head_out(h - 1)
            head_out(H - 1)
            residual(0, 10, 2)
            normalise(0)
            split_x("x_high", 8)
            for i in range(FC):
                ps = filled(dve, "ffn", 2 * i + 1)
                dve.wait_ge(sem("ffn_silu"), i + 1)
                if i >= 3:
                    dve.wait_ge(sem("hid_high"), i - 2)
                if i == 0:
                    dve.wait_ge(sem("kr_out"), 16)
                dve.tensor_tensor(hid[:, i % 3, :], sil[:, i % 3, :], ps[:, 0:T], ALU.mult)\
                   .then_inc(sem("ffn_hidden"), 1)
                frees("ffn", 2 * i + 1, "ffn_hidden", i + 1)
                after(14 + i)
                dve.wait_ge(sem("hid_high"), i + 1)
                dve.tensor_tensor(hid_l[:, i, :], hid[:, i % 3, :], hid_h[:, i, :].bitcast(F32), ALU.subtract)\
                   .then_inc(sem("hid_low"), 1)
            residual(1, 36, 0)
            normalise(1)
            split_x("x_high", 16)
            dve.wait_ge(sem("p_loaded0"), 16)
            dve.tensor_copy(p_h[0], p_raw[0]).then_inc(sem("p_high"), 1)
            dve.wait_ge(sem("p_high"), 1)
            dve.tensor_tensor(p_l[0], p_raw[0], p_h[0].bitcast(F32), ALU.subtract).then_inc(sem("p_low"), 1)
            ple(0)
            split_x("x_high", 24)
            for j in range(8):
                after(58 + j)
                if j < 4:
                    for c in (2 * j, 2 * j + 1):
                        add_up(c, "gelu", c + 1, gm_res)
            normalise(2)
            dve.wait_ge(sem("gm_loaded"), 32)
            for g in range(8):
                ps = filled(dve, "mix", g)
                dve.tensor_tensor(gm_tmp[:, g % 2, :], ps[:, 0:T], gm_bias[:, g, :], ALU.add)\
                   .then_inc(sem("mix_biased"), 1)
                frees("mix", g, "mix_biased", g + 1)
                dve.wait_ge(sem("mix_biased"), g + 1)
                dve.tensor_tensor(gm_u[:, g, :], gm_u[:, g, :], gm_tmp[:, g % 2, :], ALU.mult)\
                   .then_inc(sem("mixed"), 1)
                dve.wait_ge(sem("um_high"), g + 1)
                dve.tensor_tensor(um_l[:, g, :], gm_u[:, g, :], um_h[:, g, :].bitcast(F32), ALU.subtract)\
                   .then_inc(sem("um_low"), 1)
            residual(3, 66, 2)
            first_lows()
            normalise(3)

            route = [0]

            def r_(ins, wait=True):
                ins.then_inc(sem("route_step"), 1)
                route[0] += 1
                if wait:
                    dve.wait_ge(sem("route_step"), route[0])

            ps = filled(dve, "logits")
            one, two = slice(0, 1), slice(1, 2)
            r_(dve.tensor_copy(lg[:, 0:2, :], ps[:, 0:16].rearrange("p (b c) -> p b c", b=2)), False)
            r_(dve.tensor_copy(lg[0:TS, 2, :], ps[0:TS, 16:24]))
            frees("logits", 0, "route_step", route[0])
            for i in range(3):
                r_(dve.max(mx8[:, i, :], lg[:, i, :]), i == 2)
            for i in range(3):
                r_(dve.max_index(maxidx[:, i, :], mx8[:, i, :], lg[:, i, :]), i == 2)
            r_(dve.tensor_tensor(diff.rearrange("p (b c) -> p b c", c=1), mx8[:, :, two], mx8[:, :, one],
                                 ALU.subtract), False)
            r_(dve.tensor_copy(idx[:, :, :], maxidx[:, :, :]))
            ramp8 = const[:, C_RAMP8:C_RAMP8 + 24].rearrange("p (b c) -> p b c", b=3)
            for k, hot in enumerate((oneA, oneB)):
                r_(dve.tensor_tensor(hot, ramp8, idx[:, :, k:k + 1].broadcast_to([P, 3, E]), ALU.is_equal), k == 1)
            r_(dve.tensor_tensor(sel, oneA, oneB, ALU.add))
            sel_step = route[0]
            assert sel_step == SEL_STEP
            dve.wait_ge(sem("share_exp"), 1)
            r_(dve.tensor_scalar(den[:, :], e2[:, :], 1.0, None, ALU.add))
            r_(dve.reciprocal(share[:, 0, :], den[:, :]))
            r_(dve.tensor_tensor(share[:, 1, :], share[:, 0, :], e2[:, :], ALU.mult), False)
            ps = filled(dve, "rank")
            r_(dve.tensor_copy(rank[:, :, :], ps[:, 0:32].rearrange("p (b c) -> p b c", b=4)))
            frees("rank", 0, "route_step", route[0])
            r_(dve.tensor_scalar(over1[:, :], rank[:, 3, :], float(P), None, ALU.is_gt), False)
            r_(dve.tensor_scalar(over[:, :], rank[:, 3, :], float(2 * P), None, ALU.is_gt))
            r_(dve.tensor_tensor(over[:, :], over[:, :], over1[:, :], ALU.add))
            r_(dve.tensor_copy(sums_a[:, 8:16], over[:, :]))
            r_(dve.tensor_tensor(sums_b[:, 8:16], sums_a[:, 8:16], sums_a[:, 7:15], ALU.add))
            r_(dve.tensor_tensor(sums_a[:, 8:16], sums_b[:, 8:16], sums_b[:, 6:14], ALU.add))
            r_(dve.tensor_tensor(sums_b[:, 8:16], sums_a[:, 8:16], sums_a[:, 4:12], ALU.add))
            r_(dve.tensor_scalar(shift[:, :], sums_b[:, 7:15], float(P), float(P * (E - 1)), ALU.mult, ALU.add))
            r_(dve.tensor_tensor(shift[:, :], shift[:, :], const[:, C_BASE:C_BASE + E], ALU.subtract))
            base3 = const[:, C_BASE1:C_BASE1 + 24].rearrange("p (b c) -> p b c", b=3)
            shift3 = shift.rearrange("p (b c) -> p b c", b=1).broadcast_to([P, 3, E])
            r_(dve.tensor_scalar(big, rank[:, 0:3, :], float(P), None, ALU.is_ge))
            r_(dve.tensor_tensor(big, big, shift3, ALU.mult))
            r_(dve.tensor_tensor(big, big, rank[:, 0:3, :], ALU.add))
            r_(dve.tensor_tensor(slot_of, big, base3, ALU.add))
            for k, hot in enumerate((oneA, oneB)):
                r_(dve.tensor_tensor(picked[:, k, :, :], slot_of, hot, ALU.mult), k == 1)
            for k in range(2):
                r_(dve.tensor_reduce(where[:, k, :], picked[:, k, :, :], AX_X, ALU.add), k == 1)
            r_(dve.tensor_scalar(where[:, :, :], where[:, :, :], -1.0, None, ALU.add), False)
            r_(dve.tensor_copy(ids[:, 0:8], ramp[:, 0:8]), False)
            ramp4 = const[:, C_RAMP4:C_RAMP4 + 28].rearrange("p (b c) -> p b c", b=4)
            cum7 = sums_b[:, 8:15].rearrange("p (b c) -> p b c", b=1).broadcast_to([P, 4, E - 1])
            r_(dve.tensor_tensor(cmp, ramp4, cum7, ALU.is_ge))
            r_(dve.tensor_reduce(ids[:, 8:12], cmp, AX_X, ALU.add), False)
            r_(dve.tensor_scalar(ids[:, 12:13], sums_b[:, 15:16], float(E), None, ALU.add), False)
            r_(dve.tensor_scalar(ids[:, 13:14], sums_b[:, 15:16], float(E - 1), None, ALU.add))
            dve.tensor_copy(table[:, 0:14], ids[:, 0:14]).then_inc(sem("table_ready"), 1)
            dve.wait_ge(sem("normed"), 8 * 4)
            for c in range(DC):
                dve.tensor_scalar(res[:, c, :], x[:, c, :], ALPHA, None, ALU.mult).then_inc(sem("added"), 1)
            filled(dve, "xtr", 7)
            dve.wait_ge(sem("added"), DC)

            def one_hots(n, i):
                g0, g1 = where[:, 0, i:i + 1], where[:, 1, i:i + 1]
                dve.tensor_scalar(eq[:, i, :], ramp, g0, None, ALU.is_equal).then_inc(sem("eq_a"), 1)
                dve.tensor_scalar(eq[:, 3 + i, :], ramp, g1, share[:, 1, i:i + 1], ALU.is_equal, ALU.mult)\
                   .then_inc(sem("eq_a"), 1)
                dve.wait_ge(sem("eq_a"), n * 6 + (2 * i + 2))
                dve.scalar_tensor_tensor(onehot[:, i, :], ramp, g1, eq[:, i, :], ALU.is_equal, ALU.add)\
                   .then_inc(sem("onehot_ready"), 1)
                dve.scalar_tensor_tensor(onehot_c[:, i, :], eq[:, i, :], share[:, 0, i:i + 1],
                                         eq[:, 3 + i, :], ALU.mult, ALU.add).then_inc(sem("onehot_c_ready"), 1)

            def move_slots(n):
                dve.wait_ge(sem("onehot_ready"), n * 3 + 3)
                dve.wait_ge(sem("onehot_c_ready"), n * 3 + 3)
                dve.tensor_scalar(where[:, :, :], where[:, :, :], -float(P), None, ALU.add)\
                   .then_inc(sem("where_moved"), 1)
                dve.wait_ge(sem("where_moved"), n + 1)

            def gathered_low(n, half):
                dve.wait_ge(sem("xg_high"), n * 2 + (half + 1))
                dve.tensor_tensor(xg_l[:, 4 * half:4 * half + 4, :],
                                  bank[2 + half][:, :].rearrange("p (c s) -> p c s", c=4),
                                  xg_h[:, 4 * half:4 * half + 4, :].bitcast(F32), ALU.subtract)\
                   .then_inc(sem("xg_low"), 1)

            for i in range(3):
                one_hots(0, i)
            move_slots(0)
            for half in range(2):
                gathered_low(0, half)
            dve.wait_ge(sem("table_ready"), 1)
            tiles = dve.value_load(table[0:1, 12:13], min_val=E, max_val=MAX_TILES)
            with dve.Fori(0, tiles) as t:
                def turned_low(f):
                    dve.wait_ge(sem("hT_high"), t * FB + (f + 1))
                    at = 4 * (f % 2)
                    dve.tensor_tensor(hT_l[:, at:at + 4, :], bank[4 + f % 2][:, :].rearrange("p (c s) -> p c s", c=4),
                                      hT_h[:, at:at + 4, :].bitcast(F32), ALU.subtract)\
                       .then_inc(sem("hT_low"), 1)

                for p in range(EP):
                    kind, f = ORDER[p // 2]
                    if p % 2 and kind == "u":
                        dve.wait_ge(sem("piece_used"), t * EP + (p + 1))
                        dve.wait_ge(sem("silu_done"), t * FB + (f + 1))
                        dve.tensor_tensor(hbuf[:, f % 2, :], sbuf[:, f % 2, :], bank[1 + 2 * (f % 2)][:, :],
                                          ALU.mult).then_inc(sem("hidden_ready"), 1)
                    if p % 2 and kind == "g" and f:
                        turned_low(f - 1)
                    if p % 2 and kind == "d" and f == FB - 2:
                        turned_low(FB - 1)
                        gathered_low(t + 1, 0)
                    if p % 2 and kind == "d" and 1 <= f <= 3:
                        if f == 1:
                            dve.wait_ge(sem("ct_turned"), t + 1)
                        one_hots(t + 1, f - 1)
                        if f == 3:
                            move_slots(t + 1)
                    if p == EP - 1:
                        dve.wait_ge(sem("piece_used"), t * EP + EP)
                        dve.tensor_copy(y_sl[:, 0:512], bank[6][:, :]).then_inc(sem("y_low"), 1)
                    dve.wait_ge(sem("high_ready"), t * EP + (NP + p + HIGHS + 1))
                    dve.tensor_tensor(expert_piece((p + HIGHS) % EP, low), expert_piece((p + HIGHS) % EP, ring),
                                      expert_high(p + HIGHS).bitcast(F32), ALU.subtract)\
                       .then_inc(sem("low_ready"), 1)
                gathered_low(t + 1, 1)
                for c in range(DC):
                    dve.wait_ge(sem("scattered"), t * DC + (c + 1))
                    dve.tensor_tensor(res[:, c, :], res[:, c, :], bank[SCATTER[c]][:, 0:T], ALU.add)\
                       .then_inc(sem("added"), 1)
            dve.wait_ge(sem("added"), tiles * DC + DC)
            for c in range(1, DC):
                add_up(c, "table_ready", 1)
            normalise(4)
            split_x("x_high", 32)
            dve.wait_ge(sem("p_loaded1"), 16)
            dve.tensor_copy(p_h[1], p_raw[1]).then_inc(sem("p_high"), 1)
            dve.wait_ge(sem("p_high"), 2)
            dve.tensor_tensor(p_l[1], p_raw[1], p_h[1].bitcast(F32), ALU.subtract).then_inc(sem("p_low"), 1)
            ple(1)

        @block.scalar
        def _(act):
            def split_high(q):
                n = PIECES[q][0]
                act.wait_ge(sem(f"landed{n % TRUNK_SLOTS}"), 16 * (n // TRUNK_SLOTS + 1))
                if q >= HIGHS:
                    signal, value = PIECES[q - HIGHS][7]
                    act.wait_ge(sem(signal), value)
                act.activation(piece_high(q), piece(q, ring), ACT.Copy).then_inc(sem("high_ready"), 1)

            def after(q):
                if q + HIGHS < NP:
                    split_high(q + HIGHS)

            def first_highs():
                for p in range(HIGHS):
                    s = p // 2
                    act.wait_ge(sem(f"landed{s}"), 16 * (landed_before(s) + 1))
                    signal, value = PIECES[NP + p - HIGHS][7]
                    act.wait_ge(sem(signal), value)
                    act.activation(expert_high(p), expert_piece(p, ring), ACT.Copy)\
                       .then_inc(sem("high_ready"), 1)

            act.dma_start(const[:, :], a["const"]).then_inc(sem("const_loaded"), 16)
            act.dma_start(vec[:, :], a["vec"]).then_inc(sem("vec_loaded"), 16)
            act.dma_start(w_router[:, :, :], a["w_router"]).then_inc(sem("router_loaded"), 16)
            act.dma_start(lat[:, :, T:KEYS], a["cache_lat"]).then_inc(sem("cache_loaded"), 16)
            act.dma_start(kr[:, T:KEYS], a["cache_kr"]).then_inc(sem("cache_kr_loaded"), 16)

            def norm_tail(n):
                of, s2 = (gm_res, gm_sq) if n == 2 else (res, sq)
                for c in range(DC):
                    act.wait_ge(sem("centred"), 8 * n + c + 1)
                    act.activation(s2[:, c, :], of[:, c, :], ACT.Square).then_inc(sem("squared"), 1)
                var = filled(act, f"ln{n}", 1)
                act.activation(stat[:, 2, :], var[:, 0:T], ACT.Sqrt, bias=eps_ln, scale=1.0 / D)\
                   .then_inc(sem("deviation"), 1)
                frees(f"ln{n}", 1, "deviation", n + 1)
                to = gm_v if n == 2 else x
                g = G_GM if n == 2 else LN_G[n]
                b = B_GM if n == 2 else LN_B[n]
                for c in range(DC):
                    act.wait_ge(sem("scaled"), 8 * n + c + 1)
                    act.activation(to[:, c, :], of[:, c, :], ACT.Identity, bias=vec[:, b + c:b + c + 1],
                                   scale=vec[:, g + c:g + c + 1]).then_inc(sem("normed"), 1)
                    if n not in (2, 3):
                        act.activation(x_h[:, c, :], of[:, c, :], ACT.Identity, bias=vec[:, b + c:b + c + 1],
                                       scale=vec[:, g + c:g + c + 1]).then_inc(sem("x_high"), 1)

            def ple_gate(n):
                for c in range(DC):
                    ps = filled(act, f"gate{n}", c)
                    act.activation(ple_s[:, c, :], ps[:, 0:T], ACT.Sigmoid).then_inc(sem("ple_sigmoid"), 1)
                    frees(f"gate{n}", c, "ple_sigmoid", 8 * n + c + 1)
                    if n == 0 and c % 2:
                        after(52 + c // 2)

            act.wait_ge(sem("x_loaded"), 16)
            for c in range(DC):
                act.activation(x_h[:, c, :], x[:, c, :], ACT.Copy).then_inc(sem("x_high"), 1)
            for q in range(HIGHS):
                split_high(q)
            act.wait_ge(sem("const_loaded"), 16)
            act.wait_ge(sem("vec_loaded"), 16)
            for c in range(6):
                ps = filled(act, "in", c)
                act.activation(raw[:, c, :], ps[:, 0:T], ACT.Copy).then_inc(sem("in_copied"), 1)
                if c < 5:
                    act.activation(in_sq[:, c, :], ps[:, 0:T], ACT.Square).then_inc(sem("in_squared"), 1)
                    frees("in", c, "in_squared", c + 1)
                if c in (1, 2, 4, 5):
                    after((1, 2, 4, 5).index(c))
            frees("in", 5, "in_copied", 6)
            for i, width in enumerate((QL, KVL)):
                ps = filled(act, "rms", i)
                act.activation(stat[:, i, :], ps[:, 0:T], ACT.Sqrt, bias=eps_rms, scale=1.0 / width)\
                   .then_inc(sem("rms_dev"), 1)
                frees("rms", i, "rms_dev", i + 1)
            for c in range(4):
                ps = filled(act, "qrope", c)
                act.activation(qr_raw[:, c, :], ps[:, 0:T], ACT.Copy).then_inc(sem("qr_copied"), 1)
                frees("qrope", c, "qr_copied", c + 1)
                if c == 2:
                    after(4)
            for c in range(DC):
                ps = filled(act, "qnope", c)
                act.activation(qn[:, c, :], ps[:, 0:T], ACT.Copy).then_inc(sem("qn_ready"), 1)
                frees("qnope", c, "qn_ready", c + 1)
                if c % 3 == 1:
                    after(5 + c // 3)
            for c in range(H):
                ps = filled(act, "kup", c)
                act.activation(kT[:, c, :], ps[:, 0:KEYS], ACT.Copy).then_inc(sem("k_ready"), 1)
                frees("kup", c, "k_ready", c + 1)
            after(8)
            after(9)

            def exps(h):
                n = ATT["S", h]
                ps_p, ps_s = bank[n % 8], bank[(n + 1) % 8]
                act.wait_ge(sem("neg_max"), h + 1)
                if h == 0:
                    act.wait_ge(sem("probs_zero"), 1)
                if h >= 2:
                    filled_at(act, ATT["T", h - 2])
                b = probs[:, h % 2, :]
                for blk, at in ((0, 0), (1, P)):
                    for half in range(2):
                        rows = slice(CHUNK * half, CHUNK * half + CHUNK)
                        m = P * blk + CHUNK * (half + 1)
                        act.activation(b[rows, at:at + m], ps_p[rows, at:at + m], ACT.Exp,
                                       bias=nmx[rows, h % 2, blk:blk + 1], scale=SCALE,
                                       accum_out=psum_r[rows, h % 2, blk:blk + 1]).then_inc(sem("exp_done"), 1)
                act.activation(b[0:TS, 384:384 + TS + PAST], ps_s[0:TS, 0:TS + PAST], ACT.Exp,
                               bias=nmx[0:TS, h % 2, 2:3], scale=SCALE,
                               accum_out=psum_r[0:TS, h % 2, 2:3]).then_inc(sem("exp_done"), 1)
                free_by[n] = ("exp_done", 5 * h + 4)
                free_by[n + 1] = ("exp_done", 5 * h + 5)

            def turned_probs(h):
                ps = filled_at(act, ATT["T", h])
                if h >= 2:
                    filled_at(act, ATT["O", h - 2])
                act.activation(probsT[:, h % 2, 0:416], ps[:, 0:416], ACT.Copy).then_inc(sem("probsT_ready"), 1)
                act.activation(probsT[0:TS, h % 2, 416:448], ps[0:TS, 416:448], ACT.Copy)\
                   .then_inc(sem("probsT_ready"), 1)
                free_by[ATT["T", h]] = ("probsT_ready", 2 * h + 2)

            def head_high(h):
                ps = filled_at(act, ATT["O", h])
                act.activation(att_h[:, h, :], ps[:, 0:T], ACT.Copy).then_inc(sem("head_high"), 1)

            for h in range(H):
                exps(h)
                if h:
                    turned_probs(h - 1)
                if h > 1:
                    head_high(h - 2)
            turned_probs(H - 1)
            head_high(H - 2)
            head_high(H - 1)
            for q in range(10, 14):
                after(q)
            norm_tail(0)
            for i in range(FC):
                ps = filled(act, "ffn", 2 * i)
                if i >= 3:
                    act.wait_ge(sem("ffn_hidden"), i - 2)
                act.activation(sil[:, i % 3, :], ps[:, 0:T], ACT.Silu).then_inc(sem("ffn_silu"), 1)
                frees("ffn", 2 * i, "ffn_silu", i + 1)
                act.wait_ge(sem("ffn_hidden"), i + 1)
                act.activation(hid_h[:, i, :], hid[:, i % 3, :], ACT.Copy).then_inc(sem("hid_high"), 1)
                after(14 + i)
            for q in range(36, 52):
                after(q)
            norm_tail(1)
            ple_gate(0)
            for c in range(DC):
                if c % 4 == 0:
                    after(56 + c // 4)
                act.wait_ge(sem("ple_added"), c + 1)
                act.activation(x_h[:, c, :], x[:, c, :], ACT.Copy).then_inc(sem("x_high"), 1)
            for c in range(2 * DC):
                ps = filled(act, "gm", c)
                to = gm_res[:, c, :] if c < DC else gm_u[:, c - DC, :]
                act.activation(to, ps[:, 0:T], ACT.Gelu_apprx_tanh).then_inc(sem("gelu"), 1)
                frees("gm", c, "gelu", c + 1)
                if c % 2:
                    after(58 + c // 2)
            norm_tail(2)
            act.wait_ge(sem("normed"), 24)
            act.dma_start(out["gm_v"], gm_v[:, :, P:T]).then_inc(sem("gm_v_out"), 16)
            for g in range(8):
                ps = filled(act, "vtr", g)
                act.activation(gm_vtok[:, g, 0:256], ps[:, 0:256], ACT.Copy).then_inc(sem("vtok"), 1)
                act.activation(gm_vtok[0:TS, g, 256:384], ps[0:TS, 256:384], ACT.Copy).then_inc(sem("vtok"), 1)
                frees("vtr", g, "vtok", 2 * g + 2)
            act.wait_ge(sem("gm_v_out"), 16)
            filled(act, "vtr", 7)
            for g in range(8):
                act.wait_ge(sem("mixed"), g + 1)
                act.activation(um_h[:, g, :], gm_u[:, g, :], ACT.Copy).then_inc(sem("um_high"), 1)
            for q in range(66, NP):
                after(q)
            first_highs()
            norm_tail(3)
            for c in range(DC):
                ps = filled(act, "xtr", c)
                act.activation(xtok[:, 0:2, c * P:c * P + P], ps[:, 0:256].rearrange("p (b s) -> p b s", b=2),
                               ACT.Copy).then_inc(sem("xtok"), 1)
                act.activation(xtok[0:TS, 2, c * P:c * P + P], ps[0:TS, 256:384], ACT.Copy)\
                   .then_inc(sem("xtok"), 1)
                frees("xtr", c, "xtok", 2 * c + 2)
            act.wait_ge(sem("route_step"), SEL_STEP)
            act.activation(e2[:, :], diff[:, :], ACT.Exp).then_inc(sem("share_exp"), 1)

            def gathered_high(n, half):
                act.wait_ge(sem("gathered"), n * 2 + (half + 1))
                act.activation(xg_h[:, 4 * half:4 * half + 4, :],
                               bank[2 + half][:, :].rearrange("p (c s) -> p c s", c=4), ACT.Copy)\
                   .then_inc(sem("xg_high"), 1)

            for half in range(2):
                gathered_high(0, half)
            act.wait_ge(sem("table_ready"), 1)
            tiles = act.value_load(table[0:1, 12:13], min_val=E, max_val=MAX_TILES)
            with act.Fori(0, tiles) as t:
                def turned_high(f):
                    act.wait_ge(sem("turned"), t * FB + (f + 1))
                    act.activation(hT_h[:, 4 * (f % 2):4 * (f % 2) + 4, :],
                                   bank[4 + f % 2][:, :].rearrange("p (c s) -> p c s", c=4), ACT.Copy)\
                       .then_inc(sem("hT_high"), 1)

                for p in range(EP):
                    kind, f = ORDER[p // 2]
                    act.wait_ge(sem("piece_used"), t * EP + (p + 1))
                    if p % 2 and kind == "g":
                        if f >= 2:
                            act.wait_ge(sem("hidden_ready"), t * FB + (f - 1))
                        act.activation(sbuf[:, f % 2, :], bank[2 * (f % 2)][:, :], ACT.Silu)\
                           .then_inc(sem("silu_done"), 1)
                        if f:
                            turned_high(f - 1)
                        if f == 1:
                            act.wait_ge(sem("ct_turned"), t + 1)
                            act.activation(ct[:, :], bank[5][:, 0:T], ACT.Copy).then_inc(sem("ct_ready"), 1)
                    if p % 2 and kind == "d" and f == FB - 2:
                        turned_high(FB - 1)
                        gathered_high(t + 1, 0)
                    if p == EP - 1:
                        act.activation(y_sl[:, 512:1024], bank[7][:, :], ACT.Copy).then_inc(sem("y_high"), 1)
                    nxt = p + HIGHS
                    s = nxt // 2 % SLOTS
                    act.wait_ge(sem(f"landed{s}"),
                                t * (16 * EB // SLOTS) + 16 * (landed_before(s) + nxt // 2 // SLOTS + 1))
                    act.activation(expert_high(nxt), expert_piece(nxt % EP, ring), ACT.Copy)\
                       .then_inc(sem("high_ready"), 1)
                gathered_high(t + 1, 1)
            norm_tail(4)
            for p in range(HIGHS, 6):
                act.wait_ge(sem(f"landed{p // 2}"), tiles * (16 * EB // SLOTS) + 16 * (landed_before(0) + 1))
                filled(act, "gate1", 3 if p - HIGHS < 2 else 7)
                act.activation(tail_high(p), tail_piece(p, ring), ACT.Copy).then_inc(sem("high_tail"), 1)
                if p == 4:
                    ple_gate(1)

        @block.gpsimd
        def _(pool):
            pool.wait_ge(sem("gm_loaded"), 32)
            pool.affine_select(out=gm_w[:, :, :], in_=gm_w[:, :, :], compare_op=ALU.is_ge, fill=0.0, base=0,
                               pattern=[[0, 8], [1, P]], channel_multiplier=-1).then_inc(sem("gm_masked"), 1)

        @block.tensor
        def _(pe):
            def claim(n):
                if n >= 8:
                    signal, value = free_by[n - 8]
                    pe.wait_ge(sem(signal), value)
                return bank[n % 8]

            def dense(name, pieces, rhs_h, rhs_l, n=T, before_chunk=None):
                i = 0
                for q in pieces:
                    _, kc, _, _, _, c0, c1, _ = PIECES[q]
                    hi, lo = piece_high(q), piece(q, low)
                    pe.wait_ge(sem("high_ready"), q + 1)
                    for j in range((c1 - c0) // P):
                        ps = claim(TILE[name] + i)[:, 0:n]
                        cols = slice(j * P, j * P + P)
                        for k in range(kc):
                            if i == 0 and before_chunk:
                                before_chunk(k)
                            pe.matmul(ps, hi[:, k, cols], rhs_h[:, k, 0:n], start=(k == 0), stop=False)
                            pe.matmul(ps, hi[:, k, cols], rhs_l[:, k, 0:n], start=False, stop=False)
                        if j == 0:
                            pe.wait_ge(sem("low_ready"), q + 1)
                        for k in range(kc):
                            mm = pe.matmul(ps, lo[:, k, cols], rhs_h[:, k, 0:n], start=False, stop=(k == kc - 1))
                        mm.then_inc(sem("tile_filled"), 1)
                        i += 1

            def norm_stats(n, summed):
                ps = claim(TILE[f"ln{n}"])
                pe.wait_ge(sem("summed"), summed)
                pe.matmul(ps[:, 0:T], ones, stat[:, 0, :], start=True, stop=True).then_inc(sem("tile_filled"), 1)
                ps = claim(TILE[f"ln{n}"] + 1)
                pe.wait_ge(sem("sq_summed"), 7 * (n + 1))
                pe.matmul(ps[:, 0:T], ones, stat[:, 1, :], start=True, stop=True).then_inc(sem("tile_filled"), 1)

            dense("in", range(0, 4), x_h, x_l, before_chunk=lambda k: pe.wait_ge(sem("x_split"), k + 1))
            pe.wait_ge(sem("const_loaded"), 16)
            ps = claim(TILE["rms"])
            for c in range(QC):
                pe.wait_ge(sem("in_squared"), c + 1)
                mm = pe.matmul(ps[:, 0:T], ones, in_sq[:, c, :], start=(c == 0), stop=(c == QC - 1))
            mm.then_inc(sem("tile_filled"), 1)
            ps = claim(TILE["rms"] + 1)
            for c in range(KC):
                pe.wait_ge(sem("in_squared"), QC + c + 1)
                mm = pe.matmul(ps[:, 0:T], ones, in_sq[:, QC + c, :], start=(c == 0), stop=(c == KC - 1))
            mm.then_inc(sem("tile_filled"), 1)
            ps = claim(TILE["krot"])
            pe.wait_ge(sem("in_copied"), 6)
            pe.matmul(ps[:, 0:T], rot_m, raw[:, 5, :], start=True, stop=True).then_inc(sem("tile_filled"), 1)
            pe.wait_ge(sem("latent_low"), 1)
            dense("qrope", range(4, 8), cq_h, cq_l)
            for c in range(4):
                ps = claim(TILE["qrot"] + c)
                pe.wait_ge(sem("qr_copied"), c + 1)
                pe.matmul(ps[:, 0:T], rot_m, qr_raw[:, c, :], start=True, stop=True).then_inc(sem("tile_filled"), 1)
            pe.wait_ge(sem("latent_low"), 2)
            dense("kup", [8], lat_h, lat_l, KEYS)
            pe.wait_ge(sem("high_ready"), 10)
            pe.wait_ge(sem("low_ready"), 10)
            for i in range(8):
                ps = claim(TILE["vup"] + i)
                rows, cols = slice(P * (i // 2), P * (i // 2) + P), slice(512 * (i % 2), 512 * (i % 2) + 512)
                parts = ((lat_h, piece_high(9)), (lat_l, piece_high(9)), (lat_h, piece(9, low)))
                for m, (left, right) in enumerate(parts):
                    for k in range(KC):
                        mm = pe.matmul(ps[:, :], left[:, k, rows], right[:, k, cols],
                                       start=(m == 0 and k == 0), stop=(m == 2 and k == KC - 1))
                mm.then_inc(sem("tile_filled"), 1)

            def scores(h):
                if h == 0:
                    pe.wait_ge(sem("kr_ready"), 1)
                    pe.wait_ge(sem("cache_kr_loaded"), 16)
                pe.wait_ge(sem("qn_ready"), h + 1)
                pe.wait_ge(sem("k_ready"), h + 1)
                pe.wait_ge(sem("qr_ready"), h // 2 + 1)
                rr = slice(ROPE * (h % 2), ROPE * (h % 2) + ROPE)
                n = ATT["S", h]
                for ps, parts in ((claim(n), ((0, P, 0, P, 0), (P, 2 * P, 0, 2 * P, P))),
                                  (claim(n + 1), ((TP, T, TP, KEYS, 0),))):
                    for q0, q1, k0, k1, at in parts:
                        o = ps[0:q1 - q0, at:at + k1 - k0]
                        pe.matmul(o, qn[:, h, q0:q1], kT[:, h, k0:k1], start=True, stop=False)
                        mm = pe.matmul(o, qr[rr, h // 2, q0:q1], kr[rr, k0:k1], start=False, stop=True)
                    mm.then_inc(sem("tile_filled"), 1)

            def turn_probs(h):
                ps = claim(ATT["T", h])
                pe.wait_ge(sem("probs_ready"), 3 * h + 3)
                b = probs[:, h % 2, :]
                for j in range(3):
                    pe.transpose(ps[:, j * P:j * P + P], b[:, j * P:j * P + P], ident)
                pe.transpose(ps[:, 384:416], b[0:TS, 384:512], ident[0:TS, 0:TS])
                pe.transpose(ps[0:TS, 416:448], b[0:TS, 512:544], ident[0:TS, 0:TS])\
                  .then_inc(sem("tile_filled"), 1)

            def values(h):
                ps = claim(ATT["O", h])
                if h == 0:
                    pe.wait_ge(sem("v_ready"), 8)
                pe.wait_ge(sem("probsT_ready"), 2 * h + 2)
                b, cols = probsT[:, h % 2, :], slice(h * VH, h * VH + VH)
                pe.matmul(ps[:, 0:TP], v[:, 0, cols], b[:, 0:TP], start=True, stop=False)
                pe.matmul(ps[:, P:TP], v[:, 1, cols], b[:, TP:TP + P], start=False, stop=True)
                pe.matmul(ps[:, TP:T], v[:, 2, cols], b[:, 384:416], start=True, stop=False)
                pe.matmul(ps[:, TP:T], v[0:TS, 3, cols], b[0:TS, 416:448], start=False, stop=True)\
                  .then_inc(sem("tile_filled"), 1)

            scores(0)
            for h in range(H):
                if h + 1 < H:
                    scores(h + 1)
                turn_probs(h)
                if h:
                    values(h - 1)
            values(H - 1)
            dense("att_out", range(10, 14), att_h, att_l,
                  before_chunk=lambda k: pe.wait_ge(sem("head_low"), k + 1))
            norm_stats(0, 7)
            dense("ffn", range(14, 36), x_h, x_l, before_chunk=lambda k: pe.wait_ge(sem("x_split"), 8 + k + 1))
            for i in range(DC):
                ps = claim(TILE["down"] + i)[:, 0:T]
                for r in range(2):
                    q = 36 + 2 * i + r
                    hi, lo = piece_high(q), piece(q, low)
                    pe.wait_ge(sem("high_ready"), q + 1)
                    for k in range(FC // 2):
                        c = r * (FC // 2) + k
                        if i == 0:
                            pe.wait_ge(sem("hid_low"), c + 1)
                        pe.matmul(ps, hi[:, k, :], hid_h[:, c, :], start=(c == 0), stop=False)
                        pe.matmul(ps, hi[:, k, :], hid_l[:, c, :], start=False, stop=False)
                    pe.wait_ge(sem("low_ready"), q + 1)
                    for k in range(FC // 2):
                        c = r * (FC // 2) + k
                        mm = pe.matmul(ps, lo[:, k, :], hid_h[:, c, :], start=False, stop=(c == FC - 1))
                    mm.then_inc(sem("down_half" if r == 0 else "tile_filled"), 1)
            norm_stats(1, 14)
            dense("gate0", range(52, 56), x_h, x_l, before_chunk=lambda k: pe.wait_ge(sem("x_split"), 16 + k + 1))
            pe.wait_ge(sem("p_low"), 1)
            dense("proj0", range(56, 58), p_h[0], p_l[0])
            dense("gm", range(58, 66), x_h, x_l, before_chunk=lambda k: pe.wait_ge(sem("x_split"), 24 + k + 1))
            norm_stats(2, 21)
            for g in range(8):
                ps = claim(TILE["vtr"] + g)
                pe.wait_ge(sem("normed"), 16 + g + 1)
                pe.transpose(ps[:, 0:P], gm_v[:, g, 0:P], ident)
                pe.transpose(ps[:, P:2 * P], gm_v[:, g, P:2 * P], ident)
                pe.transpose(ps[0:TS, 2 * P:3 * P], gm_v[:, g, TP:T], ident).then_inc(sem("tile_filled"), 1)
            pe.wait_ge(sem("gm_masked"), 1)
            for g in range(8):
                ps = claim(TILE["mix"] + g)
                pe.wait_ge(sem("vtok"), 2 * g + 2)
                for b in range(2):
                    pe.matmul(ps[:, b * P:b * P + P], gm_vtok[:, g, b * P:b * P + P], gm_w[:, g, :],
                              start=True, stop=True)
                pe.matmul(ps[:, TP:T], gm_vtok[0:TS, g, 2 * P:3 * P], gm_w[0:TS, g, 0:TS], start=True, stop=True)\
                  .then_inc(sem("tile_filled"), 1)
            dense("gm_out", range(66, 70), um_h, um_l, before_chunk=lambda k: pe.wait_ge(sem("um_low"), k + 1))
            norm_stats(3, 28)
            ps = claim(TILE["logits"])
            pe.wait_ge(sem("router_loaded"), 16)
            pe.wait_ge(sem("normed"), 32)
            for i, rows in enumerate((P, P, TS)):
                for k in range(DC):
                    mm = pe.matmul(ps[0:rows, 8 * i:8 * i + 8], x[:, k, i * P:i * P + rows], w_router[:, k, :],
                                   start=(k == 0), stop=(k == DC - 1))
            mm.then_inc(sem("tile_filled"), 1)
            for c in range(DC):
                ps = claim(TILE["xtr"] + c)
                pe.transpose(ps[:, 0:P], x[:, c, 0:P], ident)
                pe.transpose(ps[:, P:2 * P], x[:, c, P:2 * P], ident)
                pe.transpose(ps[0:TS, 2 * P:3 * P], x[:, c, TP:T], ident).then_inc(sem("tile_filled"), 1)
            ps = claim(TILE["rank"])
            pe.wait_ge(sem("route_step"), SEL_STEP)
            for i in range(4):
                o = ps[:, 8 * i:8 * i + 8]
                for j in range(min(i + 1, 3)):
                    mm = pe.matmul(o, before if j == i else ones, sel[:, j, :], start=(j == 0),
                                   stop=(j == min(i, 2)))
            mm.then_inc(sem("tile_filled"), 1)
            for signal, value in (free_by[TILE["rank"]], free_by[TILE["xtr"] + 7]):
                pe.wait_ge(sem(signal), value)

            def gather(n, half):
                pe.wait_ge(sem("onehot_ready"), n * 3 + 3)
                for c in range(4):
                    d = 4 * half + c
                    for i, rows in enumerate((P, P, TS)):
                        mm = pe.matmul(bank[2 + half][:, c * P:c * P + P],
                                       xtok[0:rows, i, d * P:d * P + P], onehot[0:rows, i, :],
                                       start=(i == 0), stop=(i == 2))
                mm.then_inc(sem("gathered"), 1)

            for half in range(2):
                gather(0, half)
            pe.wait_ge(sem("table_ready"), 1)
            tiles = pe.value_load(table[0:1, 12:13], min_val=E, max_val=MAX_TILES)
            with pe.Fori(0, tiles) as t:
                def turn(f):
                    pe.wait_ge(sem("hidden_ready"), t * FB + (f + 1))
                    if f >= 2:
                        pe.wait_ge(sem("hT_low"), t * FB + (f - 1))
                    elif f == 1:
                        pe.wait_ge(sem("ct_ready"), t + 1)
                    for c in range(4):
                        tr = pe.transpose(bank[4 + f % 2][:, c * P:c * P + P], hbuf[:, f % 2, c * P:c * P + P],
                                          ident)
                    tr.then_inc(sem("turned"), 1)

                def products(p, left_h, left_l, kc, outs):
                    first, last, dst = outs
                    width = PIECE // kc
                    hi = expert_high(p).rearrange("p (k n) -> p k n", k=kc)
                    lo = expert_piece(p, low).rearrange("p (k n) -> p k n", k=kc)
                    pe.wait_ge(sem("high_ready"), t * EP + (NP + p + 1))
                    for m, (left, right) in enumerate(((left_h, hi), (left_l, hi), (left_h, lo))):
                        if m == 2:
                            pe.wait_ge(sem("low_ready"), t * EP + (NP + p + 1))
                        for k in range(kc):
                            for n in range(width // 512):
                                mm = pe.matmul(dst[n][:, :], left(k), right[:, k, 512 * n:512 * n + 512],
                                               start=(first and m == 0 and k == 0),
                                               stop=(last and m == 2 and k == kc - 1))
                    mm.then_inc(sem("piece_used"), 1)

                for j, (kind, f) in enumerate(ORDER):
                    if kind == "d":
                        pe.wait_ge(sem("hT_low"), t * FB + (f + 1))
                        for r in range(2):
                            at = 4 * (f % 2) + 2 * r
                            products(2 * j + r, lambda k, at=at: hT_h[:, at + k, :],
                                     lambda k, at=at: hT_l[:, at + k, :], 2,
                                     (f == 0 and r == 0, f == FB - 1 and r == 1, (bank[6], bank[7])))
                        if f == FB - 2:
                            turn(FB - 1)
                            gather(t + 1, 0)
                        continue
                    up = int(kind == "u")
                    if f >= 2:
                        pe.wait_ge(sem("hidden_ready" if up else "silu_done"), t * FB + (f - 1))
                    elif f == 0:
                        pe.wait_ge(sem("added"), t * DC + (3 + up))
                    if j == 0:
                        pe.wait_ge(sem("xg_low"), t * 2 + 2)
                    for r in range(2):
                        products(2 * j + r, lambda k, r=r: xg_h[:, 4 * r + k, :], lambda k, r=r: xg_l[:, 4 * r + k, :],
                                 4, (r == 0, r == 1, (bank[2 * (f % 2) + up],)))
                    if f == 1 and not up:
                        pe.wait_ge(sem("added"), t * DC + DC)
                    if f and not up:
                        turn(f - 1)
                    if f == 1 and not up:
                        pe.wait_ge(sem("onehot_c_ready"), t * 3 + 3)
                        for i, rows in enumerate((P, P, TS)):
                            tr = pe.transpose(bank[5][:, i * P:i * P + rows], onehot_c[0:rows, i, :],
                                              ident[0:rows, 0:rows])
                        tr.then_inc(sem("ct_turned"), 1)
                gather(t + 1, 1)
                pe.wait_ge(sem("y_low"), t + 1)
                for c in range(DC):
                    if c == 4:
                        pe.wait_ge(sem("y_high"), t + 1)
                    if c >= 6:
                        pe.wait_ge(sem("added"), t * DC + (DC + c - 6 + 1))
                    pe.matmul(bank[SCATTER[c]][:, 0:T], y_sl[:, c * P:c * P + P], ct[:, :], start=True, stop=True)\
                      .then_inc(sem("scattered"), 1)
            pe.wait_ge(sem("added"), tiles * DC + DC)
            norm_stats(4, 35)
            for b in range(2):
                for j in range(4):
                    ps = claim(TILE["gate1"] + 4 * b + j)[:, 0:T]
                    cols = slice(j * P, j * P + P)
                    for p in (2 * b, 2 * b + 1):
                        if j == 0 and p < HIGHS:
                            pe.wait_ge(sem("high_ready"), tiles * EP + (NP + p + 1))
                            pe.wait_ge(sem("low_ready"), tiles * EP + (NP + p + 1))
                        elif j == 0:
                            pe.wait_ge(sem("high_tail"), p - HIGHS + 1)
                            pe.wait_ge(sem("low_tail"), p - HIGHS + 1)
                        hi = tail_high(p).rearrange("p (k n) -> p k n", k=4)
                        lo = tail_piece(p, low).rearrange("p (k n) -> p k n", k=4)
                        for k in range(4):
                            c = 4 * (p % 2) + k
                            if b == 0 and j == 0:
                                pe.wait_ge(sem("x_split"), 32 + c + 1)
                            pe.matmul(ps, hi[:, k, cols], x_h[:, c, :], start=(c == 0), stop=False)
                            pe.matmul(ps, hi[:, k, cols], x_l[:, c, :], start=False, stop=False)
                            mm = pe.matmul(ps, lo[:, k, cols], x_h[:, c, :], start=False, stop=(c == DC - 1))
                    mm.then_inc(sem("tile_filled"), 1)
            pe.wait_ge(sem("p_low"), 2)
            pe.wait_ge(sem("high_tail"), 3)
            pe.wait_ge(sem("low_tail"), 3)
            for c in range(DC):
                ps = claim(TILE["proj1"] + c)[:, 0:T]
                cols = slice(c * P, c * P + P)
                for k in range(PC):
                    pe.matmul(ps, tail_high(4 + k)[:, cols], p_h[1][:, k, :], start=(k == 0), stop=False)
                    pe.matmul(ps, tail_high(4 + k)[:, cols], p_l[1][:, k, :], start=False, stop=False)
                    mm = pe.matmul(ps, tail_piece(4 + k, low)[:, cols], p_h[1][:, k, :], start=False,
                                   stop=(k == PC - 1))
                mm.then_inc(sem("tile_filled"), 1)

        @block.sync
        def _(sp):
            sp.dma_start(x, a["x"]).then_inc(sem("x_loaded"), 16)
            n = 0
            for name, blocks, width in TRUNK:
                for b in range(blocks):
                    if n >= TRUNK_SLOTS:
                        sp.wait_ge(sem("tile_filled"), LAST_TILE[n - TRUNK_SLOTS] + 1)
                    s = n % TRUNK_SLOTS
                    sp.dma_start(ring[s][:, 0:width], a[name][b]).then_inc(sem(f"landed{s}"), 16)
                    n += 1
                if name == "mla_out":
                    sp.wait_ge(sem("latent"), QC + KC)
                    sp.dma_start(out["lat"], lat[:, :, 0:T]).then_inc(sem("lat_out"), 16)
                    sp.wait_ge(sem("kr_ready"), 1)
                    sp.dma_start(out["kr"], kr[0:ROPE, 0:T]).then_inc(sem("kr_out"), 16)
                if name == "ffn_in":
                    sp.wait_ge(sem("tile_filled"), ATT["T", H - 1] + 1)
                    sp.dma_start(p_raw[0], a["p"][0]).then_inc(sem("p_loaded0"), 16)
                if name == "gm_in":
                    sp.wait_ge(sem("tile_filled"), TILE["down"] + 8)
                    sp.dma_start(gm_bias, a["gm_bias"].broadcast_to([P, 8 * T]).rearrange("p (g t) -> p g t", g=8))\
                      .then_inc(sem("gm_loaded"), 16)
                    sp.dma_start(gm_w, a["gm_w"]).then_inc(sem("gm_loaded"), 16)
            sp.wait_ge(sem("lat_out"), 16)
            for j in range(SLOTS):
                if j < TRUNK_SLOTS:
                    sp.wait_ge(sem("tile_filled"), LAST_TILE[N_TRUNK - TRUNK_SLOTS + j] + 1)
                else:
                    sp.wait_ge(sem("mixed"), 8)
                sp.dma_start(ring[j][:, :], a["moe"][0, j]).then_inc(sem(f"landed{j}"), 16)
            sp.dma_start(p_raw[1], a["p"][1]).then_inc(sem("p_loaded1"), 16)
            sp.wait_ge(sem("table_ready"), 1)
            last = sp.value_load(table[0:1, 13:14], min_val=E - 1, max_val=MAX_TILES - 1)

            def expert_load(t, e, j):
                sp.wait_ge(sem("piece_used"), t * EP + 2 * (j - SLOTS + 1))
                sp.dma_start(ring[j % SLOTS][:, :], a["moe"][bass.ds(e, 1), j % EB].rearrange("a p n -> p (a n)"))\
                  .then_inc(sem(f"landed{j % SLOTS}"), 16)

            with sp.Fori(0, last) as t:
                e = sp.value_load(table[0:1, bass.ds(t, 1)], min_val=0, max_val=E - 1)
                for j in range(SLOTS, EB):
                    expert_load(t, e, j)
                e = sp.value_load(table[0:1, bass.ds(t + 1, 1)], min_val=0, max_val=E - 1)
                for j in range(SLOTS):
                    expert_load(t, e, EB + j)
            e = sp.value_load(table[0:1, bass.ds(last, 1)], min_val=0, max_val=E - 1)
            for j in range(SLOTS, EB):
                expert_load(last, e, j)
            s = 0
            for name, blocks, width in TAIL:
                for b in range(blocks):
                    sp.wait_ge(sem("piece_used"), last * EP + 2 * (EB + s - SLOTS + 1))
                    sp.dma_start(ring[s][:, 0:width], a[name][b]).then_inc(sem(f"landed{s}"), 16)
                    s += 1
            sp.wait_ge(sem("ple_added"), 16)
            sp.dma_start(out["y"], x).then_inc(sem("y_out"), 16)
            for name in ("lat_out", "kr_out", "gm_v_out", "y_out"):
                sp.wait_ge(sem(name), 16)


def by_chunk(w, kc, per):
    n = w.shape[1] // (per * P)
    return np.ascontiguousarray(w.reshape(kc, P, n, per * P).transpose(2, 1, 0, 3).reshape(n, P, kc * per * P))


def feature_major(x):
    return np.ascontiguousarray(x.T.reshape(-1, P, x.shape[0]).transpose(1, 0, 2))


def token_major(x):
    return np.ascontiguousarray(x.transpose(1, 0, 2).reshape(-1, x.shape[2]).T)


def kernel(**inputs):
    import concourse.bacc as bacc
    from concourse.bass_utils import run_bass_kernel_spmd

    i = {k: np.asarray(v) for k, v in inputs.items()}
    w_in = i["w_mla_in"][0]
    w_in = np.concatenate([w_in, w_in[:, QL + KVL:]], axis=1)
    w_q = i["w_q_up"][0].reshape(QL, H, NOPE + ROPE)
    w_q = np.concatenate([w_q[:, :, NOPE:].reshape(QL, -1), w_q[:, :, :NOPE].reshape(QL, -1)], axis=1)
    w_kv = i["w_kv_up"][0].reshape(KVL, H, NOPE + VH)
    w_kv = np.concatenate([w_kv[:, :, :NOPE].reshape(KVL, -1), w_kv[:, :, NOPE:].reshape(KVL, -1)], axis=1)
    w_f = np.stack([i["w_ffn_gate"][0].reshape(D, FC, P), i["w_ffn_up"][0].reshape(D, FC, P)], axis=2)
    w_gm = i["w_gm_in"][0]
    w_gm = np.concatenate([w_gm[:, D:], w_gm[:, :D]], axis=1)
    moe = np.empty((E, EB, P, BLK), np.float32)
    for e in range(E):
        for kind, name in (("g", "w_moe_gate"), ("u", "w_moe_up")):
            moe[e, AT[kind]] = i[name][0, e].reshape(DC, P, FB, 512).transpose(2, 1, 0, 3).reshape(FB, P, BLK)
        moe[e, AT["d"]] = i["w_moe_down"][0, e].reshape(FB, 4, P, D).transpose(0, 2, 1, 3).reshape(FB, P, BLK)
    cols = [i["g_q_norm"][0].reshape(QC, P), i["g_kv_norm"][0].reshape(KC, P), i["g_gm_norm"][0].reshape(DC, P),
            i["b_gm_norm"][0].reshape(DC, P)]
    for name in ("ln1_g", "ln2_g", "ln1_b", "ln2_b"):
        cols.append(i[name].reshape(2 * DC, P))
    b_s = i["b_gm_spatial"][0]
    arrays = {
        "x": feature_major(np.concatenate([i["x_prompt"][0], i["x_sample"][0]])),
        "cache_lat": feature_major(i["cache_mla_latent"][0, 0]),
        "cache_kr": np.ascontiguousarray(np.concatenate([i["cache_mla_krope"][0, 0].T] * 2)),
        "p": np.stack([feature_major(np.concatenate([i["p_prompt"][n, 0], i["p_sample"][n, 0]])) for n in range(2)]),
        "vec": np.ascontiguousarray(np.concatenate(cols).T),
        "w_router": np.ascontiguousarray(i["w_router"][0].reshape(DC, P, E).transpose(1, 0, 2)),
        "gm_w": np.ascontiguousarray(i["w_gm_spatial"][0].transpose(2, 0, 1)),
        "gm_bias": np.ascontiguousarray(np.concatenate([b_s, b_s, b_s[:, :TS]], axis=1).reshape(1, 8 * T)),
        "mla_in": by_chunk(w_in, DC, 3), "q_up": by_chunk(w_q, QC, 6), "kv_up": by_chunk(w_kv, KC, 16),
        "mla_out": by_chunk(i["w_mla_out"][0], DC, 4), "ffn_in": by_chunk(w_f.reshape(D, -1), DC, 4),
        "ffn_down": by_chunk(i["w_ffn_down"][0], FC, 1), "gm_in": by_chunk(w_gm, DC, 4),
        "gm_out": by_chunk(i["w_gm_out"][0], DC, 4), "moe": moe,
    }
    for n in range(2):
        arrays[f"ple_gate{n}"] = by_chunk(i["w_ple_gate"][n], DC, 4)
        arrays[f"ple_proj{n}"] = by_chunk(i["w_ple_proj"][n], PC, 8)
    outputs = {"lat": (P, KC, T), "kr": (ROPE, T), "gm_v": (P, DC, GM_CHUNK + TS), "y": (P, DC, T)}

    nc = bacc.Bacc("TRN2", target_bir_lowering=False, num_devices=1)
    a = {n: nc.dram_tensor(f"in_{n}", v.shape, F32, kind="ExternalInput").ap() for n, v in arrays.items()}
    a["const"] = nc.inline_tensor(constants(), "tables")[:, :]
    out = {n: nc.dram_tensor(f"out_{n}", s, F32, kind="ExternalOutput").ap() for n, s in outputs.items()}
    build(nc, a, out)
    r = run_bass_kernel_spmd(nc, [{f"in_{n}": v for n, v in arrays.items()}], core_ids=[0]).results[0]
    y, lat, gm_v = token_major(r["out_y"]), token_major(r["out_lat"]), token_major(r["out_gm_v"])
    kr = np.ascontiguousarray(r["out_kr"].T)
    return (y[None, :TP], y[None, TP:], lat[None, None, :TP], kr[None, None, :TP], lat[None, None, TP:],
            kr[None, None, TP:], gm_v[None, None, :GM_CHUNK], gm_v[None, None, GM_CHUNK:])
```

```python
from contextlib import ExitStack

import numpy as np

import concourse.bass as bass
from concourse import mybir

F32 = mybir.dt.float32
F32R = mybir.dt.float32r
I32 = mybir.dt.int32
U32 = mybir.dt.uint32
ALU = mybir.AluOpType
ACT = mybir.ActivationFunctionType
AX_X = mybir.AxisListType.X

P = 128
D = 1024
DC = D // P
TP, TS = 256, 32
T = TP + TS
PAST = 128
KEYS = T + PAST
CHUNK = 64
H, NOPE, ROPE, VH = 8, 128, 64, 128
QL, KVL = 384, 256
QC, KC = QL // P, KVL // P
FF = 2816
FC = FF // P
E, FE = 8, 3584
FB = FE // 512
PLE = 256
PC = PLE // P
ALPHA = 4.0 ** 0.25
SCALE = (NOPE + ROPE) ** -0.5
EPS_LN, EPS_RMS = 1e-5, 1e-6
GM_CHUNK = 128

SLOTS = 7
TRUNK_SLOTS = 5
BLK = 4096
PIECE = 2048
HIGHS = 3
TRUNK = [("mla_in", 2, DC * 384), ("q_up", 2, QC * 768), ("kv_up", 1, KC * 2048), ("mla_out", 2, DC * 512),
         ("ffn_in", 11, DC * 512), ("ffn_down", 8, FC * 128), ("ple_proj0", 1, PC * 1024),
         ("ple_gate0", 2, DC * 512), ("gm_in", 4, DC * 512), ("gm_out", 2, DC * 512)]
TAIL = PC * 1024 + 2 * DC * 512
N_TRUNK = sum(n for _, n, _ in TRUNK)
EB = 3 * FB
assert N_TRUNK % TRUNK_SLOTS == 0 and EB % SLOTS == 0
MAX_TILES = 12

G_Q, G_KV, G_GM, B_GM = 0, 3, 5, 13
LN_G = {0: 21, 1: 37, 3: 29, 4: 45}
LN_B = {0: 53, 1: 69, 3: 61, 4: 77}
N_VEC = 85

PLAN = [("in", 3), ("in_kv", 2), ("rms_q", 1), ("in_kr", 1), ("rms_kv", 1), ("krot", 1), ("qrope", 4), ("qnope", 8), ("qrot", 4), ("kup", 8), ("vup", 8)]
ATT = {}
_n = sum(n for _, n in PLAN)
ATT["S", 0] = _n
_n += 2
ATT["S", 1] = _n
_n += 2
for _h in range(H):
    if _h + 2 < H:
        ATT["S", _h + 2] = _n
        _n += 2
    ATT["T", _h] = _n
    _n += 1
    if _h:
        ATT["O", _h - 1] = _n
        _n += 1
ATT["O", H - 1] = _n
_n += 1
PLAN += [("attention", _n - sum(n for _, n in PLAN)), ("att_out", 8), ("mean0", 1), ("var0", 1), ("ffn", 4 * 11),
         ("down", 8), ("mean1", 1), ("proj0a", 4), ("var1", 1), ("proj0b", 4), ("gate0", 8), ("gm_v", 8),
         ("gm_u0", 2), ("mean2", 1), ("gm_u2", 4), ("var2", 1), ("gm_u6", 2), ("vtr", 8), ("mix", 8),
         ("gm_out", 8), ("mean3", 1), ("var3", 1), ("logits_t", 1), ("logits", 1), ("xtr", 4), ("rank", 1), ("xtr_b", 4), ("mean4", 1),
         ("proj1a", 4), ("var4", 1), ("proj1b", 4), ("gate1", 8)]
TILE = {}
_n = 0
for _name, _k in PLAN:
    TILE[_name] = _n
    _n += _k

LAST_TILE = []
for _name, _k, _per in (("in", 1, 3), ("in_kr", 1, 1), ("qrope", 2, 6), ("kup", 1, 16), ("att_out", 2, 4), ("ffn", 11, 4),
                        ("down", 8, 1), ("proj0b", 1, 4), ("gate0", 2, 4), ("gm_v", 2, 4), ("gm_u2", 1, 2),
                        ("gm_u6", 1, 2), ("gm_out", 2, 4)):
    LAST_TILE += [TILE[_name] + _per * (_b + 1) - 1 for _b in range(_k)]
assert len(LAST_TILE) == N_TRUNK

PIECES = []
for _b, (_most, _rest) in enumerate(((TILE["in"] + 2, TILE["in"] + 3), (TILE["in_kv"] + 2, TILE["in_kr"] + 1))):
    PIECES += [(_b, DC, 384, 0, DC, 0, 256, ("tile_filled", _most)),
               (_b, DC, 384, 0, DC, 256, 384, ("tile_filled", _rest))]
for _b in range(4):
    PIECES.append((2 + _b // 2, QC, 768, 0, QC, 384 * (_b % 2), 384 * (_b % 2) + 384,
                   ("tile_filled", TILE["qrope"] + 3 * _b + 3)))
for _b, _name in enumerate(("kup", "vup")):
    PIECES.append((4, KC, 2048, 0, KC, 1024 * _b, 1024 * _b + 1024, ("tile_filled", TILE[_name] + 8)))


def _by_columns(name, block, n):
    for b in range(n):
        for h_ in range(2):
            PIECES.append((block + b, DC, 512, 0, DC, 256 * h_, 256 * h_ + 256,
                           ("tile_filled", TILE[name] + 4 * b + 2 * h_ + 2)))


_by_columns("att_out", 5, 2)
_by_columns("ffn", 7, 11)
for _b in range(8):
    PIECES += [(18 + _b, FC, P, 0, FC // 2, 0, P, ("down_half", _b + 1)),
               (18 + _b, FC, P, FC // 2, FC, 0, P, ("tile_filled", TILE["down"] + _b + 1))]
for _b in range(2):
    PIECES.append((26, PC, 1024, 0, PC, 512 * _b, 512 * _b + 512, ("tile_filled", TILE["proj0" + "ab"[_b]] + 4)))
_by_columns("gate0", 27, 2)
_by_columns("gm_v", 29, 2)
for _b, _last in enumerate((TILE["gm_u0"] + 1, TILE["gm_u2"] + 1, TILE["gm_u2"] + 3, TILE["gm_u6"] + 1)):
    PIECES.append((31 + _b // 2, DC, 512, 0, DC, 256 * (_b % 2), 256 * (_b % 2) + 256, ("tile_filled", _last + 1)))
_by_columns("gm_out", 33, 2)
NP = len(PIECES)
assert NP == 2 * N_TRUNK and (2 * EB) % HIGHS == 0
EP = 2 * EB
ORDER = [("g", 0), ("u", 0)]
for _f in range(1, FB):
    ORDER += [("g", _f), ("u", _f), ("d", _f - 1)]
ORDER += [("d", FB - 1)]
AT = {_k: [_j for _j, (_kind, _) in enumerate(ORDER) if _kind == _k] for _k in "gud"}


def constants():
    ones = np.ones((P, P), np.float32)
    ident = np.eye(P, dtype=np.float32)
    half = ROPE // 2
    rot = np.zeros((P, P), np.float32)
    for b in range(P // ROPE):
        for i in range(half):
            rot[b * ROPE + half + i, b * ROPE + i] = -1.0
            rot[b * ROPE + i, b * ROPE + half + i] = 1.0
    before = np.triu(ones, 1)
    ramp = np.broadcast_to(np.arange(1, P + 1, dtype=np.float32), (P, P))
    pos = np.concatenate([np.arange(TP), PAST + np.arange(TS)]).astype(np.float32)
    inv = (np.float32(10000.0) ** (-np.arange(half, dtype=np.float32) / np.float32(half))).astype(np.float32)
    ang = (pos[None, :] * inv[:, None]).astype(np.float32)
    cos = np.tile(np.cos(ang), (P // half, 1)).astype(np.float32)
    sin = np.tile(np.sin(ang), (P // half, 1)).astype(np.float32)
    eps = np.tile(np.array([[EPS_LN, EPS_RMS]], np.float32), (P, 1))
    base = np.broadcast_to(np.arange(E - 1, -1, -1, dtype=np.float32) * P, (P, E))
    ramp8 = np.tile(np.arange(E, dtype=np.float32), (P, 3))
    ramp8[TS:, 2 * E:] = -1.0
    base1 = np.tile(np.arange(E, dtype=np.float32) * P + 1.0, (P, 3))
    ramp4 = np.tile(np.repeat(np.arange(4, dtype=np.float32), E - 1), (P, 1))
    return np.ascontiguousarray(
        np.concatenate([ones, ident, rot, before, ramp, cos, sin, eps, base, ramp8, base1, ramp4], axis=1))


C_ONES, C_ID, C_ROT, C_BEF, C_RAMP, C_COS = 0, 128, 256, 384, 512, 640
C_SIN = C_COS + T
C_EPS = C_SIN + T
C_BASE = C_EPS + 2
C_RAMP8 = C_BASE + E
C_BASE1 = C_RAMP8 + 3 * E
C_RAMP4 = C_BASE1 + 3 * E
N_CONST = C_RAMP4 + 4 * (E - 1)
SEL_STEP = 13
MID_STEP = SEL_STEP + 6


def build(nc, a, out):
    with ExitStack() as ctx:
        names = {}

        def sem(name):
            if name not in names:
                names[name] = ctx.enter_context(nc.semaphore(name))
            return names[name]

        start = (nc.sbuf_base + 31) // 32 * 32
        place = [start]

        def sb(name, shape, dt=F32, at=None):
            if at is None:
                at = place[0]
                place[0] += (int(np.prod(shape[1:])) * 4 + 31) // 32 * 32
            return nc.alloc_sbuf_tensor_at(name, shape, dt, offset=at)

        const = sb("const", [P, N_CONST])
        vec = sb("vec", [P, N_VEC])
        w_router = sb("w_router", [P, DC, E])
        small = sb("small", [P, 400])
        table = sb("table", [P, 16], I32)
        maxidx = sb("maxidx", [P, 3, 8], U32)
        high = [sb(f"high{i}", [P, PIECE], F32R) for i in range(HIGHS)]
        ring, low = [], []
        for i in range(TRUNK_SLOTS):
            ring.append(sb(f"ring{i}", [P, BLK]))
            low.append(sb(f"low{i}", [P, BLK], F32R, at=place[0] - 4 * BLK))
        base = place[0]
        WORK = 24672
        LENT = WORK - (SLOTS - TRUNK_SLOTS) * BLK
        assert base + 4 * WORK <= nc.sbuf_usable_end
        for i in range(TRUNK_SLOTS, SLOTS):
            at = base + 4 * (LENT + BLK * (i - TRUNK_SLOTS))
            ring.append(sb(f"ring{i}", [P, BLK], at=at))
            low.append(sb(f"low{i}", [P, BLK], F32R, at=at))

        def area(name, at, chunks, width, dt=F32):
            assert at + chunks * width <= WORK
            return sb(name, [P, chunks, width], dt, at=base + 4 * at)[:, :, :]

        bank = [ctx.enter_context(nc.psum_tensor(f"bank{i}", [P, 512], F32)) for i in range(8)]

        ones, ident, rot_m = const[:, 0:128], const[:, 128:256], const[:, 256:384]
        before, ramp = const[:, C_BEF:C_BEF + P], const[:, C_RAMP:C_RAMP + P]
        cos, sin = const[:, C_COS:C_COS + T], const[:, C_SIN:C_SIN + T]
        eps_ln, eps_rms = const[:, C_EPS:C_EPS + 1], const[:, C_EPS + 1:C_EPS + 2]

        x = area("x", 0, DC, T)
        x_h = area("x_h", 2304, DC, T, F32R)
        x_l = area("x_l", 4608, DC, T, F32R)
        res = area("res", 2304, DC, T)
        sq = area("sq", 4608, DC, T)
        stat = area("stat", 6912, 4, T)
        logits_t = stat[0:E, 1, :]
        kT = area("kT", 2304, H, KEYS)
        probsT = area("probsT", 5632, 2, 448)
        raw = area("raw", 8064, 6, T)
        cq_h = area("cq_h", 9792, QC, T, F32R)
        cq_l = area("cq_l", 10656, QC, T, F32R)
        lat_h = area("lat_h", 11520, KC, 512, F32R)
        lat_l = area("lat_l", 12544, KC, 512, F32R)
        att_h = area("att_h", 8064, DC, T, F32R)
        att_l = area("att_l", 10368, DC, T, F32R)
        qn = area("qn", 13568, DC, T)
        in_sq = area("in_sq", 13568, QC + KC, T)
        qr = area("qr", 15872, 4, T)
        qr_raw = area("qr_raw", 17024, 4, T)
        v = area("v", 18176, 4, 1024)
        kr = area("kr", 22272, 1, KEYS)[:, 0, :]
        lat = area("lat", 22688, KC, KEYS)
        probs = area("probs", 23520, 2, 544)
        rope_tmp = area("rope_tmp", 23520, 4, T)
        hid_h = area("hid_h", 8064, FC, T, F32R)
        hid_l = area("hid_l", 14400, FC, T, F32R)
        sil = area("sil", 20736, 3, T)
        hid = area("hid", 21600, 3, T)
        ple_s = area("ple_s", 8064, DC, T)
        gate_s = area("gate_s", 10368, DC, T)
        p_raw = [area("p_raw0", 23520, PC, T), area("p_raw1", 15904, PC, T)]
        p_l = [area("p_l0", 23520, PC, T, F32R), area("p_l1", 15904, PC, T, F32R)]
        p_h = [area("p_h0", 24096, PC, T, F32R), area("p_h1", 15232, PC, T, F32R)]
        gm_res = area("gm_res", 8064, DC, T)
        gm_v = area("gm_v", 10368, DC, T)
        um_h = area("um_h", 8064, DC, T, F32R)
        um_l = area("um_l", 10368, DC, T, F32R)
        gm_u = area("gm_u", 12672, DC, T)
        gm_vtok = area("gm_vtok", 14976, 8, 3 * P)
        z_h = area("z_h", 14976, DC, T, F32R)
        z_l = area("z_l", 17280, DC, T, F32R)
        gm_bias = area("gm_bias", 2304, 8, T)
        gm_w = area("gm_w", 20352, 8, P)
        gm_tmp = area("gm_tmp", 21376, 2, T)
        eq = area("eq", 0, 6, P)
        xtok = area("xtok", 4608, 3, D)
        xg_h = area("xg_h", 7680, DC, P, F32R)
        xg_l = area("xg_l", 8704, DC, P, F32R)
        hT_h = area("hT_h", 9728, 8, P, F32R)
        hT_l = area("hT_l", 10752, 8, P, F32R)
        hbuf = area("hbuf", 11776, 2, 512)
        sbuf = area("sbuf", 12800, 2, 512)
        y_h = area("out_h", 13824, 1, D, F32R)[:, 0, :]
        ct = area("ct", 14848, 1, T, F32R)[:, 0, :]
        onehot = area("onehot", 768, 3, P)
        y_l = area("out_l", 1152, 1, D, F32R)[:, 0, :]
        sm = small
        mx = sm[:, 0:6].rearrange("p (b c) -> p b c", b=2)
        nmx = sm[:, 6:12].rearrange("p (b c) -> p b c", b=2)
        psum_r = sm[:, 12:18].rearrange("p (b c) -> p b c", b=2)
        prec = sm[:, 18:24].rearrange("p (b c) -> p b c", b=2)
        lg = sm[:, 24:48].rearrange("p (b c) -> p b c", b=3)
        mx8 = sm[:, 48:72].rearrange("p (b c) -> p b c", b=3)
        idx = sm[:, 72:96].rearrange("p (b c) -> p b c", b=3)
        oneA = sm[:, 96:120].rearrange("p (b c) -> p b c", b=3)
        oneB = sm[:, 120:144].rearrange("p (b c) -> p b c", b=3)
        sel = sm[:, 144:168].rearrange("p (b c) -> p b c", b=3)
        rank = sm[:, 168:200].rearrange("p (b c) -> p b c", b=4)
        big = sm[:, 200:224].rearrange("p (b c) -> p b c", b=3)
        slot_of = sm[:, 224:248].rearrange("p (b c) -> p b c", b=3)
        picked = sm[:, 248:296].rearrange("p (k b c) -> p k b c", k=2, b=3)
        where = sm[:, 296:302].rearrange("p (k b) -> p k b", k=2)
        share = sm[:, 302:308].rearrange("p (k b) -> p k b", k=2)
        over, shift = sm[:, 316:324], sm[:, 333:341]
        slot_share = sm[:, 324:325]
        sums_a, sums_b = sm[:, 367:383], sm[:, 383:399]
        diff, e2, den = sm[:, 341:344], sm[:, 344:347], sm[:, 347:350]
        ids = sm[:, 353:367]
        cmp = sm[:, 248:276].rearrange("p (b c) -> p b c", b=4)

        free_by = {}

        def filled(eng, name, i=0):
            n = TILE[name] + i
            eng.wait_ge(sem("tile_filled"), n + 1)
            return bank[n % 8]

        def filled_at(eng, n):
            eng.wait_ge(sem("tile_filled"), n + 1)
            return bank[n % 8]

        def frees(name, i, signal, value):
            free_by[TILE[name] + i] = (signal, value)

        block = ctx.enter_context(nc.Block())
        LN_OF = {0: "att_out", 1: "down", 3: "gm_out"}

        def piece(q, tensors):
            n, kc, width, k0, k1, c0, c1, _ = PIECES[q]
            m = tensors[n % TRUNK_SLOTS][:, 0:kc * width].rearrange("p (k m) -> p k m", k=kc)
            return m[:, k0:k1, c0:c1]

        def piece_high(q):
            _, _, _, k0, k1, c0, c1, _ = PIECES[q]
            m = high[q % HIGHS][:, 0:(k1 - k0) * (c1 - c0)]
            return m.rearrange("p (k m) -> p k m", k=k1 - k0)

        def expert_piece(p, tensors):
            return tensors[p // 2 % SLOTS][:, PIECE * (p % 2):PIECE * (p % 2) + PIECE]

        def expert_high(p):
            return high[(NP + p) % HIGHS][:, :]

        SCATTER = (4, 5, 0, 1, 6, 7, 2, 4)

        def tail_piece(p, tensors):
            return tensors[p // 2][:, PIECE * (p % 2):PIECE * (p % 2) + PIECE]

        def tail_high(p):
            return high[(NP + p) % HIGHS][:, :]

        def in_tile(c):
            return ("in", c) if c < QC else ("in_kv", c - QC) if c < QC + KC else ("in_kr", 0)

        def xtr_tile(c):
            return ("xtr", c) if c < 4 else ("xtr_b", c - 4)

        def proj_tile(n, c):
            return f"proj{n}" + "ab"[c // 4], c % 4

        def gm_tile(c):
            for name, first in (("gm_u6", 14), ("gm_u2", 10), ("gm_u0", 8), ("gm_v", 0)):
                if c >= first:
                    return name, c - first

        def landed_before(s):
            return N_TRUNK // TRUNK_SLOTS if s < TRUNK_SLOTS else 0

        @block.vector
        def _(dve):
            def residual(n, c):
                ps = filled(dve, LN_OF[n], c)
                if n == 1 and c == 0:
                    dve.wait_ge(sem("normed"), 8)
                at = 8 * len(done) + c + 1
                dve.scalar_tensor_tensor(res[:, c, :], x[:, c, :], ALPHA, ps[:, 0:T], ALU.mult,
                                         ALU.add).then_inc(sem("residual"), 1)
                frees(LN_OF[n], c, "residual", at)
                add_up(c, "residual", at)
                if c == DC - 1:
                    done.append(n)

            def split_low(q):
                dve.wait_ge(sem("high_ready"), q + 1)
                dve.tensor_tensor(piece(q, low), piece(q, ring), piece_high(q).bitcast(F32), ALU.subtract)\
                   .then_inc(sem("low_ready"), 1)

            def first_low(p):
                dve.wait_ge(sem("high_ready"), NP + p + 1)
                dve.tensor_tensor(expert_piece(p, low), expert_piece(p, ring), expert_high(p).bitcast(F32),
                                  ALU.subtract).then_inc(sem("low_ready"), 1)

            def after(q):
                if q + HIGHS < NP:
                    split_low(q + HIGHS)

            def add_up(c, signal, value, of=res):
                if c in (0, DC - 1):
                    return
                dve.wait_ge(sem(signal), value)
                first = of[:, 0, :] if c == 1 else stat[:, 0, :]
                if c > 1:
                    dve.wait_ge(sem("summed"), sums[0])
                dve.tensor_tensor(stat[:, 0, :], first, of[:, c, :], ALU.add).then_inc(sem("summed"), 1)
                sums[0] += 1

            def split_x(signal, value):
                for c in range(DC):
                    dve.wait_ge(sem(signal), value + c + 1)
                    dve.tensor_tensor(x_l[:, c, :], x[:, c, :], x_h[:, c, :].bitcast(F32), ALU.subtract)\
                       .then_inc(sem("x_split"), 1)

            def centre(n):
                mean = filled(dve, f"mean{n}")
                to = gm_res if n == 2 else res

                def add_pair(j):
                    dve.wait_ge(sem("squared"), 8 * n + 2 * j + 2)
                    dve.tensor_tensor(sq[:, 2 * j, :], sq[:, 2 * j, :], sq[:, 2 * j + 1, :], ALU.add)\
                       .then_inc(sem("sq_summed"), 1)

                for c in range(DC):
                    dve.scalar_tensor_tensor(to[:, c, :], mean[:, 0:T], -1.0 / D, to[:, c, :], ALU.mult,
                                             ALU.add).then_inc(sem("centred"), 1)
                    if c % 2 and c >= 3:
                        add_pair((c - 3) // 2)
                frees(f"mean{n}", 0, "centred", 8 * n + 8)
                add_pair(3)

            def x_low(c, value):
                dve.wait_ge(sem("x_high"), value + c + 1)
                b = LN_B[{8: 0, 16: 1, 32: 4}[value]] + c
                dve.scalar_tensor_tensor(x_l[:, c, :], x[:, c, :], vec[:, b:b + 1], x_h[:, c, :].bitcast(F32),
                                         ALU.add, ALU.subtract).then_inc(sem("x_split"), 1)

            def scale(n, value=None):
                of, to, g = (gm_res, gm_v, G_GM) if n == 2 else (res, x, LN_G[n])
                dve.wait_ge(sem("deviation"), n + 1)
                dve.reciprocal(stat[:, 3, :], stat[:, 2, :]).then_inc(sem("rstd"), 1)
                dve.wait_ge(sem("rstd"), n + 1)
                for c in range(DC):
                    dve.scalar_tensor_tensor(to[:, c, :], of[:, c, :], vec[:, g + c:g + c + 1], stat[:, 3, :],
                                             ALU.mult, ALU.mult).then_inc(sem("scaled"), 1)
                    if value and c >= 2:
                        x_low(c - 2, value)
                if value:
                    x_low(DC - 2, value)
                    x_low(DC - 1, value)

            def p_split(n):
                dve.wait_ge(sem(f"p_loaded{n}"), 16)
                dve.tensor_copy(p_h[n], p_raw[n]).then_inc(sem("p_high"), 1)
                dve.wait_ge(sem("p_high"), n + 1)
                dve.tensor_tensor(p_l[n], p_raw[n], p_h[n].bitcast(F32), ALU.subtract).then_inc(sem("p_low"), 1)

            def tail_low(p):
                dve.wait_ge(sem("high_tail"), p - HIGHS + 1)
                dve.tensor_tensor(tail_piece(p, low), tail_piece(p, ring), tail_high(p).bitcast(F32),
                                  ALU.subtract).then_inc(sem("low_tail"), 1)

            def ple(n):
                def z_low(c):
                    dve.wait_ge(sem("x_high"), 24 + c + 1)
                    dve.tensor_tensor(z_l[:, c, :], x[:, c, :], z_h[:, c, :].bitcast(F32), ALU.subtract)\
                       .then_inc(sem("x_split"), 1)

                for c in range(DC):
                    if n == 0 and c in (2, 4, 6):
                        after(52 + c // 2)
                    if n == 1 and c == 4:
                        tail_low(4)
                    if c == 0:
                        dve.wait_ge(sem("normed"), 16 if n == 0 else 40)
                    dve.wait_ge(sem("ple_proj"), 8 * n + c + 1)
                    dve.wait_ge(sem("ple_sigmoid"), 8 * n + c + 1)
                    dve.tensor_tensor(gate_s[:, c, :], gate_s[:, c, :], ple_s[:, c, :], ALU.mult)\
                       .then_inc(sem("ple_gated"), 1)
                    dve.wait_ge(sem("ple_gated"), 8 * n + c + 1)
                    dve.tensor_tensor(x[:, c, :], x[:, c, :], gate_s[:, c, :], ALU.add)\
                       .then_inc(sem("ple_added"), 1)
                    if n == 0 and c:
                        z_low(c - 1)
                if n == 0:
                    z_low(DC - 1)

            done, sums = [], [0]
            dve.memset(lat_h.bitcast(F32), 0.0).then_inc(sem("lat_zero"), 1)
            dve.memset(lat_l.bitcast(F32), 0.0).then_inc(sem("lat_zero"), 1)
            split_x("x_high", 0)
            for q in range(HIGHS):
                split_low(q)
            for q in range(2):
                after(q)
            dve.memset(small[:, :], 0.0).then_inc(sem("small_zero"), 1)
            for i in range(2):
                dve.wait_ge(sem("rms_dev"), i + 1)
                dve.reciprocal(stat[:, 2 + i, :], stat[:, i, :]).then_inc(sem("rms_rstd"), 1)
                dve.wait_ge(sem("rms_rstd"), i + 1)
                for c in (range(QC) if i == 0 else range(QC, QC + KC)):
                    to = raw[:, c, :] if c < QC else lat[:, c - QC, 0:T]
                    dve.scalar_tensor_tensor(to, raw[:, c, :], vec[:, G_Q + c:G_Q + c + 1], stat[:, 2 + i, :],
                                             ALU.mult, ALU.mult).then_inc(sem("latent"), 1)
                dve.wait_ge(sem("latent"), QC + KC * i)
                if i == 0:
                    full, to_h, to_l = raw[:, 0:QC, :], cq_h, cq_l
                else:
                    full, to_h, to_l = lat, lat_h[:, :, 0:KEYS], lat_l[:, :, 0:KEYS]
                    dve.wait_ge(sem("cache_loaded"), 16)
                    dve.wait_ge(sem("lat_zero"), 2)
                dve.tensor_copy(to_h, full).then_inc(sem("latent_high"), 1)
                dve.wait_ge(sem("latent_high"), i + 1)
                dve.tensor_tensor(to_l, full, to_h.bitcast(F32), ALU.subtract).then_inc(sem("latent_low"), 1)
                if i == 0:
                    after(2)
                    after(3)
            dve.wait_ge(sem("in_copied"), 6)
            dve.tensor_tensor(kr[:, 0:T], raw[:, 5, :], cos, ALU.mult).then_inc(sem("kr_part"), 1)
            ps = filled(dve, "krot")
            dve.tensor_tensor(rope_tmp[:, 0, :], ps[:, 0:T], sin, ALU.mult).then_inc(sem("kr_part"), 1)
            frees("krot", 0, "kr_part", 2)
            dve.wait_ge(sem("kr_part"), 2)
            dve.tensor_tensor(kr[:, 0:T], kr[:, 0:T], rope_tmp[:, 0, :], ALU.add).then_inc(sem("kr_ready"), 1)
            for q in range(4, 8):
                after(q)
            for c in range(4):
                dve.wait_ge(sem("qr_copied"), c + 1)
                dve.tensor_tensor(qr[:, c, :], qr_raw[:, c, :], cos, ALU.mult).then_inc(sem("qr_part"), 1)
                ps = filled(dve, "qrot", c)
                if c == 0:
                    dve.wait_ge(sem("kr_ready"), 1)
                dve.tensor_tensor(rope_tmp[:, c, :], ps[:, 0:T], sin, ALU.mult).then_inc(sem("qr_part"), 1)
                frees("qrot", c, "qr_part", 2 * c + 2)
                dve.wait_ge(sem("qr_part"), 2 * c + 2)
                dve.tensor_tensor(qr[:, c, :], qr[:, c, :], rope_tmp[:, c, :], ALU.add)\
                   .then_inc(sem("qr_ready"), 1)
            dve.wait_ge(sem("qr_ready"), 4)
            dve.memset(probs[:, :, :], 0.0).then_inc(sem("probs_zero"), 1)
            after(8)
            for i in range(8):
                ps = filled(dve, "vup", i)
                rows = P if i < 6 else TS
                dve.tensor_copy(v[0:rows, i // 2, 512 * (i % 2):512 * (i % 2) + 512], ps[0:rows, :])\
                   .then_inc(sem("v_ready"), 1)
                frees("vup", i, "v_ready", i + 1)

            def regions(h, ps_p, ps_s):
                b = probs[:, h % 2, :]
                out_ = []
                for blk, at in ((0, 0), (1, P)):
                    for half in range(2):
                        rows = slice(CHUNK * half, CHUNK * half + CHUNK)
                        n = P * blk + CHUNK * (half + 1)
                        out_.append((ps_p[rows, at:at + n], b[rows, at:at + n], rows, blk))
                out_.append((ps_s[0:TS, 0:TS + PAST], b[0:TS, 384:384 + TS + PAST], slice(0, TS), 2))
                return out_

            def row_max(h):
                n = ATT["S", h]
                ps_p, ps_s = filled_at(dve, n), filled_at(dve, n + 1)
                if h == 0:
                    dve.wait_ge(sem("small_zero"), 1)
                for s, _, rows, col in regions(h, ps_p, ps_s):
                    dve.tensor_reduce(mx[rows, h % 2, col:col + 1], s, AX_X, ALU.max).then_inc(sem("row_max"), 1)
                dve.wait_ge(sem("row_max"), 5 * h + 5)
                if h >= 2:
                    dve.wait_ge(sem("exp_done"), 5 * (h - 1))
                dve.tensor_scalar(nmx[:, h % 2, :], mx[:, h % 2, :], -SCALE, None, ALU.mult)\
                   .then_inc(sem("neg_max"), 1)

            def row_scale(h):
                dve.wait_ge(sem("exp_done"), 5 * h + 5)
                if h == 0:
                    dve.wait_ge(sem("probs_zero"), 1)
                for i, rows in enumerate((P, P, TS)):
                    dve.reciprocal(prec[0:rows, h % 2, i:i + 1], psum_r[0:rows, h % 2, i:i + 1])\
                       .then_inc(sem("row_recip"), 1)
                dve.wait_ge(sem("row_recip"), 3 * h + 3)
                for i, (rows, lo, hi) in enumerate(((P, 0, P), (P, P, 3 * P), (TS, 384, 384 + TS + PAST))):
                    t = probs[0:rows, h % 2, lo:hi]
                    dve.tensor_scalar(t, t, prec[0:rows, h % 2, i:i + 1], None, ALU.mult)\
                       .then_inc(sem("probs_ready"), 1)

            def head_out(h):
                ps = filled_at(dve, ATT["O", h])
                dve.wait_ge(sem("head_high"), h + 1)
                dve.tensor_tensor(att_l[:, h, :], ps[:, 0:T], att_h[:, h, :].bitcast(F32), ALU.subtract)\
                   .then_inc(sem("head_low"), 1)
                free_by[ATT["O", h]] = ("head_low", h + 1)

            row_max(0)
            row_max(1)
            after(9)
            for h in range(H):
                row_scale(h)
                if h + 2 < H:
                    row_max(h + 2)
                if h >= 2:
                    head_out(h - 2)
            head_out(H - 2)
            head_out(H - 1)
            for c in range(DC):
                residual(0, c)
                if c in (1, 3, 5):
                    after(10 + c // 2)
            centre(0)
            scale(0, 8)
            after(13)
            for i in range(FC):
                ps = filled(dve, "ffn", 2 * i + 1)
                dve.wait_ge(sem("ffn_silu"), i + 1)
                if i >= 3:
                    dve.wait_ge(sem("hid_high"), i - 2)
                if i == 0:
                    dve.wait_ge(sem("kr_out"), 16)
                dve.tensor_tensor(hid[:, i % 3, :], sil[:, i % 3, :], ps[:, 0:T], ALU.mult)\
                   .then_inc(sem("ffn_hidden"), 1)
                frees("ffn", 2 * i + 1, "ffn_hidden", i + 1)
                after(14 + i)
                dve.wait_ge(sem("hid_high"), i + 1)
                dve.tensor_tensor(hid_l[:, i, :], hid[:, i % 3, :], hid_h[:, i, :].bitcast(F32), ALU.subtract)\
                   .then_inc(sem("hid_low"), 1)
            p_split(0)
            for c in range(DC):
                if c == DC - 1:
                    after(50)
                residual(1, c)
                if c < DC - 1:
                    after(36 + 2 * c)
                    after(37 + 2 * c)
            centre(1)
            scale(1, 16)
            after(51)
            after(52)
            ple(0)
            after(56)
            after(57)
            for j in range(4):
                after(58 + j)
                for c in (2 * j, 2 * j + 1):
                    add_up(c, "gelu", c + 1, gm_res)
            centre(2)
            for q in (62, 63, 64):
                after(q)
            scale(2)
            dve.wait_ge(sem("gm_loaded"), 32)

            def mix_bias(g):
                ps = filled(dve, "mix", g)
                dve.tensor_tensor(gm_tmp[:, g % 2, :], ps[:, 0:T], gm_bias[:, g, :], ALU.add)\
                   .then_inc(sem("mix_biased"), 1)
                frees("mix", g, "mix_biased", g + 1)

            def mixed_low(g):
                dve.wait_ge(sem("um_high"), g + 1)
                dve.tensor_tensor(um_l[:, g, :], gm_u[:, g, :], um_h[:, g, :].bitcast(F32), ALU.subtract)\
                   .then_inc(sem("um_low"), 1)

            mix_bias(0)
            for g in range(8):
                if g < 7:
                    if g:
                        dve.wait_ge(sem("mixed"), g)
                    mix_bias(g + 1)
                dve.wait_ge(sem("mix_biased"), g + 1)
                dve.tensor_tensor(gm_u[:, g, :], gm_u[:, g, :], gm_tmp[:, g % 2, :], ALU.mult)\
                   .then_inc(sem("mixed"), 1)
                if g:
                    mixed_low(g - 1)
            mixed_low(7)
            after(65)
            for c in range(DC):
                residual(3, c)
                if c == 1:
                    after(66)
                if c == 5:
                    first_low(0)
            centre(3)
            scale(3)
            first_low(1)

            route = [0]

            def r_(ins, wait=True):
                ins.then_inc(sem("route_step"), 1)
                route[0] += 1
                if wait:
                    dve.wait_ge(sem("route_step"), route[0])

            one, two = slice(0, 1), slice(1, 2)
            ps = filled(dve, "logits")
            r_(dve.tensor_copy(lg[:, 0:2, :], ps[:, 0:16].rearrange("p (b c) -> p b c", b=2)), False)
            r_(dve.tensor_copy(lg[0:TS, 2, :], ps[0:TS, 16:24]))
            frees("logits", 0, "route_step", route[0])
            for i in range(3):
                r_(dve.max(mx8[:, i, :], lg[:, i, :]), i == 2)
            for i in range(3):
                r_(dve.max_index(maxidx[:, i, :], mx8[:, i, :], lg[:, i, :]), i == 2)
            r_(dve.tensor_tensor(diff.rearrange("p (b c) -> p b c", c=1), mx8[:, :, two], mx8[:, :, one],
                                 ALU.subtract), False)
            r_(dve.tensor_copy(idx[:, :, :], maxidx[:, :, :]))
            ramp8 = const[:, C_RAMP8:C_RAMP8 + 24].rearrange("p (b c) -> p b c", b=3)
            for k, hot in enumerate((oneA, oneB)):
                r_(dve.tensor_tensor(hot, ramp8, idx[:, :, k:k + 1].broadcast_to([P, 3, E]), ALU.is_equal), k == 1)
            r_(dve.tensor_tensor(sel, oneA, oneB, ALU.add))
            assert route[0] == SEL_STEP
            dve.wait_ge(sem("normed"), 8 * 4)
            for c in range(DC):
                dve.tensor_scalar(res[:, c, :], x[:, c, :], ALPHA, None, ALU.mult).then_inc(sem("added"), 1)
            ps = filled(dve, "rank")
            r_(dve.tensor_copy(rank[:, :, :], ps[:, 0:32].rearrange("p (b c) -> p b c", b=4)))
            frees("rank", 0, "route_step", route[0])
            r_(dve.tensor_scalar(over[:, :], rank[:, 3, :], float(P), None, ALU.is_gt))
            r_(dve.scalar_tensor_tensor(sums_a[:, 8:16], rank[:, 3, :], float(2 * P), over[:, :], ALU.is_gt, ALU.add))
            base3 = const[:, C_BASE1:C_BASE1 + 24].rearrange("p (b c) -> p b c", b=3)
            r_(dve.tensor_tensor(slot_of, rank[:, 0:3, :], base3, ALU.add), False)
            r_(dve.tensor_tensor(sums_b[:, 8:16], sums_a[:, 8:16], sums_a[:, 7:15], ALU.add))
            r_(dve.tensor_tensor(sums_a[:, 8:16], sums_b[:, 8:16], sums_b[:, 6:14], ALU.add))
            r_(dve.tensor_tensor(sums_b[:, 8:16], sums_a[:, 8:16], sums_a[:, 4:12], ALU.add))
            r_(dve.scalar_tensor_tensor(shift[:, :], sums_b[:, 7:15], float(P), const[:, C_BASE:C_BASE + E],
                                        ALU.mult, ALU.add))
            shift3 = shift.rearrange("p (b c) -> p b c", b=1).broadcast_to([P, 3, E])
            r_(dve.scalar_tensor_tensor(big, rank[:, 0:3, :], float(P), shift3, ALU.is_ge, ALU.mult))
            r_(dve.tensor_tensor(slot_of, big, slot_of, ALU.add))
            for k, hot in enumerate((oneA, oneB)):
                r_(dve.tensor_tensor(picked[:, k, :, :], slot_of, hot, ALU.mult), k == 1)
            for k in range(2):
                r_(dve.tensor_reduce(where[:, k, :], picked[:, k, :, :], AX_X, ALU.add), k == 1)

            def one_hots(n, i):
                for k in range(2):
                    dve.tensor_scalar(eq[:, 3 * k + i, :], ramp, where[:, k, i:i + 1], None, ALU.is_equal)\
                       .then_inc(sem("eq_ready"), 1)
                dve.wait_ge(sem("eq_ready"), n * 6 + (2 * i + 2))
                dve.tensor_tensor(onehot[:, i, :], eq[:, i, :], eq[:, 3 + i, :], ALU.add)\
                   .then_inc(sem("onehot_ready"), 1)

            def move_slots(n):
                dve.wait_ge(sem("onehot_ready"), n * 3 + 3)
                dve.tensor_scalar(where[:, :, :], where[:, :, :], -float(P), None, ALU.add)\
                   .then_inc(sem("where_moved"), 1)
                dve.wait_ge(sem("where_moved"), n + 1)

            def gathered_low(n, half):
                dve.wait_ge(sem("xg_high"), n * 2 + (half + 1))
                dve.tensor_tensor(xg_l[:, 4 * half:4 * half + 4, :],
                                  bank[2 + half][:, :].rearrange("p (c s) -> p c s", c=4),
                                  xg_h[:, 4 * half:4 * half + 4, :].bitcast(F32), ALU.subtract)\
                   .then_inc(sem("xg_low"), 1)

            filled(dve, *xtr_tile(DC - 1))
            dve.wait_ge(sem("added"), DC)
            for i in range(3):
                one_hots(0, i)
            move_slots(0)
            r_(dve.tensor_copy(ids[:, 0:8], const[:, C_RAMP8:C_RAMP8 + E]), False)
            ramp4 = const[:, C_RAMP4:C_RAMP4 + 28].rearrange("p (b c) -> p b c", b=4)
            cum7 = sums_b[:, 8:15].rearrange("p (b c) -> p b c", b=1).broadcast_to([P, 4, E - 1])
            r_(dve.tensor_tensor(cmp, ramp4, cum7, ALU.is_ge))
            r_(dve.tensor_reduce(ids[:, 8:12], cmp, AX_X, ALU.add), False)
            r_(dve.tensor_scalar(ids[:, 12:13], sums_b[:, 15:16], float(E), None, ALU.add), False)
            r_(dve.tensor_scalar(ids[:, 13:14], sums_b[:, 15:16], float(E - 1), None, ALU.add))
            dve.wait_ge(sem("share_exp"), 1)
            r_(dve.tensor_scalar(den[:, :], e2[:, :], 1.0, None, ALU.add))
            r_(dve.reciprocal(share[:, 0, :], den[:, :]))
            r_(dve.tensor_tensor(share[:, 1, :], share[:, 0, :], e2[:, :], ALU.mult))
            dve.tensor_copy(table[:, 0:14], ids[:, 0:14]).then_inc(sem("table_ready"), 1)
            for half in range(2):
                gathered_low(0, half)
            first_low(2)
            p_split(1)
            dve.wait_ge(sem("table_ready"), 1)
            tiles = dve.value_load(table[0:1, 12:13], min_val=E, max_val=MAX_TILES)
            with dve.Fori(0, tiles) as t:
                def turned_low(f):
                    dve.wait_ge(sem("hT_high"), t * FB + (f + 1))
                    at = 4 * (f % 2)
                    dve.tensor_tensor(hT_l[:, at:at + 4, :], bank[4 + f % 2][:, :].rearrange("p (c s) -> p c s", c=4),
                                      hT_h[:, at:at + 4, :].bitcast(F32), ALU.subtract)\
                       .then_inc(sem("hT_low"), 1)

                def add_scattered(chunks):
                    for c in chunks:
                        dve.wait_ge(sem("scattered"), t * DC + (c + 1))
                        dve.tensor_tensor(res[:, c, :], res[:, c, :], bank[SCATTER[c]][:, 0:T], ALU.add)\
                           .then_inc(sem("added"), 1)

                for p in range(EP):
                    kind, f = ORDER[p // 2]
                    if p % 2 and kind == "u":
                        dve.wait_ge(sem("piece_used"), t * EP + (p + 1))
                        dve.wait_ge(sem("silu_done"), t * FB + (f + 1))
                        dve.tensor_tensor(hbuf[:, f % 2, :], sbuf[:, f % 2, :], bank[1 + 2 * (f % 2)][:, :],
                                          ALU.mult).then_inc(sem("hidden_ready"), 1)
                    if p % 2 and kind == "g" and f:
                        turned_low(f - 1)
                    if p % 2 and kind == "d" and f == FB - 2:
                        turned_low(FB - 1)
                        gathered_low(t + 1, 0)
                    if p % 2 and kind == "d" and 1 <= f <= 3:
                        if f == 1:
                            dve.wait_ge(sem("ct_turned"), t + 1)
                        one_hots(t + 1, f - 1)
                        if f == 3:
                            move_slots(t + 1)
                    if p == EP - 1:
                        for half in range(2):
                            cols = slice(512 * half, 512 * half + 512)
                            dve.wait_ge(sem("y_high"), t * 2 + (half + 1))
                            dve.scalar_tensor_tensor(y_l[:, cols], bank[6 + half][:, :], slot_share,
                                                     y_h[:, cols].bitcast(F32), ALU.mult, ALU.subtract)\
                               .then_inc(sem("y_low"), 1)
                        gathered_low(t + 1, 1)
                        add_scattered(range(4))
                    dve.wait_ge(sem("high_ready"), t * EP + (NP + p + HIGHS + 1))
                    dve.tensor_tensor(expert_piece((p + HIGHS) % EP, low), expert_piece((p + HIGHS) % EP, ring),
                                      expert_high(p + HIGHS).bitcast(F32), ALU.subtract)\
                       .then_inc(sem("low_ready"), 1)
                add_scattered(range(4, DC))
            dve.wait_ge(sem("added"), tiles * DC + DC)
            for j in range(4):
                dve.tensor_tensor(sq[:, j, :], res[:, 2 * j, :], res[:, 2 * j + 1, :], ALU.add)\
                   .then_inc(sem("summed"), 1)
            centre(4)
            scale(4, 32)
            tail_low(3)
            ple(1)

        @block.scalar
        def _(act):
            def split_high(q):
                n = PIECES[q][0]
                if q == 0:
                    act.wait_ge(sem("first_landed"), 16)
                else:
                    act.wait_ge(sem(f"landed{n % TRUNK_SLOTS}"), 16 * (n // TRUNK_SLOTS + 1))
                if q >= HIGHS:
                    signal, value = PIECES[q - HIGHS][7]
                    act.wait_ge(sem(signal), value)
                act.activation(piece_high(q), piece(q, ring), ACT.Copy).then_inc(sem("high_ready"), 1)

            def after(q):
                if q + HIGHS < NP:
                    split_high(q + HIGHS)

            def first_high(p):
                s = p // 2
                act.wait_ge(sem(f"landed{s}"), 16 * (landed_before(s) + 1))
                signal, value = PIECES[NP + p - HIGHS][7]
                act.wait_ge(sem(signal), value)
                act.activation(expert_high(p), expert_piece(p, ring), ACT.Copy).then_inc(sem("high_ready"), 1)

            def squares(n):
                of = gm_res if n == 2 else res
                for c in range(DC):
                    act.wait_ge(sem("centred"), 8 * n + c + 1)
                    act.activation(sq[:, c, :], of[:, c, :], ACT.Square).then_inc(sem("squared"), 1)

            def deviation(n):
                var = filled(act, f"var{n}")
                act.activation(stat[:, 2, :], var[:, 0:T], ACT.Sqrt, bias=eps_ln, scale=1.0 / D)\
                   .then_inc(sem("deviation"), 1)
                frees(f"var{n}", 0, "deviation", n + 1)

            def x_rounded(n):
                for c in range(DC):
                    act.wait_ge(sem("scaled"), 8 * n + c + 1)
                    act.activation(x_h[:, c, :], x[:, c, :], ACT.Identity,
                                   bias=vec[:, LN_B[n] + c:LN_B[n] + c + 1]).then_inc(sem("x_high"), 1)

            def biased(n, split=None):
                to, b = (gm_v, B_GM) if n == 2 else (x, LN_B[n])
                for c in range(DC):
                    act.wait_ge(sem("scaled"), 8 * n + c + 1)
                    if split:
                        act.wait_ge(sem("x_split"), split + c + 1)
                    act.activation(to[:, c, :], to[:, c, :], ACT.Identity, bias=vec[:, b + c:b + c + 1])\
                       .then_inc(sem("normed"), 1)

            def projected(n, chunks):
                for c in chunks:
                    ps = filled(act, *proj_tile(n, c))
                    act.activation(ple_s[:, c, :], ps[:, 0:T], ACT.Copy).then_inc(sem("ple_proj"), 1)
                    frees(*proj_tile(n, c), "ple_proj", 8 * n + c + 1)

            def high_of_tail(p, name, i):
                act.wait_ge(sem(f"landed{p // 2}"), tiles * (16 * EB // SLOTS) + 16 * (landed_before(0) + 1))
                filled(act, name, i)
                act.activation(tail_high(p), tail_piece(p, ring), ACT.Copy).then_inc(sem("high_tail"), 1)

            def ple_gate(n):
                def z_high(c):
                    act.wait_ge(sem("ple_added"), c + 1)
                    act.activation(z_h[:, c, :], x[:, c, :], ACT.Copy).then_inc(sem("x_high"), 1)

                for c in range(DC):
                    if n == 0 and c in (2, 4, 6):
                        after(52 + c // 2)
                    if n == 1 and c == 3:
                        high_of_tail(4, "gate1", 3)
                    ps = filled(act, f"gate{n}", c)
                    act.activation(gate_s[:, c, :], ps[:, 0:T], ACT.Sigmoid).then_inc(sem("ple_sigmoid"), 1)
                    frees(f"gate{n}", c, "ple_sigmoid", 8 * n + c + 1)
                    if n == 0 and c:
                        z_high(c - 1)
                if n == 0:
                    z_high(DC - 1)

            split_high(0)
            for c in range(DC):
                act.wait_ge(sem(f"x_loaded{c // 4}"), 16)
                act.activation(x_h[:, c, :], x[:, c, :], ACT.Copy).then_inc(sem("x_high"), 1)
            for q in range(1, HIGHS):
                split_high(q)
            act.wait_ge(sem("const_loaded"), 16)
            act.wait_ge(sem("vec_loaded"), 16)

            def rms_deviation(i, name, width):
                ps = filled(act, name)
                act.activation(stat[:, i, :], ps[:, 0:T], ACT.Sqrt, bias=eps_rms, scale=1.0 / width)\
                   .then_inc(sem("rms_dev"), 1)
                frees(name, 0, "rms_dev", i + 1)

            for c in range(6):
                if c == 5:
                    rms_deviation(0, "rms_q", QL)
                    after(2)
                ps = filled(act, *in_tile(c))
                act.activation(raw[:, c, :], ps[:, 0:T], ACT.Copy).then_inc(sem("in_copied"), 1)
                if c < 5:
                    act.activation(in_sq[:, c, :], ps[:, 0:T], ACT.Square).then_inc(sem("in_squared"), 1)
                    frees(*in_tile(c), "in_squared", c + 1)
                if c in (1, 2):
                    after(c - 1)
            frees("in_kr", 0, "in_copied", 6)
            after(3)
            rms_deviation(1, "rms_kv", KVL)
            for c in range(4):
                ps = filled(act, "qrope", c)
                act.activation(qr_raw[:, c, :], ps[:, 0:T], ACT.Copy).then_inc(sem("qr_copied"), 1)
                frees("qrope", c, "qr_copied", c + 1)
                if c == 2:
                    after(4)
            for c in range(DC):
                ps = filled(act, "qnope", c)
                act.activation(qn[:, c, :], ps[:, 0:T], ACT.Copy).then_inc(sem("qn_ready"), 1)
                frees("qnope", c, "qn_ready", c + 1)
                if c % 3 == 1:
                    after(5 + c // 3)
            for c in range(H):
                ps = filled(act, "kup", c)
                act.activation(kT[:, c, :], ps[:, 0:KEYS], ACT.Copy).then_inc(sem("k_ready"), 1)
                frees("kup", c, "k_ready", c + 1)
            after(8)
            after(9)

            def exps(h):
                n = ATT["S", h]
                ps_p, ps_s = bank[n % 8], bank[(n + 1) % 8]
                act.wait_ge(sem("neg_max"), h + 1)
                if h == 0:
                    act.wait_ge(sem("probs_zero"), 1)
                if h >= 2:
                    filled_at(act, ATT["T", h - 2])
                b = probs[:, h % 2, :]
                for blk, at in ((0, 0), (1, P)):
                    for half in range(2):
                        rows = slice(CHUNK * half, CHUNK * half + CHUNK)
                        m = P * blk + CHUNK * (half + 1)
                        act.activation(b[rows, at:at + m], ps_p[rows, at:at + m], ACT.Exp,
                                       bias=nmx[rows, h % 2, blk:blk + 1], scale=SCALE,
                                       accum_out=psum_r[rows, h % 2, blk:blk + 1]).then_inc(sem("exp_done"), 1)
                act.activation(b[0:TS, 384:384 + TS + PAST], ps_s[0:TS, 0:TS + PAST], ACT.Exp,
                               bias=nmx[0:TS, h % 2, 2:3], scale=SCALE,
                               accum_out=psum_r[0:TS, h % 2, 2:3]).then_inc(sem("exp_done"), 1)
                free_by[n] = ("exp_done", 5 * h + 4)
                free_by[n + 1] = ("exp_done", 5 * h + 5)

            def turned_probs(h):
                ps = filled_at(act, ATT["T", h])
                if h >= 2:
                    filled_at(act, ATT["O", h - 2])
                act.activation(probsT[:, h % 2, 0:416], ps[:, 0:416], ACT.Copy).then_inc(sem("probsT_ready"), 1)
                act.activation(probsT[0:TS, h % 2, 416:448], ps[0:TS, 416:448], ACT.Copy)\
                   .then_inc(sem("probsT_ready"), 1)
                free_by[ATT["T", h]] = ("probsT_ready", 2 * h + 2)

            def head_high(h):
                ps = filled_at(act, ATT["O", h])
                act.activation(att_h[:, h, :], ps[:, 0:T], ACT.Copy).then_inc(sem("head_high"), 1)

            exps(0)
            exps(1)
            for h in range(H):
                turned_probs(h)
                if h + 2 < H:
                    exps(h + 2)
                if h:
                    head_high(h - 1)
            head_high(H - 1)
            for q in range(10, 13):
                after(q)
            squares(0)
            deviation(0)
            x_rounded(0)
            after(13)
            biased(0, 8)
            for i in range(FC):
                ps = filled(act, "ffn", 2 * i)
                if i >= 3:
                    act.wait_ge(sem("ffn_hidden"), i - 2)
                act.activation(sil[:, i % 3, :], ps[:, 0:T], ACT.Silu).then_inc(sem("ffn_silu"), 1)
                frees("ffn", 2 * i, "ffn_silu", i + 1)
                act.wait_ge(sem("ffn_hidden"), i + 1)
                act.activation(hid_h[:, i, :], hid[:, i % 3, :], ACT.Copy).then_inc(sem("hid_high"), 1)
                after(14 + i)
            for q in range(36, 51):
                after(q)
            squares(1)
            projected(0, range(4))
            deviation(1)
            after(51)
            x_rounded(1)
            projected(0, range(4, DC))
            after(52)
            biased(1, 16)
            ple_gate(0)
            after(56)
            after(57)
            def gelu(c):
                ps = filled(act, *gm_tile(c))
                to = gm_res[:, c, :] if c < DC else gm_u[:, c - DC, :]
                act.activation(to, ps[:, 0:T], ACT.Gelu_apprx_tanh).then_inc(sem("gelu"), 1)
                frees(*gm_tile(c), "gelu", c + 1)
                if c % 2 and c < 2 * DC - 1:
                    after(58 + c // 2)

            for c in range(10):
                gelu(c)
            squares(2)
            for c in range(10, 14):
                gelu(c)
            deviation(2)
            gelu(14)
            biased(2)
            gelu(15)
            act.wait_ge(sem("normed"), 24)
            act.dma_start(out["gm_v"], gm_v[:, :, P:T]).then_inc(sem("gm_v_out"), 16)
            for g in range(8):
                ps = filled(act, "vtr", g)
                act.activation(gm_vtok[:, g, 0:256], ps[:, 0:256], ACT.Copy).then_inc(sem("vtok"), 1)
                act.activation(gm_vtok[0:TS, g, 256:384], ps[0:TS, 256:384], ACT.Copy).then_inc(sem("vtok"), 1)
                frees("vtr", g, "vtok", 2 * g + 2)
            act.wait_ge(sem("gm_v_out"), 16)
            filled(act, "vtr", 7)
            for g in range(8):
                act.wait_ge(sem("mixed"), g + 1)
                act.activation(um_h[:, g, :], gm_u[:, g, :], ACT.Copy).then_inc(sem("um_high"), 1)
            after(65)
            after(66)
            first_high(0)
            first_high(1)
            squares(3)
            deviation(3)
            biased(3)
            ps = filled(act, "logits_t")
            act.activation(logits_t, ps[0:E, 0:T], ACT.Copy).then_inc(sem("logits_copied"), 1)
            frees("logits_t", 0, "logits_copied", 1)
            first_high(2)
            for c in range(DC):
                ps = filled(act, *xtr_tile(c))
                act.activation(xtok[:, 0:2, c * P:c * P + P], ps[:, 0:256].rearrange("p (b s) -> p b s", b=2),
                               ACT.Copy).then_inc(sem("xtok"), 1)
                act.activation(xtok[0:TS, 2, c * P:c * P + P], ps[0:TS, 256:384], ACT.Copy)\
                   .then_inc(sem("xtok"), 1)
                frees(*xtr_tile(c), "xtok", 2 * c + 2)
            act.wait_ge(sem("route_step"), SEL_STEP)
            act.activation(e2[:, :], diff[:, :], ACT.Exp).then_inc(sem("share_exp"), 1)

            def gathered_high(n, half):
                act.wait_ge(sem("gathered"), n * 2 + (half + 1))
                act.activation(xg_h[:, 4 * half:4 * half + 4, :],
                               bank[2 + half][:, :].rearrange("p (c s) -> p c s", c=4), ACT.Copy)\
                   .then_inc(sem("xg_high"), 1)

            for half in range(2):
                gathered_high(0, half)
            act.wait_ge(sem("table_ready"), 1)
            tiles = act.value_load(table[0:1, 12:13], min_val=E, max_val=MAX_TILES)
            with act.Fori(0, tiles) as t:
                def turned_high(f):
                    act.wait_ge(sem("turned"), t * FB + (f + 1))
                    act.activation(hT_h[:, 4 * (f % 2):4 * (f % 2) + 4, :],
                                   bank[4 + f % 2][:, :].rearrange("p (c s) -> p c s", c=4), ACT.Copy)\
                       .then_inc(sem("hT_high"), 1)

                for p in range(EP):
                    kind, f = ORDER[p // 2]
                    act.wait_ge(sem("piece_used"), t * EP + (p + 1))
                    if p % 2 and kind == "g":
                        if f >= 2:
                            act.wait_ge(sem("hidden_ready"), t * FB + (f - 1))
                        act.activation(sbuf[:, f % 2, :], bank[2 * (f % 2)][:, :], ACT.Silu)\
                           .then_inc(sem("silu_done"), 1)
                        if f:
                            turned_high(f - 1)
                        if f == 1:
                            act.wait_ge(sem("ct_turned"), t + 1)
                            act.activation(ct[:, :], bank[5][:, 0:T], ACT.Copy).then_inc(sem("ct_ready"), 1)
                            act.activation(slot_share, bank[5][:, T:T + 1], ACT.Copy)\
                               .then_inc(sem("slot_share_ready"), 1)
                            act.wait_ge(sem("slot_share_ready"), t + 1)
                    if p % 2 and kind == "d" and f == FB - 2:
                        turned_high(FB - 1)
                        gathered_high(t + 1, 0)
                    if p == EP - 1:
                        for half in range(2):
                            act.activation(y_h[:, 512 * half:512 * half + 512], bank[6 + half][:, :], ACT.Identity,
                                           scale=slot_share).then_inc(sem("y_high"), 1)
                        gathered_high(t + 1, 1)
                    nxt = p + HIGHS
                    s = nxt // 2 % SLOTS
                    act.wait_ge(sem(f"landed{s}"),
                                t * (16 * EB // SLOTS) + 16 * (landed_before(s) + nxt // 2 // SLOTS + 1))
                    act.activation(expert_high(nxt), expert_piece(nxt % EP, ring), ACT.Copy)\
                       .then_inc(sem("high_ready"), 1)
            squares(4)
            projected(1, range(4))
            deviation(4)
            x_rounded(4)
            projected(1, range(4, DC))
            high_of_tail(3, *proj_tile(1, DC - 1))
            biased(4, 32)
            ple_gate(1)

        @block.gpsimd
        def _(pool):
            pool.wait_ge(sem("gm_loaded"), 32)
            pool.affine_select(out=gm_w[:, :, :], in_=gm_w[:, :, :], compare_op=ALU.is_ge, fill=0.0, base=0,
                               pattern=[[0, 8], [1, P]], channel_multiplier=-1).then_inc(sem("gm_masked"), 1)

        @block.tensor
        def _(pe):
            def claim(n):
                if n >= 8:
                    signal, value = free_by[n - 8]
                    pe.wait_ge(sem(signal), value)
                return bank[n % 8]

            def busy(ps, left, right):
                pe.matmul(ps[:, :], left, right, start=True, stop=True)

            def busy_norm(n, tile):
                ps = claim(tile)
                for signal in ("deviation", "rstd"):
                    pe.wait_ge(sem(signal), n + 1)
                    busy(ps, ones, const[:, 0:512])

            def dense(name, pieces, rhs_h, rhs_l, n=T, before_chunk=None):
                i = 0
                for q in pieces:
                    _, kc, _, _, _, c0, c1, _ = PIECES[q]
                    hi, lo = piece_high(q), piece(q, low)
                    together = (c1 - c0) // P if before_chunk and i == 0 else 1
                    pe.wait_ge(sem("high_ready"), q + 1)
                    for j0 in range(0, (c1 - c0) // P, together):
                        js = range(j0, j0 + together)
                        tiles_ = [claim(TILE[name] + i + j - j0)[:, 0:n] for j in js]
                        for k in range(kc):
                            if together > 1:
                                before_chunk(k)
                            for j, ps in zip(js, tiles_):
                                cols = slice(j * P, j * P + P)
                                pe.matmul(ps, hi[:, k, cols], rhs_h[:, k, 0:n], start=(k == 0), stop=False)
                                pe.matmul(ps, hi[:, k, cols], rhs_l[:, k, 0:n], start=False, stop=False)
                        if j0 == 0:
                            pe.wait_ge(sem("low_ready"), q + 1)
                        for j, ps in zip(js, tiles_):
                            cols = slice(j * P, j * P + P)
                            for k in range(kc):
                                mm = pe.matmul(ps, lo[:, k, cols], rhs_h[:, k, 0:n], start=False,
                                               stop=(k == kc - 1))
                            mm.then_inc(sem("tile_filled"), 1)
                        i += together

            def norm_mean(n, of, signal, value):
                ps = claim(TILE[f"mean{n}"])
                pe.wait_ge(sem("summed"), 6 * n + 6)
                pe.matmul(ps[:, 0:T], ones, stat[:, 0, :], start=True, stop=False)
                pe.wait_ge(sem(signal), value)
                pe.matmul(ps[:, 0:T], ones, of[:, DC - 1, :], start=False, stop=True)\
                  .then_inc(sem("tile_filled"), 1)

            def norm_var(n):
                ps = claim(TILE[f"var{n}"])
                if n in (0, 3):
                    pe.wait_ge(sem("centred"), 8 * n + 1)
                    busy(ps, ones, const[:, 0:512])
                for j in range(4):
                    pe.wait_ge(sem("sq_summed"), 4 * n + j + 1)
                    mm = pe.matmul(ps[:, 0:T], ones, sq[:, 2 * j, :], start=(j == 0), stop=(j == 3))
                mm.then_inc(sem("tile_filled"), 1)

            pe.wait_ge(sem("lat_zero"), 2)
            for _ in range(4):
                busy(bank[7], lat_h[:, 0, 0:P].bitcast(F32), lat_l[:, 0, :].bitcast(F32))
            dense("in", [0, 1], x_h, x_l, before_chunk=lambda k: pe.wait_ge(sem("x_split"), k + 1))
            dense("in_kv", [2], x_h, x_l)
            pe.wait_ge(sem("const_loaded"), 16)

            def rms(name, first, n):
                ps = claim(TILE[name])
                for c in range(first, first + n):
                    pe.wait_ge(sem("in_squared"), c + 1)
                    mm = pe.matmul(ps[:, 0:T], ones, in_sq[:, c, :], start=(c == first), stop=(c == first + n - 1))
                mm.then_inc(sem("tile_filled"), 1)

            rms("rms_q", 0, QC)
            dense("in_kr", [3], x_h, x_l)
            rms("rms_kv", QC, KC)
            ps = claim(TILE["krot"])
            pe.wait_ge(sem("in_copied"), 6)
            pe.matmul(ps[:, 0:T], rot_m, raw[:, 5, :], start=True, stop=True).then_inc(sem("tile_filled"), 1)
            pe.wait_ge(sem("latent_low"), 1)
            dense("qrope", range(4, 8), cq_h, cq_l)
            for c in range(4):
                ps = claim(TILE["qrot"] + c)
                pe.wait_ge(sem("qr_copied"), c + 1)
                pe.matmul(ps[:, 0:T], rot_m, qr_raw[:, c, :], start=True, stop=True).then_inc(sem("tile_filled"), 1)
            pe.wait_ge(sem("latent_low"), 2)
            dense("kup", [8], lat_h, lat_l, KEYS)
            pe.wait_ge(sem("high_ready"), 10)
            pe.wait_ge(sem("low_ready"), 10)
            for i in range(8):
                ps = claim(TILE["vup"] + i)
                rows, cols = slice(P * (i // 2), P * (i // 2) + P), slice(512 * (i % 2), 512 * (i % 2) + 512)
                parts = ((lat_h, piece_high(9)), (lat_l, piece_high(9)), (lat_h, piece(9, low)))
                for m, (left, right) in enumerate(parts):
                    for k in range(KC):
                        mm = pe.matmul(ps[:, :], left[:, k, rows], right[:, k, cols],
                                       start=(m == 0 and k == 0), stop=(m == 2 and k == KC - 1))
                mm.then_inc(sem("tile_filled"), 1)

            def scores(h):
                if h == 0:
                    pe.wait_ge(sem("kr_ready"), 1)
                    pe.wait_ge(sem("cache_kr_loaded"), 16)
                pe.wait_ge(sem("qn_ready"), h + 1)
                pe.wait_ge(sem("k_ready"), h + 1)
                pe.wait_ge(sem("qr_ready"), h // 2 + 1)
                rr = slice(ROPE * (h % 2), ROPE * (h % 2) + ROPE)
                n = ATT["S", h]
                for ps, parts in ((claim(n), ((0, P, 0, P, 0), (P, 2 * P, 0, 2 * P, P))),
                                  (claim(n + 1), ((TP, T, TP, KEYS, 0),))):
                    for q0, q1, k0, k1, at in parts:
                        o = ps[0:q1 - q0, at:at + k1 - k0]
                        pe.matmul(o, qn[:, h, q0:q1], kT[:, h, k0:k1], start=True, stop=False)
                        mm = pe.matmul(o, qr[rr, h // 2, q0:q1], kr[rr, k0:k1], start=False, stop=True)
                    mm.then_inc(sem("tile_filled"), 1)

            def turn_probs(h):
                ps = claim(ATT["T", h])
                if h == 0:
                    pe.wait_ge(sem("neg_max"), 1)
                    busy(ps, ones, const[:, 0:512])
                    busy(ps, ones, const[:, 0:512])
                pe.wait_ge(sem("probs_ready"), 3 * h + 3)
                b = probs[:, h % 2, :]
                for j in range(3):
                    pe.transpose(ps[:, j * P:j * P + P], b[:, j * P:j * P + P], ident)
                pe.transpose(ps[:, 384:416], b[0:TS, 384:512], ident[0:TS, 0:TS])
                pe.transpose(ps[0:TS, 416:448], b[0:TS, 512:544], ident[0:TS, 0:TS])\
                  .then_inc(sem("tile_filled"), 1)

            def values(h):
                ps = claim(ATT["O", h])
                if h == 0:
                    pe.wait_ge(sem("v_ready"), 8)
                pe.wait_ge(sem("probsT_ready"), 2 * h + 2)
                b, cols = probsT[:, h % 2, :], slice(h * VH, h * VH + VH)
                pe.matmul(ps[:, 0:TP], v[:, 0, cols], b[:, 0:TP], start=True, stop=False)
                pe.matmul(ps[:, P:TP], v[:, 1, cols], b[:, TP:TP + P], start=False, stop=True)
                pe.matmul(ps[:, TP:T], v[:, 2, cols], b[:, 384:416], start=True, stop=False)
                pe.matmul(ps[:, TP:T], v[0:TS, 3, cols], b[0:TS, 416:448], start=False, stop=True)\
                  .then_inc(sem("tile_filled"), 1)

            scores(0)
            scores(1)
            for h in range(H):
                if h + 2 < H:
                    scores(h + 2)
                turn_probs(h)
                if h:
                    values(h - 1)
            values(H - 1)
            dense("att_out", range(10, 14), att_h, att_l,
                  before_chunk=lambda k: pe.wait_ge(sem("head_low"), k + 1))
            norm_mean(0, res, "residual", 8)
            norm_var(0)
            busy_norm(0, TILE["ffn"])
            dense("ffn", range(14, 36), x_h, x_l, before_chunk=lambda k: pe.wait_ge(sem("x_split"), 8 + k + 1))
            for i in range(DC):
                ps = claim(TILE["down"] + i)[:, 0:T]
                for r in range(2):
                    q = 36 + 2 * i + r
                    hi, lo = piece_high(q), piece(q, low)
                    pe.wait_ge(sem("high_ready"), q + 1)
                    for k in range(FC // 2):
                        c = r * (FC // 2) + k
                        if i == 0:
                            pe.wait_ge(sem("hid_low"), c + 1)
                        pe.matmul(ps, hi[:, k, :], hid_h[:, c, :], start=(c == 0), stop=False)
                        pe.matmul(ps, hi[:, k, :], hid_l[:, c, :], start=False, stop=False)
                    pe.wait_ge(sem("low_ready"), q + 1)
                    for k in range(FC // 2):
                        c = r * (FC // 2) + k
                        mm = pe.matmul(ps, lo[:, k, :], hid_h[:, c, :], start=False, stop=(c == FC - 1))
                    mm.then_inc(sem("down_half" if r == 0 else "tile_filled"), 1)
            norm_mean(1, res, "residual", 16)
            pe.wait_ge(sem("p_low"), 1)
            dense("proj0a", [52], p_h[0], p_l[0])
            norm_var(1)
            dense("proj0b", [53], p_h[0], p_l[0])
            dense("gate0", range(54, 58), x_h, x_l, before_chunk=lambda k: pe.wait_ge(sem("x_split"), 16 + k + 1))
            dense("gm_v", range(58, 62), z_h, z_l, before_chunk=lambda k: pe.wait_ge(sem("x_split"), 24 + k + 1))
            dense("gm_u0", [62], z_h, z_l)
            norm_mean(2, gm_res, "gelu", 8)
            dense("gm_u2", [63, 64], z_h, z_l)
            norm_var(2)
            dense("gm_u6", [65], z_h, z_l)
            for g in range(8):
                ps = claim(TILE["vtr"] + g)
                pe.wait_ge(sem("normed"), 16 + g + 1)
                pe.transpose(ps[:, 0:P], gm_v[:, g, 0:P], ident)
                pe.transpose(ps[:, P:2 * P], gm_v[:, g, P:2 * P], ident)
                pe.transpose(ps[0:TS, 2 * P:3 * P], gm_v[:, g, TP:T], ident).then_inc(sem("tile_filled"), 1)
            pe.wait_ge(sem("gm_masked"), 1)
            for g in range(8):
                ps = claim(TILE["mix"] + g)
                pe.wait_ge(sem("vtok"), 2 * g + 2)
                for b in range(2):
                    pe.matmul(ps[:, b * P:b * P + P], gm_vtok[:, g, b * P:b * P + P], gm_w[:, g, :],
                              start=True, stop=True)
                pe.matmul(ps[:, TP:T], gm_vtok[0:TS, g, 2 * P:3 * P], gm_w[0:TS, g, 0:TS], start=True, stop=True)\
                  .then_inc(sem("tile_filled"), 1)
            dense("gm_out", range(66, 70), um_h, um_l, before_chunk=lambda k: pe.wait_ge(sem("um_low"), k + 1))
            norm_mean(3, res, "residual", 24)
            norm_var(3)
            busy_norm(3, TILE["logits_t"])
            ps = claim(TILE["logits_t"])
            pe.wait_ge(sem("router_loaded"), 16)
            for k in range(DC):
                pe.wait_ge(sem("normed"), 24 + k + 1)
                mm = pe.matmul(ps[0:E, 0:T], w_router[:, k, :], x[:, k, :], start=(k == 0), stop=(k == DC - 1))
            mm.then_inc(sem("tile_filled"), 1)
            ps = claim(TILE["logits"])
            busy(ps, ones, const[:, 0:512])
            pe.wait_ge(sem("logits_copied"), 1)
            for i, rows in enumerate((P, P, TS)):
                tr = pe.transpose(ps[0:rows, 8 * i:8 * i + 8], logits_t[:, i * P:i * P + rows], ident[0:E, 0:E])
            tr.then_inc(sem("tile_filled"), 1)

            def turn_x(chunks):
                for c in chunks:
                    name, i = xtr_tile(c)
                    ps = claim(TILE[name] + i)
                    pe.transpose(ps[:, 0:P], x[:, c, 0:P], ident)
                    pe.transpose(ps[:, P:2 * P], x[:, c, P:2 * P], ident)
                    pe.transpose(ps[0:TS, 2 * P:3 * P], x[:, c, TP:T], ident).then_inc(sem("tile_filled"), 1)

            turn_x(range(4))
            ps = claim(TILE["rank"])
            pe.wait_ge(sem("route_step"), SEL_STEP)
            for i in range(4):
                o = ps[:, 8 * i:8 * i + 8]
                for j in range(min(i + 1, 3)):
                    mm = pe.matmul(o, before if j == i else ones, sel[:, j, :], start=(j == 0),
                                   stop=(j == min(i, 2)))
            mm.then_inc(sem("tile_filled"), 1)
            turn_x(range(4, DC))
            for signal, value in (free_by[TILE["rank"]], free_by[TILE["xtr_b"] + 3]):
                pe.wait_ge(sem(signal), value)
            pe.wait_ge(sem("route_step"), MID_STEP)
            for _ in range(2):
                busy(bank[2], ones, const[:, 0:512])

            def gather(n, half):
                pe.wait_ge(sem("onehot_ready"), n * 3 + 3)
                for c in range(4):
                    d = 4 * half + c
                    for i, rows in enumerate((P, P, TS)):
                        mm = pe.matmul(bank[2 + half][:, c * P:c * P + P],
                                       xtok[0:rows, i, d * P:d * P + P], onehot[0:rows, i, :],
                                       start=(i == 0), stop=(i == 2))
                mm.then_inc(sem("gathered"), 1)

            for half in range(2):
                gather(0, half)
            pe.wait_ge(sem("table_ready"), 1)
            tiles = pe.value_load(table[0:1, 12:13], min_val=E, max_val=MAX_TILES)
            with pe.Fori(0, tiles) as t:
                def turn(f):
                    pe.wait_ge(sem("hidden_ready"), t * FB + (f + 1))
                    if f >= 2:
                        pe.wait_ge(sem("hT_low"), t * FB + (f - 1))
                    elif f == 1:
                        pe.wait_ge(sem("slot_share_ready"), t + 1)
                    for c in range(4):
                        tr = pe.transpose(bank[4 + f % 2][:, c * P:c * P + P], hbuf[:, f % 2, c * P:c * P + P],
                                          ident)
                    tr.then_inc(sem("turned"), 1)

                def products(p, left_h, left_l, kc, outs):
                    first, last, dst = outs
                    width = PIECE // kc
                    hi = expert_high(p).rearrange("p (k n) -> p k n", k=kc)
                    lo = expert_piece(p, low).rearrange("p (k n) -> p k n", k=kc)
                    pe.wait_ge(sem("high_ready"), t * EP + (NP + p + 1))
                    for m, (left, right) in enumerate(((left_h, hi), (left_l, hi), (left_h, lo))):
                        if m == 2:
                            pe.wait_ge(sem("low_ready"), t * EP + (NP + p + 1))
                        for k in range(kc):
                            for n in range(width // 512):
                                mm = pe.matmul(dst[n][:, :], left(k), right[:, k, 512 * n:512 * n + 512],
                                               start=(first and m == 0 and k == 0),
                                               stop=(last and m == 2 and k == kc - 1))
                    mm.then_inc(sem("piece_used"), 1)

                for j, (kind, f) in enumerate(ORDER):
                    if kind == "d":
                        pe.wait_ge(sem("hT_low"), t * FB + (f + 1))
                        for r in range(2):
                            at = 4 * (f % 2) + 2 * r
                            products(2 * j + r, lambda k, at=at: hT_h[:, at + k, :],
                                     lambda k, at=at: hT_l[:, at + k, :], 2,
                                     (f == 0 and r == 0, f == FB - 1 and r == 1, (bank[6], bank[7])))
                        if f == FB - 2:
                            turn(FB - 1)
                            gather(t + 1, 0)
                        continue
                    up = int(kind == "u")
                    if f >= 2:
                        pe.wait_ge(sem("hidden_ready" if up else "silu_done"), t * FB + (f - 1))
                    elif f == 0:
                        pe.wait_ge(sem("added"), t * DC + (3 + up))
                    if j == 0:
                        pe.wait_ge(sem("xg_low"), t * 2 + 2)
                    for r in range(2):
                        products(2 * j + r, lambda k, r=r: xg_h[:, 4 * r + k, :], lambda k, r=r: xg_l[:, 4 * r + k, :],
                                 4, (r == 0, r == 1, (bank[2 * (f % 2) + up],)))
                    if f == 1 and not up:
                        pe.wait_ge(sem("added"), t * DC + DC)
                    if f and not up:
                        turn(f - 1)
                    if f == 1 and not up:
                        for i, rows in enumerate((P, P, TS)):
                            pe.transpose(bank[5][:, i * P:i * P + rows], onehot[0:rows, i, :],
                                         ident[0:rows, 0:rows])
                        for k in range(2):
                            for i, rows in enumerate((P, P, TS)):
                                tr = pe.matmul(bank[5][:, T:T + 1], eq[0:rows, 3 * k + i, :],
                                               share[0:rows, k, i:i + 1], start=(k == 0 and i == 0),
                                               stop=(k == 1 and i == 2))
                        tr.then_inc(sem("ct_turned"), 1)
                gather(t + 1, 1)
                pe.wait_ge(sem("ct_ready"), t + 1)
                pe.wait_ge(sem("y_high"), t * 2 + 1)
                for c in range(4):
                    pe.matmul(bank[SCATTER[c]][:, 0:T], y_h[:, c * P:c * P + P], ct[:, :], start=True, stop=False)
                pe.wait_ge(sem("y_low"), t * 2 + 1)
                for c in range(4):
                    pe.matmul(bank[SCATTER[c]][:, 0:T], y_l[:, c * P:c * P + P], ct[:, :], start=False, stop=True)\
                      .then_inc(sem("scattered"), 1)
                pe.wait_ge(sem("y_high"), t * 2 + 2)
                pe.wait_ge(sem("y_low"), t * 2 + 2)
                for c in range(4, DC):
                    if c == 6:
                        pe.wait_ge(sem("xg_low"), t * 2 + 3)
                    if c == 7:
                        pe.wait_ge(sem("added"), t * DC + (DC + 1))
                    pe.matmul(bank[SCATTER[c]][:, 0:T], y_h[:, c * P:c * P + P], ct[:, :], start=True, stop=False)
                    pe.matmul(bank[SCATTER[c]][:, 0:T], y_l[:, c * P:c * P + P], ct[:, :], start=False, stop=True)\
                      .then_inc(sem("scattered"), 1)
            pe.wait_ge(sem("xg_low"), tiles * 2 + 2)
            for _ in range(3):
                busy(bank[3], ones, const[:, 0:512])
            pe.wait_ge(sem("added"), tiles * DC + DC)
            ps = claim(TILE["mean4"])
            for j in range(4):
                pe.wait_ge(sem("summed"), 24 + j + 1)
                mm = pe.matmul(ps[:, 0:T], ones, sq[:, j, :], start=(j == 0), stop=(j == 3))
            mm.then_inc(sem("tile_filled"), 1)

            def products3(ps, hi, lo, x_hi, x_lo, first, last):
                pe.matmul(ps, hi, x_hi, start=first, stop=False)
                pe.matmul(ps, hi, x_lo, start=False, stop=False)
                return pe.matmul(ps, lo, x_hi, start=False, stop=last)

            def last_projection(chunks):
                hi = tail_high(0).rearrange("p (k n) -> p k n", k=PC)
                lo = tail_piece(0, low).rearrange("p (k n) -> p k n", k=PC)
                for c in chunks:
                    name, i = proj_tile(1, c)
                    ps = claim(TILE[name] + i)[:, 0:T]
                    cols = slice(c * P, c * P + P)
                    for k in range(PC):
                        mm = products3(ps, hi[:, k, cols], lo[:, k, cols], p_h[1][:, k, :], p_l[1][:, k, :],
                                       k == 0, k == PC - 1)
                    mm.then_inc(sem("tile_filled"), 1)

            pe.wait_ge(sem("p_low"), 2)
            pe.wait_ge(sem("high_ready"), tiles * EP + (NP + HIGHS))
            pe.wait_ge(sem("low_ready"), tiles * EP + (NP + HIGHS))
            last_projection(range(4))
            norm_var(4)
            last_projection(range(4, DC))
            for b in range(2):
                tiles4 = [claim(TILE["gate1"] + 4 * b + j)[:, 0:T] for j in range(4)]
                for r in range(2):
                    p = 1 + 2 * b + r
                    if p >= HIGHS:
                        pe.wait_ge(sem("high_tail"), p - HIGHS + 1)
                        pe.wait_ge(sem("low_tail"), p - HIGHS + 1)
                    hi = tail_high(p).rearrange("p (k n) -> p k n", k=4)
                    lo = tail_piece(p, low).rearrange("p (k n) -> p k n", k=4)
                    if r == 0:
                        for k in range(4):
                            if b == 0:
                                pe.wait_ge(sem("x_split"), 32 + k + 1)
                            for j in range(4):
                                cols = slice(j * P, j * P + P)
                                products3(tiles4[j], hi[:, k, cols], lo[:, k, cols], x_h[:, k, :], x_l[:, k, :],
                                          k == 0, False)
                        continue
                    for j in range(4):
                        cols = slice(j * P, j * P + P)
                        for k in range(4):
                            if b == 0 and j == 0:
                                pe.wait_ge(sem("x_split"), 32 + 4 + k + 1)
                            mm = products3(tiles4[j], hi[:, k, cols], lo[:, k, cols], x_h[:, 4 + k, :],
                                           x_l[:, 4 + k, :], False, k == 3)
                        mm.then_inc(sem("tile_filled"), 1)

        @block.sync
        def _(sp):
            n = 0
            for name, blocks, width in TRUNK:
                for b in range(blocks):
                    if n >= TRUNK_SLOTS:
                        sp.wait_ge(sem("tile_filled"), LAST_TILE[n - TRUNK_SLOTS] + 1)
                    s = n % TRUNK_SLOTS
                    if n == 0:
                        to = ring[0][:, 0:width].rearrange("p (k m) -> p k m", k=DC)
                        of = a[name][0].rearrange("p (k m) -> p k m", k=DC)
                        sp.dma_start(to[:, :, 0:256], of[:, :, 0:256]).then_inc(sem("first_landed"), 16)
                        for c in (0, 4):
                            sp.dma_start(x[:, c:c + 4, :], a["x"][:, c:c + 4, :])\
                              .then_inc(sem(f"x_loaded{c // 4}"), 16)
                        sp.dma_start(to[:, :, 256:384], of[:, :, 256:384]).then_inc(sem("landed0"), 16)
                        sp.dma_start(const[:, :], a["const"]).then_inc(sem("const_loaded"), 16)
                        sp.dma_start(vec[:, :], a["vec"]).then_inc(sem("vec_loaded"), 16)
                    else:
                        sp.dma_start(ring[s][:, 0:width], a[name][b]).then_inc(sem(f"landed{s}"), 16)
                    if n == 1:
                        sp.dma_start(lat[:, :, T:KEYS], a["cache_lat"]).then_inc(sem("cache_loaded"), 16)
                        sp.dma_start(kr[:, T:KEYS], a["cache_kr"]).then_inc(sem("cache_kr_loaded"), 16)
                        sp.dma_start(w_router[:, :, :], a["w_router"]).then_inc(sem("router_loaded"), 16)
                    n += 1
                if name == "mla_out":
                    sp.wait_ge(sem("latent"), QC + KC)
                    sp.dma_start(out["lat"], lat[:, :, 0:T]).then_inc(sem("lat_out"), 16)
                    sp.wait_ge(sem("kr_ready"), 1)
                    sp.dma_start(out["kr"], kr[0:ROPE, 0:T]).then_inc(sem("kr_out"), 16)
                if name == "ffn_in":
                    sp.wait_ge(sem("tile_filled"), ATT["T", H - 1] + 1)
                    sp.dma_start(p_raw[0], a["p"][0]).then_inc(sem("p_loaded0"), 16)
                if name == "gm_in":
                    sp.wait_ge(sem("tile_filled"), TILE["gate0"] + 8)
                    sp.dma_start(gm_bias, a["gm_bias"].broadcast_to([P, 8 * T]).rearrange("p (g t) -> p g t", g=8))\
                      .then_inc(sem("gm_loaded"), 16)
                    sp.dma_start(gm_w, a["gm_w"]).then_inc(sem("gm_loaded"), 16)
            sp.wait_ge(sem("lat_out"), 16)
            for j in range(SLOTS):
                if j < TRUNK_SLOTS:
                    sp.wait_ge(sem("tile_filled"), LAST_TILE[N_TRUNK - TRUNK_SLOTS + j] + 1)
                else:
                    sp.wait_ge(sem("mixed"), 8)
                sp.dma_start(ring[j][:, :], a["moe"][0, j]).then_inc(sem(f"landed{j}"), 16)
            sp.dma_start(p_raw[1], a["p"][1]).then_inc(sem("p_loaded1"), 16)
            sp.wait_ge(sem("table_ready"), 1)
            last = sp.value_load(table[0:1, 13:14], min_val=E - 1, max_val=MAX_TILES - 1)

            def expert_load(t, e, j):
                sp.wait_ge(sem("piece_used"), t * EP + 2 * (j - SLOTS + 1))
                sp.dma_start(ring[j % SLOTS][:, :], a["moe"][bass.ds(e, 1), j % EB].rearrange("a p n -> p (a n)"))\
                  .then_inc(sem(f"landed{j % SLOTS}"), 16)

            with sp.Fori(0, last) as t:
                e = sp.value_load(table[0:1, bass.ds(t, 1)], min_val=0, max_val=E - 1)
                for j in range(SLOTS, EB):
                    expert_load(t, e, j)
                e = sp.value_load(table[0:1, bass.ds(t + 1, 1)], min_val=0, max_val=E - 1)
                for j in range(SLOTS):
                    expert_load(t, e, EB + j)
            e = sp.value_load(table[0:1, bass.ds(last, 1)], min_val=0, max_val=E - 1)
            for j in range(SLOTS, EB):
                expert_load(last, e, j)
            for s, at in enumerate(range(0, TAIL, BLK)):
                width = min(BLK, TAIL - at)
                sp.wait_ge(sem("piece_used"), last * EP + 2 * (EB + s - SLOTS + 1))
                sp.dma_start(ring[s][:, 0:width], a["tail"][:, at:at + width]).then_inc(sem(f"landed{s}"), 16)
            for c in range(0, DC, 2):
                sp.wait_ge(sem("ple_added"), DC + c + 2)
                sp.dma_start(out["y"][:, c:c + 2, :], x[:, c:c + 2, :]).then_inc(sem("y_out"), 16)
            sp.wait_ge(sem("y_out"), 16 * (DC // 2))
            for name in ("lat_out", "kr_out", "gm_v_out"):
                sp.wait_ge(sem(name), 16)


def by_chunk(w, kc, per):
    n = w.shape[1] // (per * P)
    return np.ascontiguousarray(w.reshape(kc, P, n, per * P).transpose(2, 1, 0, 3).reshape(n, P, kc * per * P))


def feature_major(x):
    return np.ascontiguousarray(x.T.reshape(-1, P, x.shape[0]).transpose(1, 0, 2))


def token_major(x):
    return np.ascontiguousarray(x.transpose(1, 0, 2).reshape(-1, x.shape[2]).T)


def kernel(**inputs):
    import concourse.bacc as bacc
    from concourse.bass_utils import run_bass_kernel_spmd

    i = {k: np.asarray(v) for k, v in inputs.items()}
    w_in = i["w_mla_in"][0]
    w_in = np.concatenate([w_in, w_in[:, QL + KVL:]], axis=1)
    w_q = i["w_q_up"][0].reshape(QL, H, NOPE + ROPE)
    w_q = np.concatenate([w_q[:, :, NOPE:].reshape(QL, -1), w_q[:, :, :NOPE].reshape(QL, -1)], axis=1)
    w_kv = i["w_kv_up"][0].reshape(KVL, H, NOPE + VH)
    w_kv = np.concatenate([w_kv[:, :, :NOPE].reshape(KVL, -1), w_kv[:, :, NOPE:].reshape(KVL, -1)], axis=1)
    w_f = np.stack([i["w_ffn_gate"][0].reshape(D, FC, P), i["w_ffn_up"][0].reshape(D, FC, P)], axis=2)
    w_gm = i["w_gm_in"][0]
    w_gm = np.concatenate([w_gm[:, D:], w_gm[:, :D]], axis=1)
    moe = np.empty((E, EB, P, BLK), np.float32)
    for e in range(E):
        for kind, name in (("g", "w_moe_gate"), ("u", "w_moe_up")):
            moe[e, AT[kind]] = i[name][0, e].reshape(DC, P, FB, 512).transpose(2, 1, 0, 3).reshape(FB, P, BLK)
        moe[e, AT["d"]] = i["w_moe_down"][0, e].reshape(FB, 4, P, D).transpose(0, 2, 1, 3).reshape(FB, P, BLK)
    cols = [i["g_q_norm"][0].reshape(QC, P), i["g_kv_norm"][0].reshape(KC, P), i["g_gm_norm"][0].reshape(DC, P),
            i["b_gm_norm"][0].reshape(DC, P)]
    for name in ("ln1_g", "ln2_g", "ln1_b", "ln2_b"):
        cols.append(i[name].reshape(2 * DC, P))
    b_s = i["b_gm_spatial"][0]
    arrays = {
        "x": feature_major(np.concatenate([i["x_prompt"][0], i["x_sample"][0]])),
        "cache_lat": feature_major(i["cache_mla_latent"][0, 0]),
        "cache_kr": np.ascontiguousarray(np.concatenate([i["cache_mla_krope"][0, 0].T] * 2)),
        "p": np.stack([feature_major(np.concatenate([i["p_prompt"][n, 0], i["p_sample"][n, 0]])) for n in range(2)]),
        "vec": np.ascontiguousarray(np.concatenate(cols).T),
        "w_router": np.ascontiguousarray(i["w_router"][0].reshape(DC, P, E).transpose(1, 0, 2)),
        "gm_w": np.ascontiguousarray(i["w_gm_spatial"][0].transpose(2, 0, 1)),
        "gm_bias": np.ascontiguousarray(np.concatenate([b_s, b_s, b_s[:, :TS]], axis=1).reshape(1, 8 * T)),
        "mla_in": by_chunk(w_in, DC, 3), "q_up": by_chunk(w_q, QC, 6), "kv_up": by_chunk(w_kv, KC, 16),
        "mla_out": by_chunk(i["w_mla_out"][0], DC, 4), "ffn_in": by_chunk(w_f.reshape(D, -1), DC, 4),
        "ffn_down": by_chunk(i["w_ffn_down"][0], FC, 1), "gm_in": by_chunk(w_gm, DC, 4),
        "gm_out": by_chunk(i["w_gm_out"][0], DC, 4), "moe": moe,
    }
    ple = [(by_chunk(i["w_ple_gate"][n], DC, 4), by_chunk(i["w_ple_proj"][n], PC, 8)) for n in range(2)]
    arrays["ple_gate0"], arrays["ple_proj0"] = ple[0]
    arrays["tail"] = np.ascontiguousarray(np.concatenate([ple[1][1][0], ple[1][0][0], ple[1][0][1]], axis=1))
    outputs = {"lat": (P, KC, T), "kr": (ROPE, T), "gm_v": (P, DC, GM_CHUNK + TS), "y": (P, DC, T)}

    nc = bacc.Bacc("TRN2", target_bir_lowering=False, num_devices=1)
    a = {n: nc.dram_tensor(f"in_{n}", v.shape, F32, kind="ExternalInput").ap() for n, v in arrays.items()}
    a["const"] = nc.inline_tensor(constants(), "tables")[:, :]
    out = {n: nc.dram_tensor(f"out_{n}", s, F32, kind="ExternalOutput").ap() for n, s in outputs.items()}
    build(nc, a, out)
    r = run_bass_kernel_spmd(nc, [{f"in_{n}": v for n, v in arrays.items()}], core_ids=[0]).results[0]
    y, lat, gm_v = token_major(r["out_y"]), token_major(r["out_lat"]), token_major(r["out_gm_v"])
    kr = np.ascontiguousarray(r["out_kr"].T)
    return (y[None, :TP], y[None, TP:], lat[None, None, :TP], kr[None, None, :TP], lat[None, None, TP:],
            kr[None, None, TP:], gm_v[None, None, :GM_CHUNK], gm_v[None, None, GM_CHUNK:])
```
